# Optimizing a Trainium2 kernel written in Bass

```python
import math
import jax, jax.numpy as jnp
from jax import lax
import numpy as np

D_MODEL = 2048
BATCH = 1
SEQ = 256
DEPTH = 2

N_A = DEPTH // 2
N_B = DEPTH - N_A
DA_HEADS = 8
DA_HEAD_DIM = 128
DA_ROT = DA_HEAD_DIM // 4
DA_QKV = 3 * DA_HEADS * 2 * DA_HEAD_DIM
MLA_HEADS = 16
Q_LORA = 384
KV_LORA = 512
QK_NOPE = 128
QK_ROPE = 64
V_DIM = 128
D_FF = 4 * D_MODEL
ROPE_THETA = 500000.0
Q_BLOCK = 128
NORM_EPS = 1e-6
SUBLN_EPS = 1e-5

kernel_name = "yoco_diffattn_mla_hybrid"

def rms_norm(x, g, eps=NORM_EPS):
    xf = x.astype(jnp.float32)
    y = xf * lax.rsqrt(jnp.mean(xf * xf, axis=-1, keepdims=True) + eps)
    return (y * g.astype(jnp.float32)).astype(x.dtype)

def rope_cos_sin(positions, rot_dim, dtype):
    inv = ROPE_THETA ** (-jnp.arange(0, rot_dim, 2, dtype=jnp.float32) / rot_dim)
    ang = positions.astype(jnp.float32)[..., None] * inv
    return jnp.cos(ang).astype(dtype), jnp.sin(ang).astype(dtype)

def apply_rope(x, cos, sin):
    x1, x2 = jnp.split(x, 2, axis=-1)
    return jnp.concatenate([x1 * cos - x2 * sin, x2 * cos + x1 * sin], axis=-1)

def partial_rope(x, cos, sin, rot):
    return jnp.concatenate([apply_rope(x[..., :rot], cos, sin), x[..., rot:]], axis=-1)

def to_blocks(t):
    B, S = t.shape[:2]
    return jnp.moveaxis(t.reshape((B, S // Q_BLOCK, Q_BLOCK) + t.shape[2:]), 1, 0)

def from_blocks(t):
    t = jnp.moveaxis(t, 0, 1)
    return t.reshape((t.shape[0], t.shape[1] * t.shape[2]) + t.shape[3:])

def causal_softmax(s, blk_idx, seq):
    q_pos = blk_idx * Q_BLOCK + jnp.arange(Q_BLOCK)
    mask = jnp.arange(seq)[None, :] <= q_pos[:, None]
    return jax.nn.softmax(jnp.where(mask, s, -jnp.inf), axis=-1)

def diff_attention_core(q1, q2, k1, k2, v, lam):
    S = q1.shape[1]
    scale = DA_HEAD_DIM ** -0.5

    def block(args):
        qa, qb, i = args
        s1 = jnp.einsum('bqhd,bkhd->bhqk', qa, k1, preferred_element_type=jnp.float32) * scale
        s2 = jnp.einsum('bqhd,bkhd->bhqk', qb, k2, preferred_element_type=jnp.float32) * scale
        a = causal_softmax(s1, i, S) - lam * causal_softmax(s2, i, S)
        return jnp.einsum('bhqk,bkhe->bqhe', a.astype(v.dtype), v)

    out = lax.map(block, (to_blocks(q1), to_blocks(q2), jnp.arange(S // Q_BLOCK)))
    return from_blocks(out)

def diff_attention(h, w_qkv, lam_vecs, subln_g, w_o, cos, sin, layer_idx):
    B, S, _ = h.shape
    n_qk = DA_HEADS * 2 * DA_HEAD_DIM
    q, k, v = jnp.split(h @ w_qkv, [n_qk, 2 * n_qk], axis=-1)
    c, s_ = cos[:, :, None, :], sin[:, :, None, :]
    q = partial_rope(q.reshape(B, S, 2 * DA_HEADS, DA_HEAD_DIM), c, s_, DA_ROT)
    k = partial_rope(k.reshape(B, S, 2 * DA_HEADS, DA_HEAD_DIM), c, s_, DA_ROT)
    q = q.reshape(B, S, DA_HEADS, 2, DA_HEAD_DIM)
    k = k.reshape(B, S, DA_HEADS, 2, DA_HEAD_DIM)
    v = v.reshape(B, S, DA_HEADS, 2 * DA_HEAD_DIM)
    lam_init = 0.8 - 0.6 * math.exp(-0.3 * layer_idx)
    lv = lam_vecs.astype(jnp.float32)
    lam = jnp.exp(jnp.sum(lv[0] * lv[1])) - jnp.exp(jnp.sum(lv[2] * lv[3])) + lam_init
    o = diff_attention_core(q[..., 0, :], q[..., 1, :], k[..., 0, :], k[..., 1, :], v, lam)
    o = rms_norm(o, subln_g, eps=SUBLN_EPS) * (1.0 - lam_init)
    return o.reshape(B, S, DA_HEADS * 2 * DA_HEAD_DIM) @ w_o

def shared_latent_kv(x, kv_in_norm_g, w_dkv, kv_norm_g, w_ukv, cos, sin):
    B, S, _ = x.shape
    kv_a = rms_norm(x, kv_in_norm_g) @ w_dkv
    c_kv = rms_norm(kv_a[..., :KV_LORA], kv_norm_g)
    k_rope = apply_rope(kv_a[..., KV_LORA:], cos, sin)
    kv = (c_kv @ w_ukv).reshape(B, S, MLA_HEADS, QK_NOPE + V_DIM)
    return kv[..., :QK_NOPE], k_rope, kv[..., QK_NOPE:]

def mla_core(q_nope, q_rope, k_nope, k_rope, v):
    S = q_nope.shape[1]
    scale = (QK_NOPE + QK_ROPE) ** -0.5

    def block(args):
        qn, qr, i = args
        s = (jnp.einsum('bqhd,bkhd->bhqk', qn, k_nope, preferred_element_type=jnp.float32)
             + jnp.einsum('bqhr,bkr->bhqk', qr, k_rope, preferred_element_type=jnp.float32)) * scale
        p = causal_softmax(s, i, S)
        return jnp.einsum('bhqk,bkhd->bqhd', p.astype(v.dtype), v)

    out = lax.map(block, (to_blocks(q_nope), to_blocks(q_rope), jnp.arange(S // Q_BLOCK)))
    return from_blocks(out)

def mla_attention(h, w_dq, q_norm_g, w_uq, w_o, k_nope, k_rope, v, cos, sin):
    B, S, _ = h.shape
    cq = rms_norm(h @ w_dq, q_norm_g)
    q = (cq @ w_uq).reshape(B, S, MLA_HEADS, QK_NOPE + QK_ROPE)
    q_rope = apply_rope(q[..., QK_NOPE:], cos[:, :, None, :], sin[:, :, None, :])
    o = mla_core(q[..., :QK_NOPE], q_rope, k_nope, k_rope, v)
    return o.reshape(B, S, MLA_HEADS * V_DIM) @ w_o

def sq_relu_mlp(h, w_up, w_down):
    return jnp.square(jax.nn.relu(h @ w_up)) @ w_down

def setup_inputs(seed: int = 0) -> dict:
    key = jax.random.key(seed)
    ks = jax.random.split(key, 24)
    f32 = jnp.float32

    def w(k, shape, fan_in):
        return jax.random.normal(k, shape, f32) * (fan_in ** -0.5)

    def gain(k, shape):
        return 1.0 + 0.02 * jax.random.normal(k, shape, f32)

    return {
        "x": jax.random.normal(ks[0], (BATCH, SEQ, D_MODEL), f32),
        "positions": jnp.broadcast_to(jnp.arange(SEQ, dtype=jnp.int32), (BATCH, SEQ)),
        "a_norm_g": gain(ks[1], (N_A, D_MODEL)),
        "a_w_qkv": w(ks[2], (N_A, D_MODEL, DA_QKV), D_MODEL),
        "a_lambda": 0.1 * jax.random.normal(ks[3], (N_A, 4, DA_HEAD_DIM), f32),
        "a_subln_g": gain(ks[4], (N_A, 2 * DA_HEAD_DIM)),
        "a_w_o": w(ks[5], (N_A, DA_HEADS * 2 * DA_HEAD_DIM, D_MODEL), DA_HEADS * 2 * DA_HEAD_DIM),
        "kv_in_norm_g": gain(ks[6], (D_MODEL,)),
        "w_dkv": w(ks[7], (D_MODEL, KV_LORA + QK_ROPE), D_MODEL),
        "kv_norm_g": gain(ks[8], (KV_LORA,)),
        "w_ukv": w(ks[9], (KV_LORA, MLA_HEADS * (QK_NOPE + V_DIM)), KV_LORA),
        "b_norm_g": gain(ks[10], (N_B, D_MODEL)),
        "b_w_dq": w(ks[11], (N_B, D_MODEL, Q_LORA), D_MODEL),
        "b_q_norm_g": gain(ks[12], (N_B, Q_LORA)),
        "b_w_uq": w(ks[13], (N_B, Q_LORA, MLA_HEADS * (QK_NOPE + QK_ROPE)), Q_LORA),
        "b_w_o": w(ks[14], (N_B, MLA_HEADS * V_DIM, D_MODEL), MLA_HEADS * V_DIM),
        "mlp_norm_g": gain(ks[15], (DEPTH, D_MODEL)),
        "w_up": w(ks[16], (DEPTH, D_MODEL, D_FF), D_MODEL),
        "w_down": w(ks[17], (DEPTH, D_FF, D_MODEL), D_FF),
        "final_norm_g": gain(ks[18], (D_MODEL,)),
    }

def reference(x, positions, a_norm_g, a_w_qkv, a_lambda, a_subln_g, a_w_o,
              kv_in_norm_g, w_dkv, kv_norm_g, w_ukv,
              b_norm_g, b_w_dq, b_q_norm_g, b_w_uq, b_w_o,
              mlp_norm_g, w_up, w_down, final_norm_g):
    cos_a, sin_a = rope_cos_sin(positions, DA_ROT, x.dtype)
    cos_b, sin_b = rope_cos_sin(positions, QK_ROPE, x.dtype)
    k_nope = k_rope = v = None
    for l in range(DEPTH):
        if l < N_A:
            x = x + diff_attention(rms_norm(x, a_norm_g[l]), a_w_qkv[l], a_lambda[l],
                                   a_subln_g[l], a_w_o[l], cos_a, sin_a, l)
        else:
            j = l - N_A
            if j == 0:
                k_nope, k_rope, v = shared_latent_kv(x, kv_in_norm_g, w_dkv, kv_norm_g,
                                                     w_ukv, cos_b, sin_b)
            x = x + mla_attention(rms_norm(x, b_norm_g[j]), b_w_dq[j], b_q_norm_g[j],
                                  b_w_uq[j], b_w_o[j], k_nope, k_rope, v, cos_b, sin_b)
        x = x + sq_relu_mlp(rms_norm(x, mlp_norm_g[l]), w_up[l], w_down[l])
    return rms_norm(x, final_norm_g)


_drawn_inputs = setup_inputs


def setup_inputs(seed=0):
    import zlib

    import numpy as np

    out = dict(_drawn_inputs(seed))
    spreads = {}
    factors = {'a_subln_g': 4.101,
     'kv_in_norm_g': 8.0,
     'kv_norm_g': 8.0,
     'b_norm_g': 8.0,
     'b_q_norm_g': 8.0,
     'mlp_norm_g': 2.714,
     'final_norm_g': 2.868}
    for name, (base, spread) in spreads.items():
        noise = np.random.default_rng([zlib.crc32(name.encode()), seed]).standard_normal(out[name].shape)
        drawn = base * np.exp(spread * noise) if base else spread * noise
        out[name] = __import__('jax').numpy.asarray(drawn.astype(out[name].dtype))
    for name, factor in factors.items():
        out[name] = (out[name] * factor).astype(out[name].dtype)
    return out
```

```python
from contextlib import ExitStack

import concourse.bass as bass
import numpy as np
from concourse import mybir

F32 = mybir.dt.float32
F32R = mybir.dt.float32r
I32 = mybir.dt.int32
ALU = mybir.AluOpType
ACT = mybir.ActivationFunctionType
AX = mybir.AxisListType

P = 128
SEQ, D = 256, 2048
TT = SEQ // P
KC = D // P
NB = 512
DFF = 4 * D
DA_HEADS, DA_DIM, DA_ROT = 8, 128, 32
MLA_HEADS, Q_LORA, KV_LORA, NOPE, ROPE, VDIM = 16, 384, 512, 128, 64, 128
THETA = 500000.0
EPS, SUB_EPS = 1e-6, 1e-5
LAM_INIT = 0.2
DA_SCALE = float(DA_DIM) ** -0.5
MLA_SCALE = float(NOPE + ROPE) ** -0.5
MASKED = -3.0e38
KEYS = P + 2 * P

DA_PAIRS = DA_HEADS // 2
QUARTERS = DFF // D
JB = D // NB
MLA_PAIRS = MLA_HEADS // 2

B_QKV = 0
B_WO = B_QKV + 3 * DA_PAIRS
B_MLP = [B_WO + JB, 0]
B_DKV = B_MLP[0] + 2 * JB * QUARTERS
B_RQ = B_DKV + 1
B_MLA = B_RQ + 1
B_BWO = B_MLA + MLA_PAIRS // 2
B_MLP[1] = B_BWO + JB
B_END = B_MLP[1] + 2 * JB * QUARTERS

U_WO = (2 * DA_PAIRS, DA_PAIRS)
U_MLP = [(U_WO[0] + 2, U_WO[1] + 2), None]
U_DKV = (U_MLP[0][0] + 16, U_MLP[0][1] + 16)
U_MLA = (U_DKV[0] + 1, U_DKV[1] + 1)
U_BWO = (U_MLA[0] + MLA_PAIRS, U_MLA[1] + MLA_PAIRS)
U_MLP[1] = (U_BWO[0] + 2, U_BWO[1] + 2)

G_A, G_MLP, G_KVIN, G_B, G_KV, G_Q, G_SUB, G_END = 0, (16, 32), 48, 64, 80, 84, 87, 89

V_INIT, V_WO, V_MLP0, V_BWO, V_MLP1 = 0, 4, 8, 12, 16

TWO_PI = 2 * np.pi


def twelve_bit_parts(value, n):
    parts = []
    for _ in range(n):
        e = np.floor(np.log2(abs(value))) - 11
        part = np.trunc(value / 2.0 ** e) * 2.0 ** e
        parts.append(float(part))
        value -= part
    return parts


def rope_frequencies():
    a = np.float32(THETA) ** (-np.arange(0, DA_ROT, 2, dtype=np.float32) / np.float32(DA_ROT))
    b = np.float32(THETA) ** (-np.arange(0, ROPE, 2, dtype=np.float32) / np.float32(ROPE))
    return np.tile(np.concatenate([a, b]).astype(np.float32)[None], (P, 1))


def trunk(nc, x, positions, a_norm_g, a_w_qkv, a_lambda, a_subln_g, a_w_o, kv_in_norm_g, w_dkv, kv_norm_g,
          w_ukv, b_norm_g, b_w_dq, b_q_norm_g, b_w_uq, b_w_o, mlp_norm_g, w_up, w_down, final_norm_g, freqs,
          out):
    def chunked(w):
        return w.rearrange("(c p) n -> p c n", p=P)

    W_QKV, W_O, W_BO = chunked(a_w_qkv[0]), chunked(a_w_o[0]), chunked(b_w_o[0])
    W_UP = [chunked(w_up[l]) for l in range(2)]
    W_DOWN = [chunked(w_down[l]) for l in range(2)]
    W_DKV, W_DQ, W_UKV, W_UQ = chunked(w_dkv), chunked(b_w_dq[0]), chunked(w_ukv), chunked(b_w_uq[0])
    x_tok = x[0].rearrange("(t p) n -> p t n", p=P)
    out_tok = out[0].rearrange("(t p) n -> p t n", p=P)

    with ExitStack() as ctx:
        def sb(name, shape, dt=F32):
            return ctx.enter_context(nc.sbuf_tensor(name, shape, dt))

        def psum(name, shape):
            return ctx.enter_context(nc.psum_tensor(name, shape, F32))

        def sem(name):
            return ctx.enter_context(nc.semaphore(name))

        xs = sb("xs", [P, TT, D])
        opA = sb("opA", [P, KC, 2, SEQ], F32R)
        opB = sb("opB", [P, KC, 2, SEQ], F32R)
        raw = sb("raw", [P, 4, 4, NB])
        whi = sb("whi", [P, 8, NB], F32R)
        wlo = sb("wlo", [P, 8, NB], F32R)
        stage = sb("stage", [P, TT, NB])
        kv_sb = sb("kv_sb", [P, 2, TT, NB])
        qkT = sb("qkT", [P, 2, 4 * SEQ])
        krT = sb("krT", [ROPE, SEQ])
        rope_a = sb("rope_a", [P, TT, 4, DA_ROT])
        rope_b = sb("rope_b", [P, TT, 4, DA_ROT])
        prob = sb("prob", [P, 4, KEYS])
        attn = sb("attn", [P, 2, KEYS])
        attnT = sb("attnT", [P, 2, KEYS])
        o_sb = sb("o_sb", [P, 2, TT, 2 * DA_DIM])
        relu_sb = sb("relu_sb", [P, 2 * NB])
        sq_sb = sb("sq_sb", [P, 2 * NB])
        junk = sb("junk", [P, 2, NB])
        mask = sb("mask", [P, KEYS])
        ident = sb("ident", [P, P])
        gains = sb("gains", [P, G_END])
        invf = sb("invf", [P, 48])
        pos_i = sb("pos_i", [P, TT], I32)
        pos_f = sb("pos_f", [P, TT])
        cosA, sinA = sb("cosA", [P, TT, DA_ROT]), sb("sinA", [P, TT, DA_ROT])
        cosB, sinB = sb("cosB", [P, TT, ROPE]), sb("sinB", [P, TT, ROPE])
        lam_s = sb("lam_s", [P, 8])
        neg_half = sb("neg_half", [P, 4])
        xss = sb("xss", [P, 5, TT, JB])
        xms = sb("xms", [P, 5, TT])
        xms2 = sb("xms2", [P, 5, TT])
        rs = sb("rs", [P, 5, TT])
        lss = sb("lss", [P, 2, TT])
        lms = sb("lms", [P, 2, TT])
        lrs = sb("lrs", [P, 2, TT])
        nmax = sb("nmax", [P, 4, TT])
        bias = sb("bias", [P, 4, TT])
        rowsum = sb("rowsum", [P, 4, TT])
        rinv = sb("rinv", [P, 4, TT])
        rneg = sb("rneg", [P, 4, TT])
        oss = sb("oss", [P, 4])
        oms = sb("oms", [P, 4])
        ors = sb("ors", [P, 4])
        qT = qkT[:, 0, :].rearrange("p (h t) -> p h t", h=4)
        kT = qkT[:, 1, :].rearrange("p (h t) -> p h t", h=4)
        g_out = qkT[:].rearrange("p a n -> p (a n)")
        gain_rows = relu_sb[0:G_END, 0:P]
        lam_rows = sq_sb[:, 0:4 * P].rearrange("p (a n) -> p a n", a=4)
        trig = prob[:, 0, :].rearrange("p (s w) -> p s w", s=2)[:, :, 0:TT * 48].rearrange(
            "p s (t f) -> p s t f", t=TT)
        turns = prob[:, 1, :].rearrange("p (s w) -> p s w", s=2)[:, :, 0:TT * 48].rearrange(
            "p s (t f) -> p s t f", t=TT)
        turns_lo = prob[:, 2, :].rearrange("p (s w) -> p s w", s=2)[:, :, 0:TT * 48].rearrange(
            "p s (t f) -> p s t f", t=TT)
        turns_hi = sb("turns_hi", [P, 2, TT, 48], F32R)

        acc = [psum(f"acc{s}", [P, 2, NB]) for s in range(2)]
        side = [psum(f"side{i}", [P, NB]) for i in range(4)]

        raw_ready = [sem(f"raw_ready{r}") for r in range(4)]
        dq_ready = [sem(f"dq_ready{r}") for r in range(4)]
        x_in = [sem(f"x_in{t}") for t in range(TT)]
        small_in = sem("small_in")
        gains_in = sem("gains_in")
        g_out_in = sem("g_out_in")
        out_done = sem("out_done")
        const_ready = sem("const_ready")
        gains_t = sem("gains_t")
        gains_ready = sem("gains_ready")
        trig_step = sem("trig_step")
        tables_ready = sem("tables_ready")
        lam_step = sem("lam_step")
        hi_ready = sem("hi_ready")
        lo_ready = sem("lo_ready")
        pe_halves = sem("pe_halves")
        drained = [sem(f"drained{s}") for s in range(2)]
        xT_done = sem("xT_done")
        xT_hi = sem("xT_hi")
        xT_lo = sem("xT_lo")
        xsq = sem("xsq")
        xstat = sem("xstat")
        rs_ready = sem("rs_ready")
        rope_parts = sem("rope_parts")
        roped = sem("roped")
        qkT_done = sem("qkT_done")
        qkT_ready = sem("qkT_ready")
        scores_done = sem("scores_done")
        masked = sem("masked")
        maxed = sem("maxed")
        bias_ready = sem("bias_ready")
        exp_done = sem("exp_done")
        rinv_ready = sem("rinv_ready")
        rneg_ready = sem("rneg_ready")
        half_attn = sem("half_attn")
        attn_ready = sem("attn_ready")
        attnT_done = sem("attnT_done")
        attnT_ready = sem("attnT_ready")
        pv_done = sem("pv_done")
        oss_ready = sem("oss_ready")
        oms_ready = sem("oms_ready")
        ors_ready = sem("ors_ready")
        o_ready = sem("o_ready")
        oT_done = sem("oT_done")
        opB_hi = sem("opB_hi")
        opB_lo = sem("opB_lo")
        relu_done = sem("relu_done")
        hid_hi = sem("hid_hi")
        hid_lo = sem("hid_lo")
        lat_ss = sem("lat_ss")
        lat_ms = sem("lat_ms")
        lat_rs = sem("lat_rs")
        latT_done = sem("latT_done")
        latT_hi = sem("latT_hi")
        latT_lo = sem("latT_lo")
        krT_ready = sem("krT_ready")
        xg_ready = sem("xg_ready")
        out_ready = [sem("out_ready0"), sem("out_ready1")]

        block = ctx.enter_context(nc.Block())

        @block.sync
        def _(sp):
            for t in range(TT):
                sp.dma_start(xs[:, t, :], x_tok[:, t, :]).then_inc(x_in[t], 16)

            def quad(b, r, src, first=False):
                if not first:
                    sp.wait_ge(lo_ready, 8 * b + 2 * r - 6)
                sp.dma_start(raw[:, r, 0:src.shape[1], 0:src.shape[2]], src).then_inc(raw_ready[r], 16)

            def whole(b, w, col, row=0, first=False):
                for r in range(4):
                    quad(b, r, w[:, bass.ds(row + 4 * r, 4), bass.ds(col, NB)], first)

            def qkv(p, first):
                whole(B_QKV + 3 * p, W_QKV, NB * p, first=first)
                whole(B_QKV + 3 * p + 1, W_QKV, NB * p + D)
                whole(B_QKV + 3 * p + 2, W_QKV, NB * p + 2 * D)

            qkv(0, True)
            with sp.Fori(1, DA_PAIRS) as p:
                qkv(p, False)
            with sp.Fori(0, JB) as j:
                whole(B_WO + j, W_O, NB * j)

            def mlp(l):
                with sp.Fori(0, QUARTERS) as q:
                    with sp.Fori(0, JB) as j:
                        whole(B_MLP[l] + 2 * JB * q + j, W_UP[l], D * q + NB * j)
                    with sp.Fori(0, JB) as j:
                        whole(B_MLP[l] + 2 * JB * q + JB + j, W_DOWN[l], NB * j, row=KC * q)

            mlp(0)
            whole(B_DKV, W_DKV, 0)
            for r in range(4):
                quad(B_RQ, r, W_DKV[:, 4 * r:4 * r + 4, KV_LORA:KV_LORA + ROPE])
                sp.dma_start(raw[:, r, :, ROPE:ROPE + Q_LORA], W_DQ[:, 4 * r:4 * r + 4, :]).then_inc(dq_ready[r], 16)
            with sp.Fori(0, MLA_PAIRS // 2) as g:
                for u in range(2):
                    quad(B_MLA + g, 2 * u, W_UKV[:, :, bass.ds(2 * NB * g + NB * u, NB)])
                    quad(B_MLA + g, 2 * u + 1, W_UQ[:, :, bass.ds(2 * Q_LORA * g + Q_LORA * u, Q_LORA)])
            with sp.Fori(0, JB) as j:
                whole(B_BWO + j, W_BO, NB * j)
            mlp(1)
            for j in range(JB):
                for t in range(TT):
                    sp.wait_ge(out_ready[t], j + 1)
                sp.dma_start(out_tok[:, :, NB * j:NB * j + NB], xs[:, :, NB * j:NB * j + NB]).then_inc(out_done, 16)
            sp.wait_ge(out_done, 16 * JB)

        @block.gpsimd
        def _(pool):
            nc.gpsimd.memset(neg_half[:], -0.5).then_inc(const_ready, 1)
            nc.gpsimd.memset(ident[:], 0.0).then_inc(const_ready, 1)
            nc.gpsimd.memset(mask[:], 0.0).then_inc(const_ready, 1)
            pool.wait_ge(const_ready, 3)
            nc.gpsimd.affine_select(out=ident[:], in_=ident[:], compare_op=ALU.not_equal, fill=1.0, base=0,
                                    pattern=[[-1, P]], channel_multiplier=1).then_inc(const_ready, 1)
            for c in (0, 2 * P):
                nc.gpsimd.affine_select(out=mask[:, c:c + P], in_=mask[:, c:c + P], compare_op=ALU.is_ge,
                                        fill=MASKED, base=0, pattern=[[-1, P]],
                                        channel_multiplier=1).then_inc(const_ready, 1)

            def stream_scale(t):
                pool.wait_ge(xstat, 2 * t + 2)
                nc.gpsimd.tensor_tensor(rs[:, t, :], xms2[:, t, :], neg_half[:, 0:TT], ALU.pow).then_inc(rs_ready, 1)

            def sub_norm(p):
                pool.wait_ge(oms_ready, p + 1)
                nc.gpsimd.tensor_tensor(ors[:], oms[:], neg_half[:], ALU.pow).then_inc(ors_ready, 1)

            stream_scale(0)
            with pool.Fori(0, DA_PAIRS) as p:
                sub_norm(p)
            stream_scale(2)
            for k in range(2):
                pool.wait_ge(lat_ms, k + 1)
                nc.gpsimd.tensor_tensor(lrs[:, k, :], lms[:, k, :], neg_half[:, 0:TT], ALU.pow).then_inc(lat_rs, 1)
            stream_scale(4)

        @block.tensor
        def _(pe):
            mm, tr = nc.tensor.matmul, nc.tensor.transpose

            def wait_set(s, uses):
                pe.wait_ge(drained[s], 2 * uses)

            def half_tok(b, hf, s, op, n=NB, chunks=2, first=False, last=False):
                pe.wait_ge(lo_ready, 8 * b + hf + 1)
                place = 2 * (hf % 4)
                for c in range(chunks):
                    for t in range(TT):
                        a_hi, a_lo = (op[c][i][:, P * t:P * t + P] for i in range(2))
                        w_hi, w_lo = whi[:, place + c, 0:n], wlo[:, place + c, 0:n]
                        o = acc[s][:, t, 0:n]
                        mm(o, a_hi, w_hi, start=first and c == 0, stop=False)
                        mm(o, a_hi, w_lo, start=False, stop=False)
                        done = mm(o, a_lo, w_hi, start=False, stop=last and c == chunks - 1)
                done.then_inc(pe_halves, 1)

            def chunks_of(buf, c0, n=2):
                return [[buf[:, c0 + c, i, :] for i in range(2)] for c in range(n)]

            def block_tok(b, s, uses, buf, n=NB, ready=None, aside=None):
                if not (isinstance(uses, int) and uses == 0):
                    wait_set(s, uses)
                for hf in range(8):
                    if ready and hf % 2 == 0:
                        ready(hf // 2)
                    half_tok(b, hf, s, chunks_of(buf, 2 * hf), n, first=hf == 0, last=hf == 7)
                    if aside and hf in aside:
                        aside[hf]()

            def block_feat(b, s, uses):
                wait_set(s, uses)
                for hf in range(8):
                    pe.wait_ge(lo_ready, 8 * b + hf + 1)
                    place = 2 * (hf % 4)
                    for c in range(2):
                        x_hi, x_lo = (opA[:, 2 * hf + c, i, :] for i in range(2))
                        for f in range(4):
                            w_hi = whi[:, place + c, P * f:P * f + P]
                            w_lo = wlo[:, place + c, P * f:P * f + P]
                            o = acc[s][:, f // 2, SEQ * (f % 2):SEQ * (f % 2) + SEQ]
                            first = hf == 0 and c == 0 and f % 2 == 0
                            end = hf == 7 and c == 1 and f % 2 == 1
                            mm(o, w_hi, x_hi, start=first, stop=False, skip_group_check=True)
                            mm(o, w_hi, x_lo, start=False, stop=False, skip_group_check=True)
                            done = mm(o, w_lo, x_hi, start=False, stop=end, skip_group_check=True)
                    done.then_inc(pe_halves, 1)

            def transpose_x(v, s=None, uses=None):
                if s is not None:
                    pe.wait_ge(drained[s], 2 * uses)
                if v >= 2:
                    pe.wait_ge(xT_lo, 4 * (v - 1))
                j = v % JB
                for k in range(2):
                    bank = side[2 * (v % 2) + k]
                    for cc in range(2):
                        for t in range(TT):
                            col = NB * j + P * (2 * k + cc)
                            done = tr(bank[:, SEQ * cc + P * t:SEQ * cc + P * t + P], xs[:, t, col:col + P], ident[:])
                    done.then_inc(xT_done, 1)

            pe.wait_ge(const_ready, 4)
            pe.wait_ge(gains_in, 16 * 8)
            tr(side[3][:, 0:G_END], gain_rows, ident[0:G_END, 0:G_END]).then_inc(gains_t, 1)
            for t in range(TT):
                pe.wait_ge(x_in[t], 16)
            pe.wait_ge(gains_ready, 2)
            for v in range(JB):
                transpose_x(V_INIT + v)

            def transpose_qk(i, b0):
                pe.wait_ge(roped, i + 1)
                for hh in range(4):
                    for t in range(TT):
                        done = tr(side[b0 + hh // 2][:, SEQ * (hh % 2) + P * t:SEQ * (hh % 2) + P * t + P],
                                  stage[:, t, P * hh:P * hh + P], ident[:])
                done.then_inc(qkT_done, 1)

            def da_scores(p):
                pe.wait_ge(qkT_ready, 4 * p + 4)
                for m in range(4):
                    mm(side[m][:, 0:P], qT[:, m, 0:P], kT[:, m, 0:P], start=True, stop=True)
                    mm(side[m][:, P:KEYS], qT[:, m, P:SEQ], kT[:, m, :], start=True,
                       stop=True).then_inc(scores_done, 1)

            def transpose_attn(heads_before, b0, masks):
                pe.wait_ge(masked, masks)
                for h in range(2):
                    pe.wait_ge(attn_ready, 2 * heads_before + 2 * h + 2)
                    for k in range(3):
                        done = tr(side[b0 + h][:, P * k:P * k + P], attn[:, h, P * k:P * k + P], ident[:])
                    done.then_inc(attnT_done, 1)

            def da_values(p, v_drained, banks_read=None):
                pe.wait_ge(drained[0], v_drained)
                if banks_read is not None:
                    pe.wait_ge(qkT_ready, banks_read)
                for h in range(2):
                    pe.wait_ge(attnT_ready, 2 * p + h + 1)
                    cols = slice(2 * DA_DIM * h, 2 * DA_DIM * (h + 1))
                    mm(side[h][:, 0:SEQ], attnT[:, h, 0:P], kv_sb[:, 0, 0, cols], start=True, stop=True)
                    mm(side[h][:, SEQ:NB], attnT[:, h, P:2 * P], kv_sb[:, 0, 0, cols], start=True, stop=False)
                    mm(side[h][:, SEQ:NB], attnT[:, h, 2 * P:KEYS], kv_sb[:, 0, 1, cols], start=False,
                       stop=True).then_inc(pv_done, 1)

            def transpose_o(p):
                pe.wait_ge(o_ready, p + 1)
                for h in range(2):
                    for e in range(2):
                        for t in range(TT):
                            done = tr(side[h][:, SEQ * e + P * t:SEQ * e + P * t + P], o_sb[:, h, t, P * e:P * e + P],
                                      ident[:])
                    done.then_inc(oT_done, 1)

            def opA_ready(first):
                return lambda g: pe.wait_ge(xT_lo, 4 * (first + g) + 4)

            def qkv(p, first):
                b = B_QKV + 3 * p
                prev = None if first else p - 1
                block_tok(b, 0, 2 * p, opA, ready=opA_ready(V_INIT) if first else None,
                          aside={} if first else {1: lambda: da_scores(prev)})
                block_tok(b + 1, 1, p, opA, aside={2: lambda: transpose_qk(2 * p, 0)} if first else {
                    1: lambda: transpose_attn(2 * prev, 2, 4 * prev + 4),
                    2: lambda: transpose_qk(2 * p, 0),
                    4: lambda: da_values(prev, 4 * prev + 4, 4 * prev + 6)})
                aside = {3: lambda: transpose_qk(2 * p + 1, 2)}
                if not first:
                    aside[1] = lambda: transpose_o(prev)
                block_tok(b + 2, 0, 2 * p + 1, opA, aside=aside)

            qkv(0, True)
            with pe.Fori(1, DA_PAIRS) as p:
                qkv(p, False)

            last = DA_PAIRS - 1
            block_tok(B_WO, 1, U_WO[1], opB, ready=lambda g: pe.wait_ge(opB_lo, 4 * g + 4), aside={
                1: lambda: da_scores(last),
                3: lambda: transpose_attn(2 * last, 2, 4 * last + 4),
                4: lambda: da_values(last, 4 * last + 4),
                5: lambda: transpose_o(last)})

            def out_proj(b0, uses, v0):
                for j in range(1, JB):
                    s, ps = (j + 1) % 2, j % 2
                    block_tok(b0 + j, s, uses[s] + j // 2, opB, aside={
                        1: lambda: transpose_x(v0 + j - 1, ps, uses[ps] + (j - 1) // 2 + 1)})
                transpose_x(v0 + JB - 1, 0, uses[0] + 2)

            out_proj(B_WO, U_WO, V_WO)

            def mlp(l, v_in, v_out):
                u = U_MLP[l]

                def up(q):
                    with pe.Fori(0, JB // 2) as i:
                        for k in range(2):
                            block_feat(B_MLP[l] + 2 * JB * q + 2 * i + k, 1 - k, u[1 - k] + JB * q + i)

                def hidden_ready(q):
                    return lambda g: pe.wait_ge(hid_lo, 2 * (JB * (QUARTERS * l + q) + g) + 2)

                pe.wait_ge(xT_lo, 4 * v_in + 4 * JB)
                with pe.Fori(0, QUARTERS - 1) as q:
                    up(q)
                    with pe.Fori(0, JB // 2) as i:
                        for k in range(2):
                            block_tok(B_MLP[l] + 2 * JB * q + JB + 2 * i + k, 1 - k, u[1 - k] + JB * q + 2 + i, opB,
                                      ready=hidden_ready(q))
                q = QUARTERS - 1
                up(q)
                for j in range(JB):
                    s, ps = (j + 1) % 2, j % 2
                    aside = {}
                    if v_out is not None and j:
                        aside[1] = lambda: transpose_x(v_out + j - 1, ps, u[ps] + JB * q + 2 + (j - 1) // 2 + 1)
                    block_tok(B_MLP[l] + 2 * JB * q + JB + j, s, u[s] + JB * q + 2 + j // 2, opB,
                              ready=hidden_ready(q), aside=aside)
                if v_out is not None:
                    transpose_x(v_out + JB - 1, 0, u[0] + JB * q + 4)

            mlp(0, V_WO, V_MLP0)

            def transpose_ckv():
                pe.wait_ge(drained[1], 2 * (U_DKV[1] + 1))
                pe.wait_ge(xT_lo, 4 * (V_MLP0 + JB))
                for k in range(2):
                    for cc in range(2):
                        for t in range(TT):
                            col = P * (2 * k + cc)
                            done = tr(side[k][:, SEQ * cc + P * t:SEQ * cc + P * t + P], stage[:, t, col:col + P], ident[:])
                    done.then_inc(latT_done, 1)

            block_tok(B_DKV, 1, U_DKV[1], opA, ready=opA_ready(V_MLP0))
            block_tok(B_RQ, 0, U_DKV[0], opA, n=ROPE + Q_LORA, aside={2: transpose_ckv})
            pe.wait_ge(drained[0], 2 * (U_DKV[0] + 1))
            for c in range(3):
                for t in range(TT):
                    bank, col = (side[3], SEQ * c) if c < 2 else (side[2], SEQ)
                    done = tr(bank[:, col + P * t:col + P * t + P], kv_sb[:, 1, t, ROPE + P * c:ROPE + P * c + P], ident[:])
            pe.wait_ge(roped, 2 * DA_PAIRS + 1)
            for t in range(TT):
                done = tr(side[2][0:ROPE, P * t:P * t + P], kv_sb[:, 1, t, 0:ROPE], ident[:])
            done.then_inc(latT_done, 1)

            ckvT = chunks_of(opB, 12, 4)
            cqT = chunks_of(opA, 0, 3)
            qh = qT[:, 0:2, :]
            qr = qT[0:ROPE, 2:4, :]
            kh = kT[:, 0:2, :]

            def mla_transposes(p, par):
                pe.wait_ge(drained[1], 2 * (U_MLA[1] + p) + 2)
                pe.wait_ge(opB_lo, DA_PAIRS * 4 + p)
                for h in range(2):
                    for t in range(TT):
                        done = tr(side[0][:, SEQ * h + P * t:SEQ * h + P * t + P],
                                  kv_sb[:, par, t, 2 * P * h:2 * P * h + P], ident[:])
                done.then_inc(qkT_done, 1)
                pe.wait_ge(roped, 2 * DA_PAIRS + 2 + p)
                for h in range(2):
                    for t in range(TT):
                        done = tr(side[1][:, SEQ * h + P * t:SEQ * h + P * t + P],
                                  stage[:, t, 192 * h:192 * h + P], ident[:])
                done.then_inc(qkT_done, 1)
                for h in range(2):
                    for t in range(TT):
                        done = tr(side[2][0:ROPE, SEQ * h + P * t:SEQ * h + P * t + P],
                                  stage[:, t, 192 * h + P:192 * h + P + ROPE], ident[:])
                done.then_inc(qkT_done, 1)

            def mla_scores(p):
                pe.wait_ge(qkT_ready, 2 * DA_PAIRS * 2 + 3 * p + 3)
                for h in range(2):
                    bank = side[3 * (1 - h)]
                    for q0, q1, k1, o0, o1 in ((0, P, P, 0, P), (P, SEQ, SEQ, P, KEYS)):
                        mm(bank[:, o0:o1], qh[:, h, q0:q1], kh[:, h, 0:k1], start=True, stop=False)
                        done = mm(bank[:, o0:o1], qr[:, h, q0:q1], krT[:, 0:k1], start=False, stop=True)
                    done.then_inc(scores_done, 1)

            def mla_values(p, par):
                for h in range(2):
                    pe.wait_ge(attnT_ready, DA_HEADS + 2 * p + h + 1)
                    v = slice(2 * P * h + P, 2 * P * (h + 1))
                    mm(side[1][:, SEQ * h:SEQ * (h + 1)], kv_sb[:, par, 0, v], attnT[:, h, 0:SEQ], start=True,
                       stop=False, skip_group_check=True)
                    done = mm(side[1][:, SEQ * h + P:SEQ * (h + 1)], kv_sb[:, par, 1, v], attnT[:, h, SEQ:KEYS],
                              start=False, stop=True, skip_group_check=True)
                done.then_inc(pv_done, 1)

            def mla_weightsT(p):
                transpose_attn(DA_HEADS + 2 * p, 2, 4 * DA_PAIRS + 2 * p + 2)

            def mla_pair(g, u, p, with_prev):
                b = B_MLA + g
                wait_set(1, U_MLA[1] + p)
                half_tok(b, 4 * u, 1, ckvT[0:2], first=True)
                if with_prev:
                    mla_transposes(p - 1, 1 - u)
                half_tok(b, 4 * u + 1, 1, ckvT[2:4], last=True)
                if with_prev:
                    mla_scores(p - 1)
                wait_set(0, U_MLA[0] + p)
                half_tok(b, 4 * u + 2, 0, cqT[0:2], n=Q_LORA, first=True)
                half_tok(b, 4 * u + 3, 0, cqT[2:3], n=Q_LORA, chunks=1, last=True)
                if with_prev:
                    mla_weightsT(p - 1)
                    mla_values(p - 1, 1 - u)

            pe.wait_ge(latT_lo, 7)
            pe.wait_ge(krT_ready, 1)
            mla_pair(0, 0, 0, False)
            with pe.Fori(0, MLA_PAIRS // 2 - 1) as g:
                mla_pair(g, 1, 2 * g + 1, True)
                mla_pair(g + 1, 0, 2 * g + 2, True)
            mla_pair(MLA_PAIRS // 2 - 1, 1, MLA_PAIRS - 1, True)

            last_pair = MLA_PAIRS - 1

            def heads_ready(g):
                pe.wait_ge(opB_lo, 4 * DA_PAIRS + 2 * g + 2)

            block_tok(B_BWO, 1, U_BWO[1], opB, ready=heads_ready, aside={
                0: lambda: mla_transposes(last_pair, 1),
                1: lambda: mla_scores(last_pair),
                3: lambda: mla_weightsT(last_pair),
                4: lambda: mla_values(last_pair, 1)})
            out_proj(B_BWO, U_BWO, V_BWO)
            mlp(1, V_BWO, None)

        @block.scalar
        def _(act):
            fn = nc.scalar.activation

            act.dma_start(pos_i[:], positions.rearrange("a (t p) -> p (a t)", p=P),
                          allow_slow_non_contiguous=True).then_inc(small_in, 16)
            act.dma_start(invf[:], freqs).then_inc(small_in, 16)
            act.dma_start(lam_rows, a_lambda.rearrange("a r n -> (a r n)").partition_broadcast(P).rearrange(
                "p (r n) -> p r n", r=4)).then_inc(small_in, 16)
            for row, g in ((G_A, a_norm_g[0]), (G_MLP[0], mlp_norm_g[0]), (G_MLP[1], mlp_norm_g[1]),
                           (G_KVIN, kv_in_norm_g), (G_B, b_norm_g[0]), (G_KV, kv_norm_g), (G_Q, b_q_norm_g[0]),
                           (G_SUB, a_subln_g[0])):
                n = g.shape[0] // P
                act.dma_start(gain_rows[row:row + n, :], g.rearrange("(c p) -> c p", p=P)).then_inc(gains_in, 16)

            def split(b, hf, kind=None):
                r = hf // 2
                c0, place = 2 * (hf % 2), 2 * (hf % 4)
                act.wait_ge(raw_ready[r], 16 * b + 16)
                if kind == "rq":
                    act.wait_ge(dq_ready[r], 16)
                if not isinstance(b, int) or 8 * b + hf >= 4:
                    act.wait_ge(pe_halves, 8 * b + hf - 3)
                if kind in ("dkv", "rq"):
                    for c in range(2):
                        k = 4 * r + c0 + c
                        parts = [(0, NB, G_KVIN)] if kind == "dkv" else [(0, ROPE, G_KVIN), (ROPE, ROPE + Q_LORA, G_B)]
                        for n0, n1, g in parts:
                            done = fn(whi[:, place + c, n0:n1], raw[:, r, c0 + c, n0:n1], ACT.Copy,
                                      scale=gains[:, g + k:g + k + 1])
                else:
                    n, ch = (Q_LORA, 2 - hf % 2) if kind == "mla" and r % 2 else (NB, 2)
                    done = fn(whi[:, place:place + ch, 0:n], raw[:, r, c0:c0 + ch, 0:n], ACT.Copy)
                done.then_inc(hi_ready, 1)

            def body(b, asides=None, kind=None, nxt=None):
                for hf in range(3, 11):
                    if hf < 8:
                        split(b, hf, kind)
                    else:
                        split(b + 1, hf - 8, nxt)
                    if asides and hf in asides:
                        asides[hf]()

            def used(b):
                act.wait_ge(pe_halves, 8 * b + 8)

            def x_squares(v, s, uses):
                act.wait_ge(drained[s], 2 * uses)
                j = v % JB
                for t in range(TT):
                    if v or t:
                        act.wait_ge(xsq, 2 * v + t)
                    fn(junk[:, 0, :], xs[:, t, NB * j:NB * j + NB], ACT.Square,
                       accum_out=xss[:, v // JB, t, j:j + 1]).then_inc(xsq, 1)

            def x_hi(v, gain):
                j = v % JB
                for k in range(2):
                    act.wait_ge(xT_done, 2 * v + k + 1)
                    for cc in range(2):
                        c = JB * j + 2 * k + cc
                        g = {} if gain is None else {"scale": gains[:, gain + c:gain + c + 1]}
                        fn(opA[:, c, 0, :], side[2 * (v % 2) + k][:, SEQ * cc:SEQ * cc + SEQ], ACT.Copy,
                           **g).then_inc(xT_hi, 1)

            act.wait_ge(lam_step, 2)
            fn(lam_s[:, 2:4], lam_s[:, 0:2], ACT.Exp).then_inc(lam_step, 1)
            act.wait_ge(trig_step, 15)
            tables = ((cosA, 1, 0, 16, 1.0, 1.0), (sinA, 0, 0, 16, -1.0, 1.0), (cosB, 1, 16, 32, 1.0, 1.0),
                      (sinB, 0, 16, 32, -1.0, 1.0))
            for tab, k, f0, n, s0, s1 in tables:
                fn(tab[:, :, 0:n], trig[:, k, :, f0:f0 + n], ACT.Sin, scale=s0)
                fn(tab[:, :, n:2 * n], trig[:, k, :, f0:f0 + n], ACT.Sin, scale=s1).then_inc(tables_ready, 1)
            act.wait_ge(gains_ready, 2)
            for v in range(JB):
                x_hi(V_INIT + v, G_A)
            for hf in range(3):
                split(0, hf)
            for t in range(TT):
                act.wait_ge(x_in[t], 16)
            for v in range(JB):
                for t in range(TT):
                    if v or t:
                        act.wait_ge(xsq, 2 * v + t)
                    fn(junk[:, 0, :], xs[:, t, NB * v:NB * v + NB], ACT.Square,
                       accum_out=xss[:, 0, t, v:v + 1]).then_inc(xsq, 1)

            def drain_scaled(b, s, dst, scale, n=NB):
                used(b)
                for t in range(TT):
                    fn(dst(t), acc[s][:, t, 0:n], ACT.Copy, scale=scale(t)).then_inc(drained[s], 1)

            def drain_qkv(b, s, dst, i=None):
                act.wait_ge(rs_ready, 1)
                if i is not None and not (isinstance(i, int) and i == 0):
                    act.wait_ge(qkT_done, i)
                drain_scaled(b, s, lambda t: dst[:, t, :], lambda t: rs[:, 0, t:t + 1])

            def copy_qkT(i, dst, b0):
                act.wait_ge(qkT_done, i + 1)
                for k in range(2):
                    fn(dst[:, 2 * k:2 * k + 2, :], side[b0 + k][:].rearrange("p (h t) -> p h t", h=2),
                       ACT.Copy).then_inc(qkT_ready, 1)

            def exps(maps_before, maps, banks, scale):
                for m in maps:
                    act.wait_ge(bias_ready, maps_before + m + 1)
                    for t, (c0, c1) in enumerate(((0, P), (P, KEYS))):
                        done = fn(prob[:, banks[m], c0:c1], prob[:, banks[m], c0:c1], ACT.Exp, scale=scale,
                                  bias=bias[:, banks[m], t:t + 1], accum_out=rowsum[:, banks[m], t:t + 1])
                    done.then_inc(exp_done, 1)

            def copy_attnT(heads_before, b0):
                for h in range(2):
                    act.wait_ge(attnT_done, heads_before + h + 1)
                    fn(attnT[:, h, :], side[b0 + h][:, 0:KEYS], ACT.Copy).then_inc(attnT_ready, 1)

            def o_squares(p):
                for h in range(2):
                    act.wait_ge(pv_done, 2 * p + h + 1)
                    for t in range(TT):
                        done = fn(junk[:, h, SEQ * t:SEQ * t + SEQ], side[h][:, SEQ * t:SEQ * t + SEQ], ACT.Square,
                                  accum_out=oss[:, 2 * h + t:2 * h + t + 1])
                done.then_inc(oss_ready, 1)

            def o_hi(p):
                for h in range(2):
                    act.wait_ge(oT_done, 2 * p + h + 1)
                    for e in range(2):
                        fn(opB[:, bass.ds(4 * p + 2 * h + e, 1), 0, :], side[h][:, SEQ * e:SEQ * e + SEQ].unsqueeze(1),
                           ACT.Copy, scale=gains[:, G_SUB + e:G_SUB + e + 1]).then_inc(opB_hi, 1)

            def qkv(p, first):
                b = B_QKV + 3 * p
                pv = None if first else p - 1
                body(b, {} if first else {5: lambda: exps(4 * pv, (0, 1), (0, 1, 2, 3), DA_SCALE),
                                          6: lambda: exps(4 * pv, (2, 3), (0, 1, 2, 3), DA_SCALE)})
                drain_qkv(b, 0, stage, 2 * p)
                body(b + 1, {5: lambda: copy_qkT(2 * p, qT, 0)} if first else {
                    4: lambda: copy_attnT(2 * pv, 2),
                    5: lambda: copy_qkT(2 * p, qT, 0),
                    7: lambda: o_squares(pv)})
                drain_qkv(b + 1, 1, stage, 2 * p + 1)
                asides = {6: lambda: copy_qkT(2 * p + 1, kT, 2)}
                if not first:
                    asides[4] = lambda: o_hi(pv)
                body(b + 2, asides)
                drain_qkv(b + 2, 0, kv_sb[:, 0])

            qkv(0, True)
            with act.Fori(1, DA_PAIRS) as p:
                qkv(p, False)
            last = DA_PAIRS - 1

            def rest():
                copy_attnT(2 * last, 2)
                o_squares(last)
                o_hi(last)

            body(B_WO, {5: lambda: exps(4 * last, (0, 1), (0, 1, 2, 3), DA_SCALE),
                        6: lambda: exps(4 * last, (2, 3), (0, 1, 2, 3), DA_SCALE), 7: rest})

            def out_proj(b0, uses, v0, gain):
                x_squares(v0, 1, uses[1] + 1)
                for j in range(1, JB):
                    s = (j + 1) % 2
                    body(b0 + j, {4: lambda: x_hi(v0 + j - 1, gain)})
                    x_squares(v0 + j, s, uses[s] + j // 2 + 1)
                x_hi(v0 + JB - 1, gain)

            out_proj(B_WO, U_WO, V_WO, G_MLP[0])

            def mlp(l, v_out, nxt, squares_from):
                u = U_MLP[l]

                def drain_up(b, s, t):
                    used(b)
                    for k in range(2):
                        fn(relu_sb[:, NB * k:NB * k + NB], acc[s][:, k, :], ACT.Relu).then_inc(relu_done, 1)

                def hid_hi_part(s, uses, t, j):
                    for k in range(2):
                        act.wait_ge(drained[s], 2 * uses + k + 1)
                        fn(opB[:, bass.ds(4 * j + 2 * k, 2), 0, :],
                           sq_sb[:, NB * k:NB * k + NB].rearrange("p (c t) -> p c t", c=2),
                           ACT.Copy).then_inc(hid_hi, 1)

                def up(q):
                    with act.Fori(0, JB // 2) as i:
                        for k in range(2):
                            b, s = B_MLP[l] + 2 * JB * q + 2 * i + k, 1 - k
                            body(b)
                            t = JB * (QUARTERS * l + q) + 2 * i + k
                            drain_up(b, s, t)
                            hid_hi_part(s, u[s] + JB * q + i, t, 2 * i + k)

                with act.Fori(0, QUARTERS - 1) as q:
                    up(q)
                    with act.Fori(0, JB) as j:
                        body(B_MLP[l] + 2 * JB * q + JB + j)
                q = QUARTERS - 1
                up(q)
                for j in range(JB):
                    s = (j + 1) % 2
                    asides = {}
                    if v_out is not None and j:
                        asides[4] = lambda: x_hi(v_out + j - 1, None)
                    if l == 1 and j == JB - 1:
                        for hf in range(3, 8):
                            split(B_MLP[l] + 2 * JB * q + JB + j, hf)
                    else:
                        body(B_MLP[l] + 2 * JB * q + JB + j, asides, nxt=nxt if j == JB - 1 else None)
                    x_squares(squares_from + j, s, u[s] + JB * q + 2 + j // 2 + 1)
                if v_out is not None:
                    x_hi(v_out + JB - 1, None)

            mlp(0, V_MLP0, "dkv", V_MLP0)

            def latent(k, b, s, dst, n, c0):
                act.wait_ge(rs_ready, 3)
                used(b)
                for t in range(TT):
                    if k or t:
                        act.wait_ge(lat_ss, 2 * k + t)
                    fn(junk[:, 0, 0:n - c0], acc[s][:, t, c0:n], ACT.Square, scale=rs[:, 2, t:t + 1],
                       accum_out=lss[:, k, t:t + 1]).then_inc(lat_ss, 1)
                for t in range(TT):
                    fn(dst[:, t, 0:n], acc[s][:, t, 0:n], ACT.Copy, scale=rs[:, 2, t:t + 1]).then_inc(drained[s], 1)

            def latent_hi(buf, c0, n, bank, before, gain, done_at):
                act.wait_ge(latT_done, done_at)
                for c in range(n):
                    b, col = bank(c)
                    fn(buf[:, c0 + c, 0, :], b[:, col:col + SEQ], ACT.Copy,
                       scale=gains[:, gain + c:gain + c + 1]).then_inc(latT_hi, 1)

            body(B_DKV, kind="dkv", nxt="rq")
            latent(0, B_DKV, 1, stage, KV_LORA, 0)
            body(B_RQ, {5: lambda: latent_hi(opB, 12, 4, lambda c: (side[c // 2], SEQ * (c % 2)), 0, G_KV, 2)},
                 kind="rq", nxt="mla")
            latent(1, B_RQ, 0, kv_sb[:, 1], ROPE + Q_LORA, ROPE)
            act.wait_ge(latT_done, 3)
            fn(krT[:], side[2][0:ROPE, 0:SEQ], ACT.Copy).then_inc(krT_ready, 1)
            latent_hi(opA, 0, 3, lambda c: (side[3], SEQ * c) if c < 2 else (side[2], SEQ), 4, G_Q, 3)

            def mla_drain(b, hf, s, dst, scale, n):
                act.wait_ge(pe_halves, 8 * b + hf + 1)
                for t in range(TT):
                    fn(dst[:, t, 0:n], acc[s][:, t, 0:n], ACT.Copy, scale=scale(t)).then_inc(drained[s], 1)

            def mla_copies(p):
                for k, (dst, src) in enumerate(((kT[:, 0:2, :], side[0][:]), (qT[:, 0:2, :], side[1][:]))):
                    act.wait_ge(qkT_done, 2 * DA_PAIRS + 3 * p + k + 1)
                    fn(dst, src.rearrange("p (h t) -> p h t", h=2), ACT.Copy).then_inc(qkT_ready, 1)
                act.wait_ge(qkT_done, 2 * DA_PAIRS + 3 * p + 3)
                fn(qT[0:ROPE, 2:4, :], side[2][0:ROPE, :].rearrange("p (h t) -> p h t", h=2),
                   ACT.Copy).then_inc(qkT_ready, 1)

            def mla_exps(p):
                exps(4 * DA_PAIRS + 2 * p, (0, 1), (0, 1), MLA_SCALE)

            def mla_hi(p):
                act.wait_ge(pv_done, DA_HEADS + p + 1)
                fn(opB[:, bass.ds(2 * p, 2), 0, :], side[1][:].rearrange("p (h t) -> p h t", h=2),
                   ACT.Copy).then_inc(opB_hi, 1)

            def mla_pair(g, u, p, with_prev, nb=None, nxt="mla"):
                b = B_MLA + g
                nb, h0 = (b, 4) if u == 0 else (b + 1, 0)
                split(b, 4 * u + 3, "mla")
                if with_prev:
                    mla_copies(p - 1)
                split(nb, h0, nxt)
                if with_prev:
                    mla_exps(p - 1)
                split(nb, h0 + 1, nxt)
                split(nb, h0 + 2, nxt)
                mla_drain(b, 4 * u + 1, 1, kv_sb[:, u], lambda t: lrs[:, 0, t:t + 1], NB)
                mla_drain(b, 4 * u + 3, 0, stage, lambda t: lrs[:, 1, t:t + 1], Q_LORA)
                if with_prev:
                    copy_attnT(DA_HEADS + 2 * (p - 1), 2)
                    mla_hi(p - 1)

            act.wait_ge(lat_rs, 2)
            mla_pair(0, 0, 0, False)
            with act.Fori(0, MLA_PAIRS // 2 - 1) as g:
                mla_pair(g, 1, 2 * g + 1, True)
                mla_pair(g + 1, 0, 2 * g + 2, True)
            mla_pair(MLA_PAIRS // 2 - 1, 1, MLA_PAIRS - 1, True, nxt=None)

            last_pair = MLA_PAIRS - 1

            def mla_rest():
                copy_attnT(DA_HEADS + 2 * last_pair, 2)
                mla_hi(last_pair)

            body(B_BWO, {3: lambda: mla_copies(last_pair), 5: lambda: mla_exps(last_pair), 7: mla_rest})
            out_proj(B_BWO, U_BWO, V_BWO, G_MLP[1])
            act.wait_ge(opB_lo, 4 * DA_PAIRS + MLA_PAIRS)
            act.dma_start(g_out, final_norm_g.partition_broadcast(P)).then_inc(g_out_in, 16)
            mlp(1, None, None, V_MLP1)
            act.wait_ge(rs_ready, 5)
            for j in range(JB):
                act.wait_ge(xg_ready, 2 * j + 1)
                fn(xs[:, 0, NB * j:NB * j + NB], xs[:, 0, NB * j:NB * j + NB], ACT.Copy,
                   scale=rs[:, 4, 0:1]).then_inc(out_ready[0], 1)

        @block.vector
        def _(dve):
            tt_, ts_, stt = nc.vector.tensor_tensor, nc.vector.tensor_scalar, nc.vector.scalar_tensor_tensor

            def split(b, hf, kind=None):
                r = hf // 2
                c0, place = 2 * (hf % 2), 2 * (hf % 4)
                dve.wait_ge(hi_ready, 8 * b + hf + 1)
                if kind in ("dkv", "rq"):
                    for c in range(2):
                        k = 4 * r + c0 + c
                        parts = [(0, NB, G_KVIN)] if kind == "dkv" else [(0, ROPE, G_KVIN), (ROPE, ROPE + Q_LORA, G_B)]
                        for n0, n1, g in parts:
                            done = stt(out=wlo[:, place + c, n0:n1], in0=raw[:, r, c0 + c, n0:n1],
                                       scalar=gains[:, g + k:g + k + 1], in1=whi[:, place + c, n0:n1].bitcast(F32),
                                       op0=ALU.mult, op1=ALU.subtract)
                else:
                    n, ch = (Q_LORA, 2 - hf % 2) if kind == "mla" and r % 2 else (NB, 2)
                    done = tt_(wlo[:, place:place + ch, 0:n], raw[:, r, c0:c0 + ch, 0:n],
                               whi[:, place:place + ch, 0:n].bitcast(F32), ALU.subtract)
                done.then_inc(lo_ready, 1)

            def body(b, asides=None, kind=None, nxt=None):
                for hf in range(3, 11):
                    if hf < 8:
                        split(b, hf, kind)
                    else:
                        split(b + 1, hf - 8, nxt)
                    if asides and hf in asides:
                        asides[hf]()

            def used(b):
                dve.wait_ge(pe_halves, 8 * b + 8)

            def x_lo(v, gain):
                j = v % JB
                for k in range(2):
                    dve.wait_ge(xT_hi, 4 * v + 2 * k + 2)
                    for cc in range(2):
                        c = JB * j + 2 * k + cc
                        src, hi = side[2 * (v % 2) + k][:, SEQ * cc:SEQ * cc + SEQ], opA[:, c, 0, :].bitcast(F32)
                        if gain is None:
                            tt_(opA[:, c, 1, :], src, hi, ALU.subtract).then_inc(xT_lo, 1)
                        else:
                            stt(out=opA[:, c, 1, :], in0=src, scalar=gains[:, gain + c:gain + c + 1], in1=hi,
                                op0=ALU.mult, op1=ALU.subtract).then_inc(xT_lo, 1)

            def stream_stats(t, squared):
                dve.wait_ge(xsq, 2 * JB * (t + 1))
                nc.vector.tensor_reduce(xms[:, t, :], xss[:, t, :, :], AX.X, ALU.add).then_inc(xstat, 1)
                dve.wait_ge(xstat, 2 * t + 1)
                ts_(xms2[:, t, :], xms[:, t, :], 1.0 / D, EPS, ALU.mult, ALU.add).then_inc(xstat, 1)
                if squared:
                    dve.wait_ge(xstat, 2 * t + 2)
                    nc.vector.reciprocal(rs[:, t, :], xms2[:, t, :]).then_inc(rs_ready, 1)

            dve.wait_ge(small_in, 48)
            tt_(lam_rows[:, 0:4:2, :], lam_rows[:, 0:4:2, :], lam_rows[:, 1:4:2, :], ALU.mult).then_inc(lam_step, 1)
            dve.wait_ge(lam_step, 1)
            nc.vector.tensor_reduce(lam_s[:, 0:2], lam_rows[:, 0:4:2, :], AX.X, ALU.add).then_inc(lam_step, 1)
            dve.wait_ge(gains_t, 1)
            nc.vector.tensor_copy(gains[:, 0:G_SUB], side[3][:, 0:G_SUB]).then_inc(gains_ready, 1)
            ts_(gains[:, G_SUB:G_END], side[3][:, G_SUB:G_END], 1.0 - LAM_INIT, None, ALU.mult).then_inc(gains_ready, 1)

            n_trig = [0]

            def step(ins):
                n_trig[0] += 1
                ins.then_inc(trig_step, 1)
                dve.wait_ge(trig_step, n_trig[0])

            step(nc.vector.tensor_copy(pos_f[:], pos_i[:]))
            for k in range(2):
                for t in range(TT):
                    last_angle = ts_(trig[:, k, t, :], invf[:], pos_f[:, t:t + 1], None, ALU.mult)
            step(last_angle)
            magic = 1.5 * 2.0 ** 23
            ts_(turns[:, 0], trig[:, 0], 1.0 / TWO_PI, None, ALU.mult)
            step(ts_(turns[:, 1], trig[:, 1], 1.0 / TWO_PI, 0.25, ALU.mult, ALU.add))
            step(ts_(turns, turns, magic, None, ALU.add))
            step(ts_(turns, turns, magic, None, ALU.subtract))
            step(nc.vector.tensor_copy(turns_hi[:], turns))
            step(tt_(turns_lo, turns, turns_hi[:].bitcast(F32), ALU.subtract))
            for part in twelve_bit_parts(TWO_PI, 3):
                for turn in (turns_hi[:].bitcast(F32), turns_lo):
                    step(stt(out=trig, in0=turn, scalar=-part, in1=trig, op0=ALU.mult, op1=ALU.add))
            step(ts_(trig[:, 1], trig[:, 1], float(np.pi / 2), None, ALU.add))
            step(ts_(trig, trig, 3.1415925, -3.1415925, ALU.min, ALU.max))
            dve.wait_ge(lam_step, 3)
            tt_(lam_s[:, 4:5], lam_s[:, 3:4], lam_s[:, 2:3], ALU.subtract).then_inc(lam_step, 1)
            dve.wait_ge(lam_step, 4)
            ts_(lam_s[:, 5:6], lam_s[:, 4:5], LAM_INIT, None, ALU.subtract).then_inc(lam_step, 1)
            neg_lam = lam_s[:, 5:6]

            for v in range(JB):
                x_lo(V_INIT + v, G_A)
            for hf in range(3):
                split(0, hf)
            stream_stats(0, False)
            dve.wait_ge(tables_ready, 4)

            def rotate(view, cos, sin, heads, width, i):
                h = width // 2

                def b(tab, c0, c1):
                    return tab[:, :, c0:c1].unsqueeze(2).to_broadcast([P, TT, heads, c1 - c0])

                a = rope_a[:].rearrange("p t h w -> p t (h w)")[:, :, 0:heads * width].rearrange(
                    "p t (h w) -> p t h w", h=heads)
                c = rope_b[:].rearrange("p t h w -> p t (h w)")[:, :, 0:heads * width].rearrange(
                    "p t (h w) -> p t h w", h=heads)
                tt_(a, view, b(cos, 0, width), ALU.mult).then_inc(rope_parts, 1)
                tt_(c[:, :, :, 0:h], view[:, :, :, h:width], b(sin, 0, h), ALU.mult).then_inc(rope_parts, 1)
                tt_(c[:, :, :, h:width], view[:, :, :, 0:h], b(sin, h, width), ALU.mult).then_inc(rope_parts, 1)
                dve.wait_ge(rope_parts, 3 * i + 3)
                tt_(view, a, c, ALU.add).then_inc(roped, 1)

            def rope_qk(p, k):
                dve.wait_ge(drained[k], (4 if k == 0 else 2) * p + 2)
                if not (isinstance(p, int) and p == 0 and k == 0):
                    dve.wait_ge(roped, 2 * p + k)
                rotate(stage[:].rearrange("p t (h w) -> p t h w", w=DA_DIM)[:, :, :, 0:DA_ROT], cosA, sinA, 4,
                       DA_ROT, 2 * p + k)

            def softmax_bias(maps_before, m, bank, scale):
                dve.wait_ge(scores_done, maps_before + m + 1)
                tt_(prob[:, m, :], bank[:, 0:KEYS], mask[:], ALU.add).then_inc(masked, 1)
                dve.wait_ge(masked, maps_before + m + 1)
                nc.vector.tensor_reduce(nmax[:, m, 0:1], prob[:, m, 0:P], AX.X, ALU.max)
                nc.vector.tensor_reduce(nmax[:, m, 1:2], prob[:, m, P:KEYS], AX.X, ALU.max).then_inc(maxed, 1)
                dve.wait_ge(maxed, maps_before + m + 1)
                ts_(bias[:, m, :], nmax[:, m, :], -scale, None, ALU.mult).then_inc(bias_ready, 1)

            def da_softmax(p, maps):
                for m in maps:
                    softmax_bias(4 * p, m, side[m], DA_SCALE)

            def da_weights(p):
                dve.wait_ge(exp_done, 4 * p + 4)
                nc.vector.reciprocal(rinv[:], rowsum[:]).then_inc(rinv_ready, 1)
                dve.wait_ge(rinv_ready, p + 1)
                ts_(rneg[:], rinv[:], neg_lam, None, ALU.mult).then_inc(rneg_ready, 1)
                tiles = [(h, t, c0, c1) for h in range(2) for t, (c0, c1) in enumerate(((0, P), (P, KEYS)))]
                for h, t, c0, c1 in tiles:
                    ts_(prob[:, 2 * h, c0:c1], prob[:, 2 * h, c0:c1], rinv[:, 2 * h, t:t + 1], None,
                        ALU.mult).then_inc(half_attn, 1)
                dve.wait_ge(rneg_ready, p + 1)
                for k, (h, t, c0, c1) in enumerate(tiles):
                    dve.wait_ge(half_attn, 4 * p + k + 1)
                    stt(out=attn[:, h, c0:c1], in0=prob[:, 2 * h + 1, c0:c1], scalar=rneg[:, 2 * h + 1, t:t + 1],
                        in1=prob[:, 2 * h, c0:c1], op0=ALU.mult, op1=ALU.add).then_inc(attn_ready, 1)

            def o_means(p):
                dve.wait_ge(oss_ready, p + 1)
                ts_(oms[:], oss[:], 1.0 / (2 * DA_DIM), SUB_EPS, ALU.mult, ALU.add).then_inc(oms_ready, 1)

            def o_scale(p):
                dve.wait_ge(ors_ready, p + 1)
                for h in range(2):
                    for t in range(TT):
                        done = ts_(o_sb[:, h, t, :], side[h][:, SEQ * t:SEQ * t + SEQ],
                                   ors[:, 2 * h + t:2 * h + t + 1], None, ALU.mult)
                done.then_inc(o_ready, 1)

            def o_lo(p):
                for h in range(2):
                    dve.wait_ge(opB_hi, 4 * p + 2 * h + 2)
                    for e in range(2):
                        stt(out=opB[:, bass.ds(4 * p + 2 * h + e, 1), 1, :],
                            in0=side[h][:, SEQ * e:SEQ * e + SEQ].unsqueeze(1),
                            scalar=gains[:, G_SUB + e:G_SUB + e + 1],
                            in1=opB[:, bass.ds(4 * p + 2 * h + e, 1), 0, :].bitcast(F32), op0=ALU.mult,
                            op1=ALU.subtract).then_inc(opB_lo, 1)

            def qkv(p, first):
                b = B_QKV + 3 * p
                pv = None if first else p - 1
                body(b, {} if first else {4: lambda: da_softmax(pv, (0, 1)), 5: lambda: da_softmax(pv, (2, 3)),
                                          7: lambda: da_weights(pv)})
                rope_qk(p, 0)
                body(b + 1, {} if first else {7: lambda: o_means(pv), 8: lambda: o_scale(pv)})
                rope_qk(p, 1)
                body(b + 2, {} if first else {4: lambda: o_lo(pv)})

            qkv(0, True)
            with dve.Fori(1, DA_PAIRS) as p:
                qkv(p, False)
            last = DA_PAIRS - 1

            def rest():
                da_weights(last)
                o_means(last)
                o_scale(last)
                o_lo(last)

            body(B_WO, {4: lambda: da_softmax(last, (0, 1)), 5: lambda: da_softmax(last, (2, 3)), 7: rest})

            def add_product(b, s, uses, cols):
                used(b)
                for t in range(TT):
                    tt_(xs[:, t, cols], acc[s][:, t, :], xs[:, t, cols], ALU.add).then_inc(drained[s], 1)

            def out_proj(b0, uses, v0, gain):
                add_product(b0, 1, uses[1], slice(0, NB))
                for j in range(1, JB):
                    s = (j + 1) % 2
                    body(b0 + j, {4: lambda: x_lo(v0 + j - 1, gain)})
                    add_product(b0 + j, s, uses[s] + j // 2, slice(NB * j, NB * j + NB))
                x_lo(v0 + JB - 1, gain)

            out_proj(B_WO, U_WO, V_WO, G_MLP[0])
            stream_stats(1, True)

            def mlp(l, v_out, nxt):
                u = U_MLP[l]

                def square_up(s, t):
                    for k in range(2):
                        dve.wait_ge(relu_done, 2 * t + k + 1)
                        stt(out=sq_sb[:, NB * k:NB * k + NB], in0=acc[s][:, k, :], scalar=0.0,
                            in1=relu_sb[:, NB * k:NB * k + NB], op0=ALU.max, op1=ALU.mult).then_inc(drained[s], 1)

                def hid_lo_part(t, j):
                    for k in range(2):
                        dve.wait_ge(hid_hi, 2 * t + k + 1)
                        tt_(opB[:, bass.ds(4 * j + 2 * k, 2), 1, :],
                            sq_sb[:, NB * k:NB * k + NB].rearrange("p (c t) -> p c t", c=2),
                            opB[:, bass.ds(4 * j + 2 * k, 2), 0, :].bitcast(F32), ALU.subtract).then_inc(hid_lo, 1)

                def up(q):
                    with dve.Fori(0, JB // 2) as i:
                        for k in range(2):
                            body(B_MLP[l] + 2 * JB * q + 2 * i + k)
                            t = JB * (QUARTERS * l + q) + 2 * i + k
                            square_up(1 - k, t)
                            hid_lo_part(t, 2 * i + k)

                def add_scaled(b, s, prior, cols):
                    used(b)
                    dve.wait_ge(drained[s], prior)
                    dve.wait_ge(rs_ready, 2 * l + 2)
                    for t in range(TT):
                        stt(out=xs[:, t, cols], in0=acc[s][:, t, :], scalar=rs[:, 2 * l + 1, t:t + 1],
                            in1=xs[:, t, cols], op0=ALU.mult, op1=ALU.add).then_inc(drained[s], 1)

                with dve.Fori(0, QUARTERS - 1) as q:
                    up(q)
                    with dve.Fori(0, JB // 2) as i:
                        for k in range(2):
                            b, s = B_MLP[l] + 2 * JB * q + JB + 2 * i + k, 1 - k
                            body(b)
                            add_scaled(b, s, 2 * (u[s] + JB * q + 2 + i), bass.ds(NB * (2 * i + k), NB))
                q = QUARTERS - 1
                up(q)
                for j in range(JB):
                    b, s = B_MLP[l] + 2 * JB * q + JB + j, (j + 1) % 2
                    asides = {}
                    if v_out is not None and j:
                        asides[4] = lambda: x_lo(v_out + j - 1, None)
                    if l == 1 and j == JB - 1:
                        for hf in range(3, 8):
                            split(b, hf)
                    else:
                        body(b, asides, nxt=nxt if j == JB - 1 else None)
                    add_scaled(b, s, 2 * (u[s] + JB * q + 2 + j // 2), slice(NB * j, NB * j + NB))
                    if l == 1:
                        dve.wait_ge(g_out_in, 16)
                        dve.wait_ge(xsq, 2 * (V_MLP1 + j) + 2)
                        for t in range(TT):
                            tt_(xs[:, t, NB * j:NB * j + NB], xs[:, t, NB * j:NB * j + NB],
                                g_out[:, NB * j:NB * j + NB], ALU.mult).then_inc(xg_ready, 1)
                if v_out is not None:
                    x_lo(v_out + JB - 1, None)

            mlp(0, V_MLP0, "dkv")
            stream_stats(2, False)

            def latent_stats(k, width):
                dve.wait_ge(lat_ss, 2 * k + 2)
                ts_(lms[:, k, :], lss[:, k, :], 1.0 / width, EPS, ALU.mult, ALU.add).then_inc(lat_ms, 1)

            def latent_lo(buf, c0, n, bank, before, gain):
                for c in range(n):
                    dve.wait_ge(latT_hi, before + min(n, 2 * (c // 2) + 2))
                    b, col = bank(c)
                    stt(out=buf[:, c0 + c, 1, :], in0=b[:, col:col + SEQ], scalar=gains[:, gain + c:gain + c + 1],
                        in1=buf[:, c0 + c, 0, :].bitcast(F32), op0=ALU.mult, op1=ALU.subtract).then_inc(latT_lo, 1)

            body(B_DKV, kind="dkv", nxt="rq")
            latent_stats(0, KV_LORA)
            body(B_RQ, {5: lambda: latent_lo(opB, 12, 4, lambda c: (side[c // 2], SEQ * (c % 2)), 0, G_KV)},
                 kind="rq", nxt="mla")
            dve.wait_ge(drained[0], 2 * (U_DKV[0] + 1))
            dve.wait_ge(roped, 2 * DA_PAIRS)
            rotate(kv_sb[:, 1, :, 0:ROPE].unsqueeze(2), cosB, sinB, 1, ROPE, 2 * DA_PAIRS)
            latent_stats(1, Q_LORA)
            latent_lo(opA, 0, 3, lambda c: (side[3], SEQ * c) if c < 2 else (side[2], SEQ), 4, G_Q)

            def rope_mla(p):
                dve.wait_ge(drained[0], 2 * (U_MLA[0] + p) + 2)
                dve.wait_ge(roped, 2 * DA_PAIRS + 1 + p)
                rotate(stage[:, :, 0:Q_LORA].rearrange("p t (h w) -> p t h w", h=2)[:, :, :, NOPE:NOPE + ROPE], cosB,
                       sinB, 2, ROPE, 2 * DA_PAIRS + 1 + p)

            def mla_softmax(p):
                for m in range(2):
                    softmax_bias(4 * DA_PAIRS + 2 * p, m, side[3 * (1 - m)], MLA_SCALE)

            def mla_weights(p):
                dve.wait_ge(exp_done, 4 * DA_PAIRS + 2 * p + 2)
                nc.vector.reciprocal(rinv[:, 0:2, :], rowsum[:, 0:2, :]).then_inc(rinv_ready, 1)
                dve.wait_ge(rinv_ready, DA_PAIRS + p + 1)
                for h in range(2):
                    for t, (c0, c1) in enumerate(((0, P), (P, KEYS))):
                        ts_(attn[:, h, c0:c1], prob[:, h, c0:c1], rinv[:, h, t:t + 1], None,
                            ALU.mult).then_inc(attn_ready, 1)

            def mla_lo(p):
                dve.wait_ge(opB_hi, 4 * DA_PAIRS + p + 1)
                tt_(opB[:, bass.ds(2 * p, 2), 1, :], side[1][:].rearrange("p (h t) -> p h t", h=2),
                    opB[:, bass.ds(2 * p, 2), 0, :].bitcast(F32), ALU.subtract).then_inc(opB_lo, 1)

            def mla_pair(g, u, p, with_prev, nxt="mla"):
                b = B_MLA + g
                nb, h0 = (b, 4) if u == 0 else (b + 1, 0)
                split(b, 4 * u + 3, "mla")
                split(nb, h0, nxt)
                if with_prev:
                    mla_softmax(p - 1)
                split(nb, h0 + 1, nxt)
                if with_prev:
                    mla_weights(p - 1)
                split(nb, h0 + 2, nxt)
                rope_mla(p)
                if with_prev:
                    mla_lo(p - 1)

            mla_pair(0, 0, 0, False)
            with dve.Fori(0, MLA_PAIRS // 2 - 1) as g:
                mla_pair(g, 1, 2 * g + 1, True)
                mla_pair(g + 1, 0, 2 * g + 2, True)
            mla_pair(MLA_PAIRS // 2 - 1, 1, MLA_PAIRS - 1, True, nxt=None)
            last_pair = MLA_PAIRS - 1

            def mla_rest():
                mla_weights(last_pair)
                mla_lo(last_pair)

            body(B_BWO, {4: lambda: mla_softmax(last_pair), 7: mla_rest})
            out_proj(B_BWO, U_BWO, V_BWO, G_MLP[1])
            stream_stats(3, True)
            mlp(1, None, None)
            stream_stats(4, False)
            dve.wait_ge(rs_ready, 5)
            for j in range(JB):
                dve.wait_ge(xg_ready, 2 * j + 2)
                ts_(xs[:, 1, NB * j:NB * j + NB], xs[:, 1, NB * j:NB * j + NB], rs[:, 4, 1:2], None,
                    ALU.mult).then_inc(out_ready[1], 1)


_INS = ["x", "positions", "a_norm_g", "a_w_qkv", "a_lambda", "a_subln_g", "a_w_o", "kv_in_norm_g", "w_dkv",
        "kv_norm_g", "w_ukv", "b_norm_g", "b_w_dq", "b_q_norm_g", "b_w_uq", "b_w_o", "mlp_norm_g", "w_up", "w_down",
        "final_norm_g"]


def kernel(**inputs):
    import concourse.bacc as _bacc
    from concourse.bass_utils import run_bass_kernel_spmd as _run

    nc = _bacc.Bacc("TRN2", target_bir_lowering=False, num_devices=1)
    arrays, args = {}, []
    for name in _INS:
        a = np.ascontiguousarray(inputs[name])
        arrays[f"in_{name}"] = a
        args.append(nc.dram_tensor(f"in_{name}", a.shape, mybir.dt.from_np(a.dtype), kind="ExternalInput").ap())
    arrays["in_freqs"] = rope_frequencies()
    args.append(nc.dram_tensor("in_freqs", (P, 48), F32, kind="ExternalInput").ap())
    args.append(nc.dram_tensor("out_0", (1, SEQ, D), F32, kind="ExternalOutput").ap())
    trunk(nc, *args)
    r = _run(nc, [arrays], core_ids=[0])
    return r.results[0]["out_0"]
```

```python
from contextlib import ExitStack

import concourse.bass as bass
import numpy as np
from concourse import mybir

F32 = mybir.dt.float32
F32R = mybir.dt.float32r
I32 = mybir.dt.int32
ALU = mybir.AluOpType
ACT = mybir.ActivationFunctionType
AX = mybir.AxisListType

P = 128
SEQ, D = 256, 2048
TT = SEQ // P
KC = D // P
NB = 512
DFF = 4 * D
DA_HEADS, DA_DIM, DA_ROT = 8, 128, 32
MLA_HEADS, Q_LORA, KV_LORA, NOPE, ROPE, VDIM = 16, 384, 512, 128, 64, 128
THETA = 500000.0
EPS, SUB_EPS = 1e-6, 1e-5
LAM_INIT = 0.2
DA_SCALE = float(DA_DIM) ** -0.5
MLA_SCALE = float(NOPE + ROPE) ** -0.5
MASKED = -3.0e38
KEYS = P + 2 * P

DA_PAIRS = DA_HEADS // 2
QUARTERS = DFF // D
JB = D // NB
MLA_PAIRS = MLA_HEADS // 2

B_QKV = 0
B_WO = B_QKV + 3 * DA_PAIRS
B_MLP = [B_WO + JB, 0]
B_DKV = B_MLP[0] + 2 * JB * QUARTERS
B_RQ = B_DKV + 1
B_MLA = B_RQ + 1
B_BWO = B_MLA + MLA_PAIRS // 2
B_MLP[1] = B_BWO + JB
B_END = B_MLP[1] + 2 * JB * QUARTERS

U_WO = (2 * DA_PAIRS, DA_PAIRS)
U_MLP = [(U_WO[0] + 2, U_WO[1] + 2), None]
U_DKV = (U_MLP[0][0] + 16, U_MLP[0][1] + 16)
U_MLA = (U_DKV[0] + 1, U_DKV[1] + 1)
U_BWO = (U_MLA[0] + MLA_PAIRS, U_MLA[1] + MLA_PAIRS)
U_MLP[1] = (U_BWO[0] + 2, U_BWO[1] + 2)

G_A, G_MLP, G_KVIN, G_B, G_KV, G_Q, G_SUB, G_END = 0, (16, 32), 48, 64, 80, 84, 87, 89

V_INIT, V_WO, V_MLP0, V_BWO, V_MLP1 = 0, 4, 8, 12, 16

TWO_PI = 2 * np.pi


def twelve_bit_parts(value, n):
    parts = []
    for _ in range(n):
        e = np.floor(np.log2(abs(value))) - 11
        part = np.trunc(value / 2.0 ** e) * 2.0 ** e
        parts.append(float(part))
        value -= part
    return parts


def rope_frequencies():
    a = np.float32(THETA) ** (-np.arange(0, DA_ROT, 2, dtype=np.float32) / np.float32(DA_ROT))
    b = np.float32(THETA) ** (-np.arange(0, ROPE, 2, dtype=np.float32) / np.float32(ROPE))
    return np.tile(np.concatenate([a, b]).astype(np.float32)[None], (P, 1))


def trunk(nc, x, positions, a_norm_g, a_w_qkv, a_lambda, a_subln_g, a_w_o, kv_in_norm_g, w_dkv, kv_norm_g,
          w_ukv, b_norm_g, b_w_dq, b_q_norm_g, b_w_uq, b_w_o, mlp_norm_g, w_up, w_down, final_norm_g, freqs,
          out):
    def chunked(w):
        return w.rearrange("(c p) n -> p c n", p=P)

    W_QKV, W_O, W_BO = chunked(a_w_qkv[0]), chunked(a_w_o[0]), chunked(b_w_o[0])
    W_UP = [chunked(w_up[l]) for l in range(2)]
    W_DOWN = [chunked(w_down[l]) for l in range(2)]
    W_DKV, W_DQ, W_UKV, W_UQ = chunked(w_dkv), chunked(b_w_dq[0]), chunked(w_ukv), chunked(b_w_uq[0])
    x_tok = x[0].rearrange("(t p) n -> p t n", p=P)
    out_tok = out[0].rearrange("(t p) n -> p t n", p=P)

    with ExitStack() as ctx:
        def sb(name, shape, dt=F32):
            return ctx.enter_context(nc.sbuf_tensor(name, shape, dt))

        def psum(name, shape):
            return ctx.enter_context(nc.psum_tensor(name, shape, F32))

        def sem(name):
            return ctx.enter_context(nc.semaphore(name))

        xs = sb("xs", [P, TT, D])
        opA = sb("opA", [P, KC, 2, SEQ], F32R)
        opB = sb("opB", [P, KC, 2, SEQ], F32R)
        raw = sb("raw", [P, 4, 4, NB])
        whi = sb("whi", [P, 8, NB], F32R)
        wlo = sb("wlo", [P, 8, NB], F32R)
        stage = sb("stage", [P, TT, NB])
        kv_sb = sb("kv_sb", [P, 2, TT, NB])
        qkT = sb("qkT", [P, 2, 4 * SEQ])
        krT = sb("krT", [ROPE, SEQ])
        rope_a = sb("rope_a", [P, TT, 4, DA_ROT])
        rope_b = sb("rope_b", [P, TT, 4, DA_ROT])
        prob = sb("prob", [P, 4, KEYS])
        attn = sb("attn", [P, 2, KEYS])
        attnT = sb("attnT", [P, 2, KEYS])
        o_sb = sb("o_sb", [P, 2, TT, 2 * DA_DIM])
        relu_sb = sb("relu_sb", [P, 2 * NB])
        sq_sb = sb("sq_sb", [P, 2 * NB])
        junk = sb("junk", [P, 2, NB])
        mask = sb("mask", [P, KEYS])
        ident = sb("ident", [P, P])
        gains = sb("gains", [P, G_END])
        invf = sb("invf", [P, 48])
        pos_i = sb("pos_i", [P, TT], I32)
        pos_f = sb("pos_f", [P, TT])
        cosA, sinA = sb("cosA", [P, TT, DA_ROT]), sb("sinA", [P, TT, DA_ROT])
        cosB, sinB = sb("cosB", [P, TT, ROPE]), sb("sinB", [P, TT, ROPE])
        lam_s = sb("lam_s", [P, 8])
        neg_half = sb("neg_half", [P, 4])
        xss = sb("xss", [P, 5, TT, JB])
        xms = sb("xms", [P, 5, TT])
        xms2 = sb("xms2", [P, 5, TT])
        rs = sb("rs", [P, 5, TT])
        lss = sb("lss", [P, 2, TT])
        lms = sb("lms", [P, 2, TT])
        lrs = sb("lrs", [P, 2, TT])
        nmax = sb("nmax", [P, 4, TT])
        bias = sb("bias", [P, 4, TT])
        rowsum = sb("rowsum", [P, 4, TT])
        rinv = sb("rinv", [P, 4, TT])
        rneg = sb("rneg", [P, 4, TT])
        oss = sb("oss", [P, 4])
        oms = sb("oms", [P, 4])
        ors = sb("ors", [P, 4])
        qT = qkT[:, 0, :].rearrange("p (h t) -> p h t", h=4)
        kT = qkT[:, 1, :].rearrange("p (h t) -> p h t", h=4)
        g_out = qkT[:].rearrange("p a n -> p (a n)")
        y_sb = [kv_sb[:, 0], kv_sb[:, 1], stage[:], o_sb[:].rearrange("p h t (a n) -> p (h t a) n", a=1).rearrange(
            "p (t k) n -> p t (k n)", t=TT)]
        gain_rows_a = relu_sb[0:KC, P:2 * P]
        gain_rows = relu_sb[0:G_END, 0:P]
        lam_rows = sq_sb[:, 0:4 * P].rearrange("p (a n) -> p a n", a=4)
        trig = prob[:, 0, :].rearrange("p (s w) -> p s w", s=2)[:, :, 0:TT * 48].rearrange(
            "p s (t f) -> p s t f", t=TT)
        turns = prob[:, 1, :].rearrange("p (s w) -> p s w", s=2)[:, :, 0:TT * 48].rearrange(
            "p s (t f) -> p s t f", t=TT)
        turns_lo = prob[:, 2, :].rearrange("p (s w) -> p s w", s=2)[:, :, 0:TT * 48].rearrange(
            "p s (t f) -> p s t f", t=TT)
        turns_hi = sb("turns_hi", [P, 2, TT, 48], F32R)

        acc = [psum(f"acc{s}", [P, 2, NB]) for s in range(2)]
        side = [psum(f"side{i}", [P, NB]) for i in range(4)]

        raw_ready = [sem(f"raw_ready{r}") for r in range(4)]
        dq_ready = [sem(f"dq_ready{r}") for r in range(4)]
        x_in = [sem(f"x_in{j}") for j in range(JB)]
        small_in = sem("small_in")
        gain_a_in = sem("gain_a_in")
        gains_in = sem("gains_in")
        g_out_in = sem("g_out_in")
        out_done = sem("out_done")
        const_ready = sem("const_ready")
        gains_t = sem("gains_t")
        gains_ready = sem("gains_ready")
        trig_step = sem("trig_step")
        tables_ready = sem("tables_ready")
        lam_step = sem("lam_step")
        hi_ready = sem("hi_ready")
        lo_ready = sem("lo_ready")
        pe_halves = sem("pe_halves")
        drained = [sem(f"drained{s}") for s in range(2)]
        xT_done = sem("xT_done")
        xT_hi = sem("xT_hi")
        xT_lo = sem("xT_lo")
        xsq = sem("xsq")
        xstat = sem("xstat")
        rs_ready = sem("rs_ready")
        rope_parts = sem("rope_parts")
        roped = sem("roped")
        qkT_done = sem("qkT_done")
        qkT_ready = sem("qkT_ready")
        scores_done = sem("scores_done")
        masked = sem("masked")
        maxed = sem("maxed")
        bias_ready = sem("bias_ready")
        exp_done = sem("exp_done")
        rinv_ready = sem("rinv_ready")
        rneg_ready = sem("rneg_ready")
        half_attn = sem("half_attn")
        attn_ready = sem("attn_ready")
        attnT_done = sem("attnT_done")
        attnT_ready = sem("attnT_ready")
        pv_done = sem("pv_done")
        oss_ready = sem("oss_ready")
        oms_ready = sem("oms_ready")
        ors_ready = sem("ors_ready")
        o_ready = sem("o_ready")
        oT_done = sem("oT_done")
        opB_hi = sem("opB_hi")
        opB_lo = sem("opB_lo")
        relu_done = sem("relu_done")
        hid_hi = sem("hid_hi")
        hid_lo = sem("hid_lo")
        lat_ss = sem("lat_ss")
        lat_ms = sem("lat_ms")
        lat_rs = sem("lat_rs")
        latT_done = sem("latT_done")
        latT_hi = sem("latT_hi")
        latT_lo = sem("latT_lo")
        krT_ready = sem("krT_ready")
        xg_ready = sem("xg_ready")
        out_ready = [sem("out_ready0"), sem("out_ready1")]

        block = ctx.enter_context(nc.Block())

        @block.sync
        def _(sp):
            def quad(b, r, src, first=False):
                if not first:
                    sp.wait_ge(lo_ready, 8 * b + 2 * r - 6)
                sp.dma_start(raw[:, r, 0:src.shape[1], 0:src.shape[2]], src).then_inc(raw_ready[r], 16)

            def whole(b, w, col, row=0):
                for r in range(4):
                    quad(b, r, w[:, bass.ds(row + 4 * r, 4), bass.ds(col, NB)])

            def qkv(p, first):
                if first:
                    sp.dma_start(gain_rows_a, a_norm_g[0].rearrange("(c p) -> c p", p=P)).then_inc(gain_a_in, 16)
                    for j in range(JB):
                        sp.dma_start(xs[:, :, NB * j:NB * j + NB], x_tok[:, :, NB * j:NB * j + NB]).then_inc(x_in[j], 16)
                        quad(B_QKV, j, W_QKV[:, 4 * j:4 * j + 4, 0:NB], True)
                else:
                    whole(B_QKV + 3 * p, W_QKV, NB * p)
                whole(B_QKV + 3 * p + 1, W_QKV, NB * p + D)
                whole(B_QKV + 3 * p + 2, W_QKV, NB * p + 2 * D)

            qkv(0, True)
            with sp.Fori(1, DA_PAIRS) as p:
                qkv(p, False)
            with sp.Fori(0, JB) as j:
                whole(B_WO + j, W_O, NB * j)

            def mlp(l):
                with sp.Fori(0, QUARTERS) as q:
                    with sp.Fori(0, JB) as j:
                        whole(B_MLP[l] + 2 * JB * q + j, W_UP[l], D * q + NB * j)
                    with sp.Fori(0, JB) as j:
                        whole(B_MLP[l] + 2 * JB * q + JB + j, W_DOWN[l], NB * j, row=KC * q)

            mlp(0)
            whole(B_DKV, W_DKV, 0)
            for r in range(4):
                quad(B_RQ, r, W_DKV[:, 4 * r:4 * r + 4, KV_LORA:KV_LORA + ROPE])
                sp.dma_start(raw[:, r, :, ROPE:ROPE + Q_LORA], W_DQ[:, 4 * r:4 * r + 4, :]).then_inc(dq_ready[r], 16)
            with sp.Fori(0, MLA_PAIRS // 2) as g:
                for u in range(2):
                    quad(B_MLA + g, 2 * u, W_UKV[:, :, bass.ds(2 * NB * g + NB * u, NB)])
                    quad(B_MLA + g, 2 * u + 1, W_UQ[:, :, bass.ds(2 * Q_LORA * g + Q_LORA * u, Q_LORA)])
            with sp.Fori(0, JB) as j:
                whole(B_BWO + j, W_BO, NB * j)
            mlp(1)
            for j in range(JB):
                for t in range(TT):
                    sp.wait_ge(out_ready[t], j + 1)
                sp.dma_start(out_tok[:, :, NB * j:NB * j + NB], y_sb[j]).then_inc(out_done, 16)
            sp.wait_ge(out_done, 16 * JB)

        @block.gpsimd
        def _(pool):
            nc.gpsimd.memset(neg_half[:], -0.5).then_inc(const_ready, 1)
            nc.gpsimd.memset(ident[:], 0.0).then_inc(const_ready, 1)
            nc.gpsimd.memset(mask[:], 0.0).then_inc(const_ready, 1)
            pool.wait_ge(const_ready, 3)
            nc.gpsimd.affine_select(out=ident[:], in_=ident[:], compare_op=ALU.not_equal, fill=1.0, base=0,
                                    pattern=[[-1, P]], channel_multiplier=1).then_inc(const_ready, 1)
            for c in (0, 2 * P):
                nc.gpsimd.affine_select(out=mask[:, c:c + P], in_=mask[:, c:c + P], compare_op=ALU.is_ge,
                                        fill=MASKED, base=0, pattern=[[-1, P]],
                                        channel_multiplier=1).then_inc(const_ready, 1)

            def stream_scale(t):
                pool.wait_ge(xstat, 2 * t + 2)
                nc.gpsimd.tensor_tensor(rs[:, t, :], xms2[:, t, :], neg_half[:, 0:TT], ALU.pow).then_inc(rs_ready, 1)

            def sub_norm(p):
                pool.wait_ge(oms_ready, p + 1)
                nc.gpsimd.tensor_tensor(ors[:], oms[:], neg_half[:], ALU.pow).then_inc(ors_ready, 1)

            stream_scale(0)
            with pool.Fori(0, DA_PAIRS) as p:
                sub_norm(p)
            stream_scale(2)
            for k in range(2):
                pool.wait_ge(lat_ms, k + 1)
                nc.gpsimd.tensor_tensor(lrs[:, k, :], lms[:, k, :], neg_half[:, 0:TT], ALU.pow).then_inc(lat_rs, 1)
            stream_scale(4)

        @block.tensor
        def _(pe):
            mm, tr = nc.tensor.matmul, nc.tensor.transpose

            def wait_bank(s, uses, bank):
                if not (isinstance(uses, int) and uses == 0):
                    pe.wait_ge(drained[s], 2 * uses - 1 + bank)

            def half_tok(b, hf, s, op, n=NB, chunks=2, first=False, last=False, uses=0):
                pe.wait_ge(lo_ready, 8 * b + hf + 1)
                place = 2 * (hf % 4)
                for c in range(chunks):
                    for t in range(TT):
                        if first and c == 0:
                            wait_bank(s, uses, t)
                        a_hi, a_lo = (op[c][i][:, P * t:P * t + P] for i in range(2))
                        w_hi, w_lo = whi[:, place + c, 0:n], wlo[:, place + c, 0:n]
                        o = acc[s][:, t, 0:n]
                        mm(o, a_hi, w_hi, start=first and c == 0, stop=False)
                        mm(o, a_hi, w_lo, start=False, stop=False)
                        done = mm(o, a_lo, w_hi, start=False, stop=last and c == chunks - 1)
                done.then_inc(pe_halves, 1)

            def chunks_of(buf, c0, n=2):
                return [[buf[:, c0 + c, i, :] for i in range(2)] for c in range(n)]

            def block_tok(b, s, uses, buf, n=NB, ready=None, aside=None):
                for hf in range(8):
                    if ready:
                        ready(hf)
                    half_tok(b, hf, s, chunks_of(buf, 2 * hf), n, first=hf == 0, last=hf == 7, uses=uses)
                    if aside and hf in aside:
                        aside[hf]()

            def block_feat(b, s, uses, ready=None, aside=None):
                for hf in range(8):
                    if ready:
                        ready(hf)
                    pe.wait_ge(lo_ready, 8 * b + hf + 1)
                    place = 2 * (hf % 4)
                    for c in range(2):
                        x_hi, x_lo = (opA[:, 2 * hf + c, i, :] for i in range(2))
                        for f in range(4):
                            if hf == 0 and c == 0 and f % 2 == 0:
                                wait_bank(s, uses, f // 2)
                            w_hi = whi[:, place + c, P * f:P * f + P]
                            w_lo = wlo[:, place + c, P * f:P * f + P]
                            o = acc[s][:, f // 2, SEQ * (f % 2):SEQ * (f % 2) + SEQ]
                            first = hf == 0 and c == 0 and f % 2 == 0
                            end = hf == 7 and c == 1 and f % 2 == 1
                            mm(o, w_hi, x_hi, start=first, stop=False, skip_group_check=True)
                            mm(o, w_hi, x_lo, start=False, stop=False, skip_group_check=True)
                            done = mm(o, w_lo, x_hi, start=False, stop=end, skip_group_check=True)
                    done.then_inc(pe_halves, 1)
                    if aside and hf in aside:
                        aside[hf]()

            def transpose_x(v, s=None, uses=None):
                if s is not None:
                    pe.wait_ge(drained[s], 2 * uses)
                if v >= 2:
                    pe.wait_ge(xT_lo, 4 * (v - 1))
                j = v % JB
                for k in range(2):
                    bank = side[2 * (v % 2) + k]
                    for cc in range(2):
                        for t in range(TT):
                            col = NB * j + P * (2 * k + cc)
                            done = tr(bank[:, SEQ * cc + P * t:SEQ * cc + P * t + P], xs[:, t, col:col + P], ident[:])
                    done.then_inc(xT_done, 1)

            pe.wait_ge(const_ready, 4)
            pe.wait_ge(gain_a_in, 16)
            tr(side[3][:, 0:KC], gain_rows_a, ident[0:KC, 0:KC]).then_inc(gains_t, 1)
            pe.wait_ge(gains_ready, 1)

            def transpose_gains():
                pe.wait_ge(gains_in, 16 * 7)
                pe.wait_ge(xT_lo, 4 * JB)
                tr(side[3][:, 0:G_END - KC], gain_rows[0:G_END - KC, :],
                   ident[0:G_END - KC, 0:G_END - KC]).then_inc(gains_t, 1)

            def transpose_x_in(v):
                pe.wait_ge(x_in[v], 16)
                transpose_x(V_INIT + v)

            transpose_x_in(0)

            def transpose_qk(i, b0):
                pe.wait_ge(roped, i + 1)
                for hh in range(4):
                    for t in range(TT):
                        done = tr(side[b0 + hh // 2][:, SEQ * (hh % 2) + P * t:SEQ * (hh % 2) + P * t + P],
                                  stage[:, t, P * hh:P * hh + P], ident[:])
                done.then_inc(qkT_done, 1)

            def da_scores(p):
                pe.wait_ge(qkT_ready, 4 * p + 4)
                for m in range(4):
                    mm(side[m][:, 0:P], qT[:, m, 0:P], kT[:, m, 0:P], start=True, stop=True)
                    mm(side[m][:, P:KEYS], qT[:, m, P:SEQ], kT[:, m, :], start=True,
                       stop=True).then_inc(scores_done, 1)

            def transpose_attn(heads_before, b0, masks):
                pe.wait_ge(masked, masks)
                for h in range(2):
                    pe.wait_ge(attn_ready, 2 * heads_before + 2 * h + 2)
                    for k in range(3):
                        done = tr(side[b0 + h][:, P * k:P * k + P], attn[:, h, P * k:P * k + P], ident[:])
                    done.then_inc(attnT_done, 1)

            def da_values(p, v_drained, banks_read=None):
                pe.wait_ge(drained[0], v_drained)
                if banks_read is not None:
                    pe.wait_ge(qkT_ready, banks_read)
                for h in range(2):
                    pe.wait_ge(attnT_ready, 2 * p + h + 1)
                    cols = slice(2 * DA_DIM * h, 2 * DA_DIM * (h + 1))
                    mm(side[h][:, 0:SEQ], attnT[:, h, 0:P], kv_sb[:, 0, 0, cols], start=True, stop=True)
                    mm(side[h][:, SEQ:NB], attnT[:, h, P:2 * P], kv_sb[:, 0, 0, cols], start=True, stop=False)
                    mm(side[h][:, SEQ:NB], attnT[:, h, 2 * P:KEYS], kv_sb[:, 0, 1, cols], start=False,
                       stop=True).then_inc(pv_done, 1)

            def transpose_o(p):
                pe.wait_ge(o_ready, p + 1)
                for h in range(2):
                    for e in range(2):
                        for t in range(TT):
                            done = tr(side[h][:, SEQ * e + P * t:SEQ * e + P * t + P], o_sb[:, h, t, P * e:P * e + P],
                                      ident[:])
                    done.then_inc(oT_done, 1)

            def opA_ready(first):
                return lambda hf: pe.wait_ge(xT_lo, 4 * (first + hf // 2) + 4)

            def qkv(p, first):
                b = B_QKV + 3 * p
                prev = None if first else p - 1
                if first:
                    block_tok(b, 0, 0, opA, ready=opA_ready(V_INIT), aside={
                        0: lambda: transpose_x_in(1), 2: lambda: transpose_x_in(2), 4: lambda: transpose_x_in(3)})
                else:
                    block_tok(b, 0, 2 * p, opA, aside={0: lambda: da_scores(prev)})
                block_tok(b + 1, 1, p, opA, aside={0: transpose_gains, 5: lambda: transpose_qk(2 * p, 0)} if first else {
                    1: lambda: transpose_attn(2 * prev, 2, 4 * prev + 4),
                    2: lambda: transpose_qk(2 * p, 0),
                    4: lambda: da_values(prev, 4 * prev + 4, 4 * prev + 6)})
                aside = {3: lambda: transpose_qk(2 * p + 1, 2)}
                if not first:
                    aside[1] = lambda: transpose_o(prev)
                block_tok(b + 2, 0, 2 * p + 1, opA, aside=aside)

            qkv(0, True)
            with pe.Fori(1, DA_PAIRS) as p:
                qkv(p, False)

            last = DA_PAIRS - 1
            block_tok(B_WO, 1, U_WO[1], opB, ready=lambda hf: pe.wait_ge(opB_lo, 2 * hf + 2), aside={
                0: lambda: da_scores(last),
                3: lambda: transpose_attn(2 * last, 2, 4 * last + 4),
                4: lambda: da_values(last, 4 * last + 4),
                5: lambda: transpose_o(last)})

            def out_proj(b0, uses, v0):
                for j in range(1, JB):
                    s, ps = (j + 1) % 2, j % 2
                    block_tok(b0 + j, s, uses[s] + j // 2, opB, aside={
                        1: lambda: transpose_x(v0 + j - 1, ps, uses[ps] + (j - 1) // 2 + 1)})

            out_proj(B_WO, U_WO, V_WO)

            def mlp(l, v_in, v_out):
                u = U_MLP[l]

                def up(q):
                    with pe.Fori(0, JB // 2) as i:
                        for k in range(2):
                            block_feat(B_MLP[l] + 2 * JB * q + 2 * i + k, 1 - k, u[1 - k] + JB * q + i)

                def hidden_ready(q):
                    return lambda hf: pe.wait_ge(hid_lo, 2 * JB * (QUARTERS * l + q) + hf + 1)

                for j in range(JB):
                    s = (j + 1) % 2
                    block_feat(B_MLP[l] + j, s, u[s] + j // 2, ready=None if j else opA_ready(v_in), aside={} if j else {
                        1: lambda: transpose_x(v_in + JB - 1, 0, u[0])})
                with pe.Fori(0, QUARTERS - 1) as q:
                    with pe.Fori(0, JB // 2) as i:
                        for k in range(2):
                            block_tok(B_MLP[l] + 2 * JB * q + JB + 2 * i + k, 1 - k, u[1 - k] + JB * q + 2 + i, opB,
                                      ready=hidden_ready(q))
                    up(q + 1)
                q = QUARTERS - 1
                for j in range(JB):
                    s, ps = (j + 1) % 2, j % 2
                    aside = {}
                    if v_out is not None and j:
                        aside[1] = lambda: transpose_x(v_out + j - 1, ps, u[ps] + JB * q + 2 + (j - 1) // 2 + 1)
                    block_tok(B_MLP[l] + 2 * JB * q + JB + j, s, u[s] + JB * q + 2 + j // 2, opB,
                              ready=hidden_ready(q), aside=aside)

            mlp(0, V_WO, V_MLP0)

            def transpose_ckv():
                pe.wait_ge(drained[1], 2 * (U_DKV[1] + 1))
                pe.wait_ge(xT_lo, 4 * (V_MLP0 + JB))
                for k in range(2):
                    for cc in range(2):
                        for t in range(TT):
                            col = P * (2 * k + cc)
                            done = tr(side[k][:, SEQ * cc + P * t:SEQ * cc + P * t + P], stage[:, t, col:col + P], ident[:])
                    done.then_inc(latT_done, 1)

            block_tok(B_DKV, 1, U_DKV[1], opA, ready=opA_ready(V_MLP0), aside={
                1: lambda: transpose_x(V_MLP0 + JB - 1, 0, U_DKV[0])})
            block_tok(B_RQ, 0, U_DKV[0], opA, n=ROPE + Q_LORA, aside={2: transpose_ckv})
            pe.wait_ge(drained[0], 2 * (U_DKV[0] + 1))
            for c in range(3):
                for t in range(TT):
                    bank, col = (side[3], SEQ * c) if c < 2 else (side[2], SEQ)
                    done = tr(bank[:, col + P * t:col + P * t + P], kv_sb[:, 1, t, ROPE + P * c:ROPE + P * c + P], ident[:])
            pe.wait_ge(roped, 2 * DA_PAIRS + 1)
            for t in range(TT):
                done = tr(side[2][0:ROPE, P * t:P * t + P], kv_sb[:, 1, t, 0:ROPE], ident[:])
            done.then_inc(latT_done, 1)

            ckvT = chunks_of(opB, 12, 4)
            cqT = chunks_of(opA, 0, 3)
            qh = qT[:, 0:2, :]
            qr = qT[0:ROPE, 2:4, :]
            kh = kT[:, 0:2, :]

            def mla_transposes(p, par):
                pe.wait_ge(drained[1], 2 * (U_MLA[1] + p) + 2)
                pe.wait_ge(opB_lo, DA_PAIRS * 4 + p - 1)
                pe.wait_ge(attnT_ready, DA_HEADS + 2 * p)
                for h in range(2):
                    for t in range(TT):
                        done = tr(side[0][:, SEQ * h + P * t:SEQ * h + P * t + P],
                                  kv_sb[:, par, t, 2 * P * h:2 * P * h + P], ident[:])
                done.then_inc(qkT_done, 1)
                pe.wait_ge(roped, 2 * DA_PAIRS + 2 + p)
                for h in range(2):
                    for t in range(TT):
                        done = tr(side[1][:, SEQ * h + P * t:SEQ * h + P * t + P],
                                  stage[:, t, 192 * h:192 * h + P], ident[:])
                done.then_inc(qkT_done, 1)
                for h in range(2):
                    for t in range(TT):
                        done = tr(side[2][0:ROPE, SEQ * h + P * t:SEQ * h + P * t + P],
                                  stage[:, t, 192 * h + P:192 * h + P + ROPE], ident[:])
                done.then_inc(qkT_done, 1)

            def mla_scores(p):
                pe.wait_ge(qkT_ready, 2 * DA_PAIRS * 2 + 3 * p + 3)
                for h in range(2):
                    bank = side[3 * (1 - h)]
                    for q0, q1, k1, o0, o1 in ((0, P, P, 0, P), (P, SEQ, SEQ, P, KEYS)):
                        mm(bank[:, o0:o1], qh[:, h, q0:q1], kh[:, h, 0:k1], start=True, stop=False)
                        done = mm(bank[:, o0:o1], qr[:, h, q0:q1], krT[:, 0:k1], start=False, stop=True)
                    done.then_inc(scores_done, 1)

            def mla_values(p, par):
                for h in range(2):
                    pe.wait_ge(attnT_ready, DA_HEADS + 2 * p + h + 1)
                    v = slice(2 * P * h + P, 2 * P * (h + 1))
                    mm(side[1][:, SEQ * h:SEQ * (h + 1)], kv_sb[:, par, 0, v], attnT[:, h, 0:SEQ], start=True,
                       stop=False, skip_group_check=True)
                    done = mm(side[1][:, SEQ * h + P:SEQ * (h + 1)], kv_sb[:, par, 1, v], attnT[:, h, SEQ:KEYS],
                              start=False, stop=True, skip_group_check=True)
                done.then_inc(pv_done, 1)

            def mla_weightsT(p):
                transpose_attn(DA_HEADS + 2 * p, 2, 4 * DA_PAIRS + 2 * p + 2)

            def mla_pair(g, u, p, prev=True, prev2=True):
                b = B_MLA + g
                half_tok(b, 4 * u, 1, ckvT[0:2], first=True, uses=U_MLA[1] + p)
                if prev:
                    mla_transposes(p - 1, 1 - u)
                half_tok(b, 4 * u + 1, 1, ckvT[2:4], last=True)
                if prev:
                    mla_scores(p - 1)
                if prev2:
                    mla_values(p - 2, u)
                half_tok(b, 4 * u + 2, 0, cqT[0:2], n=Q_LORA, first=True, uses=U_MLA[0] + p)
                half_tok(b, 4 * u + 3, 0, cqT[2:3], n=Q_LORA, chunks=1, last=True)
                if prev:
                    mla_weightsT(p - 1)

            pe.wait_ge(latT_lo, 7)
            pe.wait_ge(krT_ready, 1)
            mla_pair(0, 0, 0, prev=False, prev2=False)
            mla_pair(0, 1, 1, prev2=False)
            with pe.Fori(1, MLA_PAIRS // 2) as g:
                mla_pair(g, 0, 2 * g)
                mla_pair(g, 1, 2 * g + 1)

            last_pair = MLA_PAIRS - 1

            def heads_ready(hf):
                pe.wait_ge(opB_lo, 4 * DA_PAIRS + hf + 1)

            def last_values():
                pe.wait_ge(opB_lo, 4 * DA_PAIRS + last_pair)
                mla_values(last_pair, 1)

            def scores_and_values():
                mla_scores(last_pair)
                mla_values(last_pair - 1, 0)

            block_tok(B_BWO, 1, U_BWO[1], opB, ready=heads_ready, aside={
                0: lambda: mla_transposes(last_pair, 1),
                1: scores_and_values,
                3: lambda: mla_weightsT(last_pair),
                4: last_values})
            out_proj(B_BWO, U_BWO, V_BWO)
            mlp(1, V_BWO, None)

        @block.scalar
        def _(act):
            fn = nc.scalar.activation

            def split(b, hf, kind=None):
                r = hf // 2
                c0, place = 2 * (hf % 2), 2 * (hf % 4)
                act.wait_ge(raw_ready[r], 16 * b + 16)
                if kind == "rq":
                    act.wait_ge(dq_ready[r], 16)
                if not isinstance(b, int) or 8 * b + hf >= 4:
                    act.wait_ge(pe_halves, 8 * b + hf - 3)
                if kind in ("dkv", "rq"):
                    for c in range(2):
                        k = 4 * r + c0 + c
                        parts = [(0, NB, G_KVIN)] if kind == "dkv" else [(0, ROPE, G_KVIN), (ROPE, ROPE + Q_LORA, G_B)]
                        for n0, n1, g in parts:
                            done = fn(whi[:, place + c, n0:n1], raw[:, r, c0 + c, n0:n1], ACT.Copy,
                                      scale=gains[:, g + k:g + k + 1])
                else:
                    n, ch = (Q_LORA, 2 - hf % 2) if kind == "mla" and r % 2 else (NB, 2)
                    done = fn(whi[:, place:place + ch, 0:n], raw[:, r, c0:c0 + ch, 0:n], ACT.Copy)
                done.then_inc(hi_ready, 1)

            def body(b, asides=None, kind=None, nxt=None):
                for hf in range(3, 11):
                    if hf < 8:
                        split(b, hf, kind)
                    else:
                        split(b + 1, hf - 8, nxt)
                    if asides and hf in asides:
                        asides[hf]()

            def used(b):
                act.wait_ge(pe_halves, 8 * b + 8)

            def x_squares(v, s, uses):
                act.wait_ge(drained[s], 2 * uses)
                j = v % JB
                for t in range(TT):
                    if v or t:
                        act.wait_ge(xsq, 2 * v + t)
                    fn(junk[:, 0, :], xs[:, t, NB * j:NB * j + NB], ACT.Square,
                       accum_out=xss[:, v // JB, t, j:j + 1]).then_inc(xsq, 1)

            def x_hi(v, gain):
                j = v % JB
                for k in range(2):
                    act.wait_ge(xT_done, 2 * v + k + 1)
                    for cc in range(2):
                        c = JB * j + 2 * k + cc
                        g = {} if gain is None else {"scale": gains[:, gain + c:gain + c + 1]}
                        fn(opA[:, c, 0, :], side[2 * (v % 2) + k][:, SEQ * cc:SEQ * cc + SEQ], ACT.Copy,
                           **g).then_inc(xT_hi, 1)

            def start_tables():
                act.wait_ge(trig_step, 15)
                tables = ((cosA, 1, 0, 16, 1.0, 1.0), (sinA, 0, 0, 16, -1.0, 1.0), (cosB, 1, 16, 32, 1.0, 1.0),
                          (sinB, 0, 16, 32, -1.0, 1.0))
                for tab, k, f0, n, s0, s1 in tables:
                    fn(tab[:, :, 0:n], trig[:, k, :, f0:f0 + n], ACT.Sin, scale=s0)
                    fn(tab[:, :, n:2 * n], trig[:, k, :, f0:f0 + n], ACT.Sin, scale=s1).then_inc(tables_ready, 1)
                act.wait_ge(lam_step, 2)
                fn(lam_s[:, 2:4], lam_s[:, 0:2], ACT.Exp).then_inc(lam_step, 1)

            def start_squares(groups):
                for v in groups:
                    act.wait_ge(x_in[v], 16)
                    for t in range(TT):
                        if v or t:
                            act.wait_ge(xsq, 2 * v + t)
                        fn(junk[:, 0, :], xs[:, t, NB * v:NB * v + NB], ACT.Square,
                           accum_out=xss[:, 0, t, v:v + 1]).then_inc(xsq, 1)

            act.wait_ge(const_ready, 1)
            fn(rope_a[:, 0, 0, 0:4], neg_half[:], ACT.Copy)
            act.wait_ge(gains_ready, 1)
            x_hi(V_INIT, G_A)
            act.dma_start(pos_i[:], positions.rearrange("a (t p) -> p (a t)", p=P),
                          allow_slow_non_contiguous=True).then_inc(small_in, 16)
            act.dma_start(invf[:], freqs).then_inc(small_in, 16)
            act.dma_start(lam_rows, a_lambda.rearrange("a r n -> (a r n)").partition_broadcast(P).rearrange(
                "p (r n) -> p r n", r=4)).then_inc(small_in, 16)
            for row, g in ((G_MLP[0], mlp_norm_g[0]), (G_MLP[1], mlp_norm_g[1]), (G_KVIN, kv_in_norm_g),
                           (G_B, b_norm_g[0]), (G_KV, kv_norm_g), (G_Q, b_q_norm_g[0]), (G_SUB, a_subln_g[0])):
                n = g.shape[0] // P
                act.dma_start(gain_rows[row - KC:row - KC + n, :], g.rearrange("(c p) -> c p", p=P)).then_inc(gains_in, 16)
            start_squares((0, 1))
            split(0, 0)
            split(0, 1)
            x_hi(V_INIT + 1, G_A)
            split(0, 2)

            def drain_scaled(b, s, dst, scale, n=NB):
                used(b)
                for t in range(TT):
                    fn(dst(t), acc[s][:, t, 0:n], ACT.Copy, scale=scale(t)).then_inc(drained[s], 1)

            def drain_qkv(b, s, dst, i=None):
                act.wait_ge(rs_ready, 1)
                if i is not None and not (isinstance(i, int) and i == 0):
                    act.wait_ge(qkT_done, i)
                drain_scaled(b, s, lambda t: dst[:, t, :], lambda t: rs[:, 0, t:t + 1])

            def copy_qkT(i, dst, b0):
                act.wait_ge(qkT_done, i + 1)
                for k in range(2):
                    fn(dst[:, 2 * k:2 * k + 2, :], side[b0 + k][:].rearrange("p (h t) -> p h t", h=2),
                       ACT.Copy).then_inc(qkT_ready, 1)

            def exps(maps_before, maps, banks, scale):
                for m in maps:
                    act.wait_ge(bias_ready, maps_before + m + 1)
                    for t, (c0, c1) in enumerate(((0, P), (P, KEYS))):
                        done = fn(prob[:, banks[m], c0:c1], prob[:, banks[m], c0:c1], ACT.Exp, scale=scale,
                                  bias=bias[:, banks[m], t:t + 1], accum_out=rowsum[:, banks[m], t:t + 1])
                    done.then_inc(exp_done, 1)

            def copy_attnT(heads_before, b0):
                for h in range(2):
                    act.wait_ge(attnT_done, heads_before + h + 1)
                    fn(attnT[:, h, :], side[b0 + h][:, 0:KEYS], ACT.Copy).then_inc(attnT_ready, 1)

            def o_squares(p):
                for h in range(2):
                    act.wait_ge(pv_done, 2 * p + h + 1)
                    for t in range(TT):
                        done = fn(junk[:, h, SEQ * t:SEQ * t + SEQ], side[h][:, SEQ * t:SEQ * t + SEQ], ACT.Square,
                                  accum_out=oss[:, 2 * h + t:2 * h + t + 1])
                done.then_inc(oss_ready, 1)

            def o_hi(p):
                for h in range(2):
                    act.wait_ge(oT_done, 2 * p + h + 1)
                    for e in range(2):
                        fn(opB[:, bass.ds(4 * p + 2 * h + e, 1), 0, :], side[h][:, SEQ * e:SEQ * e + SEQ].unsqueeze(1),
                           ACT.Copy, scale=gains[:, G_SUB + e:G_SUB + e + 1]).then_inc(opB_hi, 1)

            def qkv(p, first):
                b = B_QKV + 3 * p
                pv = None if first else p - 1
                body(b, {3: lambda: x_hi(V_INIT + 2, G_A), 5: lambda: x_hi(V_INIT + 3, G_A),
                         6: lambda: start_squares((2,)), 8: lambda: start_squares((3,))} if first else {
                    4: lambda: exps(4 * pv, (0, 1), (0, 1, 2, 3), DA_SCALE),
                    5: lambda: exps(4 * pv, (2, 3), (0, 1, 2, 3), DA_SCALE)})
                drain_qkv(b, 0, stage, 2 * p)
                body(b + 1, {3: start_tables, 8: lambda: copy_qkT(2 * p, qT, 0)} if first else {
                    4: lambda: copy_attnT(2 * pv, 2),
                    5: lambda: copy_qkT(2 * p, qT, 0),
                    7: lambda: o_squares(pv)})
                drain_qkv(b + 1, 1, stage, 2 * p + 1)
                asides = {6: lambda: copy_qkT(2 * p + 1, kT, 2)}
                if not first:
                    asides[4] = lambda: o_hi(pv)
                body(b + 2, asides)
                drain_qkv(b + 2, 0, kv_sb[:, 0])

            qkv(0, True)
            act.wait_ge(gains_ready, 3)
            with act.Fori(1, DA_PAIRS) as p:
                qkv(p, False)
            last = DA_PAIRS - 1

            def rest():
                copy_attnT(2 * last, 2)
                o_squares(last)
                o_hi(last)

            body(B_WO, {4: lambda: exps(4 * last, (0, 1), (0, 1, 2, 3), DA_SCALE),
                        5: lambda: exps(4 * last, (2, 3), (0, 1, 2, 3), DA_SCALE), 7: rest})

            def out_proj(b0, uses, v0, gain):
                x_squares(v0, 1, uses[1] + 1)
                for j in range(1, JB):
                    s = (j + 1) % 2
                    body(b0 + j, {4: lambda: x_hi(v0 + j - 1, gain)})
                    x_squares(v0 + j, s, uses[s] + j // 2 + 1)

            out_proj(B_WO, U_WO, V_WO, G_MLP[0])

            def mlp(l, v_in, v_out, nxt, squares_from):
                u = U_MLP[l]

                def drain_up(b, s, t):
                    used(b)
                    for k in range(2):
                        fn(relu_sb[:, NB * k:NB * k + NB], acc[s][:, k, :], ACT.Relu).then_inc(relu_done, 1)

                def hid_hi_part(s, uses, t, j):
                    for k in range(2):
                        act.wait_ge(drained[s], 2 * uses + k + 1)
                        fn(opB[:, bass.ds(4 * j + 2 * k, 2), 0, :],
                           sq_sb[:, NB * k:NB * k + NB].rearrange("p (c t) -> p c t", c=2),
                           ACT.Copy).then_inc(hid_hi, 1)

                def up_block(q, i, k, asides=None):
                    b, s = B_MLP[l] + 2 * JB * q + 2 * i + k, 1 - k
                    body(b, asides)
                    t = JB * (QUARTERS * l + q) + 2 * i + k
                    drain_up(b, s, t)
                    hid_hi_part(s, u[s] + JB * q + i, t, 2 * i + k)

                for j in range(JB):
                    up_block(0, j // 2, j % 2, {} if j else {4: lambda: x_hi(v_in + JB - 1, G_MLP[l])})
                with act.Fori(0, QUARTERS - 1) as q:
                    with act.Fori(0, JB) as j:
                        body(B_MLP[l] + 2 * JB * q + JB + j)
                    with act.Fori(0, JB // 2) as i:
                        for k in range(2):
                            up_block(q + 1, i, k)
                q = QUARTERS - 1
                for j in range(JB):
                    s = (j + 1) % 2
                    asides = {}
                    if v_out is not None and j:
                        asides[4] = lambda: x_hi(v_out + j - 1, None)
                    if l == 1 and j == JB - 1:
                        for hf in range(3, 8):
                            split(B_MLP[l] + 2 * JB * q + JB + j, hf)
                    else:
                        body(B_MLP[l] + 2 * JB * q + JB + j, asides, nxt=nxt if j == JB - 1 else None)
                    x_squares(squares_from + j, s, u[s] + JB * q + 2 + j // 2 + 1)

            mlp(0, V_WO, V_MLP0, "dkv", V_MLP0)

            def latent(k, b, s, dst, n, c0):
                act.wait_ge(rs_ready, 3)
                used(b)
                for t in range(TT):
                    if k or t:
                        act.wait_ge(lat_ss, 2 * k + t)
                    fn(junk[:, 0, 0:n - c0], acc[s][:, t, c0:n], ACT.Square, scale=rs[:, 2, t:t + 1],
                       accum_out=lss[:, k, t:t + 1]).then_inc(lat_ss, 1)
                for t in range(TT):
                    fn(dst[:, t, 0:n], acc[s][:, t, 0:n], ACT.Copy, scale=rs[:, 2, t:t + 1]).then_inc(drained[s], 1)

            def latent_hi(buf, c0, n, bank, before, gain, done_at):
                act.wait_ge(latT_done, done_at)
                for c in range(n):
                    b, col = bank(c)
                    fn(buf[:, c0 + c, 0, :], b[:, col:col + SEQ], ACT.Copy,
                       scale=gains[:, gain + c:gain + c + 1]).then_inc(latT_hi, 1)

            body(B_DKV, {4: lambda: x_hi(V_MLP0 + JB - 1, None)}, kind="dkv", nxt="rq")
            latent(0, B_DKV, 1, stage, KV_LORA, 0)
            body(B_RQ, {5: lambda: latent_hi(opB, 12, 4, lambda c: (side[c // 2], SEQ * (c % 2)), 0, G_KV, 2)},
                 kind="rq", nxt="mla")
            latent(1, B_RQ, 0, kv_sb[:, 1], ROPE + Q_LORA, ROPE)
            act.wait_ge(latT_done, 3)
            fn(krT[:], side[2][0:ROPE, 0:SEQ], ACT.Copy).then_inc(krT_ready, 1)
            latent_hi(opA, 0, 3, lambda c: (side[3], SEQ * c) if c < 2 else (side[2], SEQ), 4, G_Q, 3)

            def mla_drain(b, hf, s, dst, scale, n):
                act.wait_ge(pe_halves, 8 * b + hf + 1)
                for t in range(TT):
                    fn(dst[:, t, 0:n], acc[s][:, t, 0:n], ACT.Copy, scale=scale(t)).then_inc(drained[s], 1)

            def mla_copies(p):
                for k, (dst, src) in enumerate(((kT[:, 0:2, :], side[0][:]), (qT[:, 0:2, :], side[1][:]))):
                    act.wait_ge(qkT_done, 2 * DA_PAIRS + 3 * p + k + 1)
                    fn(dst, src.rearrange("p (h t) -> p h t", h=2), ACT.Copy).then_inc(qkT_ready, 1)
                act.wait_ge(qkT_done, 2 * DA_PAIRS + 3 * p + 3)
                fn(qT[0:ROPE, 2:4, :], side[2][0:ROPE, :].rearrange("p (h t) -> p h t", h=2),
                   ACT.Copy).then_inc(qkT_ready, 1)

            def mla_exps(p):
                exps(4 * DA_PAIRS + 2 * p, (0, 1), (0, 1), MLA_SCALE)

            def mla_hi(p):
                act.wait_ge(pv_done, DA_HEADS + p + 1)
                fn(opB[:, bass.ds(2 * p, 2), 0, :], side[1][:].rearrange("p (h t) -> p h t", h=2),
                   ACT.Copy).then_inc(opB_hi, 1)

            def mla_pair(g, u, p, prev=True, prev2=True, nxt="mla"):
                b = B_MLA + g
                nb, h0 = (b, 4) if u == 0 else (b + 1, 0)
                split(b, 4 * u + 3, "mla")
                if prev:
                    mla_copies(p - 1)
                split(nb, h0, nxt)
                if prev:
                    mla_exps(p - 1)
                split(nb, h0 + 1, nxt)
                if prev2:
                    mla_hi(p - 2)
                split(nb, h0 + 2, nxt)
                mla_drain(b, 4 * u + 3, 1, kv_sb[:, u], lambda t: lrs[:, 0, t:t + 1], NB)
                mla_drain(b, 4 * u + 3, 0, stage, lambda t: lrs[:, 1, t:t + 1], Q_LORA)
                if prev:
                    copy_attnT(DA_HEADS + 2 * (p - 1), 2)

            act.wait_ge(lat_rs, 2)
            mla_pair(0, 0, 0, prev=False, prev2=False)
            mla_pair(0, 1, 1, prev2=False)
            with act.Fori(1, MLA_PAIRS // 2 - 1) as g:
                mla_pair(g, 0, 2 * g)
                mla_pair(g, 1, 2 * g + 1)
            mla_pair(MLA_PAIRS // 2 - 1, 0, MLA_PAIRS - 2)
            mla_pair(MLA_PAIRS // 2 - 1, 1, MLA_PAIRS - 1, nxt=None)

            last_pair = MLA_PAIRS - 1

            def mla_rest():
                copy_attnT(DA_HEADS + 2 * last_pair, 2)
                mla_hi(last_pair)

            def mla_exps_and_hi():
                mla_exps(last_pair)
                mla_hi(last_pair - 1)

            body(B_BWO, {3: lambda: mla_copies(last_pair), 5: mla_exps_and_hi, 7: mla_rest})
            out_proj(B_BWO, U_BWO, V_BWO, G_MLP[1])
            act.wait_ge(opB_lo, 4 * DA_PAIRS + MLA_PAIRS)
            act.dma_start(g_out, final_norm_g.partition_broadcast(P)).then_inc(g_out_in, 16)
            mlp(1, V_BWO, None, None, V_MLP1)
            act.wait_ge(rs_ready, 5)
            for j in range(JB):
                act.wait_ge(xg_ready, 2 * j + 1)
                fn(y_sb[j][:, 0, :], y_sb[j][:, 0, :], ACT.Copy,
                   scale=rs[:, 4, 0:1]).then_inc(out_ready[0], 1)

        @block.vector
        def _(dve):
            tt_, ts_, stt = nc.vector.tensor_tensor, nc.vector.tensor_scalar, nc.vector.scalar_tensor_tensor

            def split(b, hf, kind=None):
                r = hf // 2
                c0, place = 2 * (hf % 2), 2 * (hf % 4)
                dve.wait_ge(hi_ready, 8 * b + hf + 1)
                if kind in ("dkv", "rq"):
                    for c in range(2):
                        k = 4 * r + c0 + c
                        parts = [(0, NB, G_KVIN)] if kind == "dkv" else [(0, ROPE, G_KVIN), (ROPE, ROPE + Q_LORA, G_B)]
                        for n0, n1, g in parts:
                            done = stt(out=wlo[:, place + c, n0:n1], in0=raw[:, r, c0 + c, n0:n1],
                                       scalar=gains[:, g + k:g + k + 1], in1=whi[:, place + c, n0:n1].bitcast(F32),
                                       op0=ALU.mult, op1=ALU.subtract)
                else:
                    n, ch = (Q_LORA, 2 - hf % 2) if kind == "mla" and r % 2 else (NB, 2)
                    done = tt_(wlo[:, place:place + ch, 0:n], raw[:, r, c0:c0 + ch, 0:n],
                               whi[:, place:place + ch, 0:n].bitcast(F32), ALU.subtract)
                done.then_inc(lo_ready, 1)

            def body(b, asides=None, kind=None, nxt=None):
                for hf in range(3, 11):
                    if hf < 8:
                        split(b, hf, kind)
                    else:
                        split(b + 1, hf - 8, nxt)
                    if asides and hf in asides:
                        asides[hf]()

            def used(b):
                dve.wait_ge(pe_halves, 8 * b + 8)

            def x_lo(v, gain):
                j = v % JB
                for k in range(2):
                    dve.wait_ge(xT_hi, 4 * v + 2 * k + 2)
                    for cc in range(2):
                        c = JB * j + 2 * k + cc
                        src, hi = side[2 * (v % 2) + k][:, SEQ * cc:SEQ * cc + SEQ], opA[:, c, 0, :].bitcast(F32)
                        if gain is None:
                            tt_(opA[:, c, 1, :], src, hi, ALU.subtract).then_inc(xT_lo, 1)
                        else:
                            stt(out=opA[:, c, 1, :], in0=src, scalar=gains[:, gain + c:gain + c + 1], in1=hi,
                                op0=ALU.mult, op1=ALU.subtract).then_inc(xT_lo, 1)

            def stream_stats(t, squared):
                dve.wait_ge(xsq, 2 * JB * (t + 1))
                nc.vector.tensor_reduce(xms[:, t, :], xss[:, t, :, :], AX.X, ALU.add).then_inc(xstat, 1)
                dve.wait_ge(xstat, 2 * t + 1)
                ts_(xms2[:, t, :], xms[:, t, :], 1.0 / D, EPS, ALU.mult, ALU.add).then_inc(xstat, 1)
                if squared:
                    dve.wait_ge(xstat, 2 * t + 2)
                    nc.vector.reciprocal(rs[:, t, :], xms2[:, t, :]).then_inc(rs_ready, 1)

            n_trig = [0]

            def step(ins):
                n_trig[0] += 1
                ins.then_inc(trig_step, 1)
                dve.wait_ge(trig_step, n_trig[0])

            def start_angles():
                dve.wait_ge(small_in, 48)
                tt_(lam_rows[:, 0:4:2, :], lam_rows[:, 0:4:2, :], lam_rows[:, 1:4:2, :], ALU.mult).then_inc(lam_step, 1)
                dve.wait_ge(lam_step, 1)
                nc.vector.tensor_reduce(lam_s[:, 0:2], lam_rows[:, 0:4:2, :], AX.X, ALU.add).then_inc(lam_step, 1)
                step(nc.vector.tensor_copy(pos_f[:], pos_i[:]))
                for k in range(2):
                    for t in range(TT):
                        last_angle = ts_(trig[:, k, t, :], invf[:], pos_f[:, t:t + 1], None, ALU.mult)
                step(last_angle)
                magic = 1.5 * 2.0 ** 23
                ts_(turns[:, 0], trig[:, 0], 1.0 / TWO_PI, None, ALU.mult)
                step(ts_(turns[:, 1], trig[:, 1], 1.0 / TWO_PI, 0.25, ALU.mult, ALU.add))
                step(ts_(turns, turns, magic, None, ALU.add))
                step(ts_(turns, turns, magic, None, ALU.subtract))
                step(nc.vector.tensor_copy(turns_hi[:], turns))
                step(tt_(turns_lo, turns, turns_hi[:].bitcast(F32), ALU.subtract))
                for part in twelve_bit_parts(TWO_PI, 3):
                    for turn in (turns_hi[:].bitcast(F32), turns_lo):
                        step(stt(out=trig, in0=turn, scalar=-part, in1=trig, op0=ALU.mult, op1=ALU.add))
                step(ts_(trig[:, 1], trig[:, 1], float(np.pi / 2), None, ALU.add))
                step(ts_(trig, trig, 3.1415925, -3.1415925, ALU.min, ALU.max))

            def start_lambda():
                dve.wait_ge(lam_step, 3)
                tt_(lam_s[:, 4:5], lam_s[:, 3:4], lam_s[:, 2:3], ALU.subtract).then_inc(lam_step, 1)
                dve.wait_ge(lam_step, 4)
                ts_(lam_s[:, 5:6], lam_s[:, 4:5], LAM_INIT, None, ALU.subtract).then_inc(lam_step, 1)
                dve.wait_ge(tables_ready, 4)

            neg_lam = lam_s[:, 5:6]
            dve.wait_ge(gains_t, 1)
            nc.vector.tensor_copy(gains[:, 0:KC], side[3][:, 0:KC]).then_inc(gains_ready, 1)

            def other_gains():
                dve.wait_ge(gains_t, 2)
                nc.vector.tensor_copy(gains[:, KC:G_SUB], side[3][:, 0:G_SUB - KC]).then_inc(gains_ready, 1)
                ts_(gains[:, G_SUB:G_END], side[3][:, G_SUB - KC:G_END - KC], 1.0 - LAM_INIT, None,
                    ALU.mult).then_inc(gains_ready, 1)

            x_lo(V_INIT, G_A)
            split(0, 0)
            split(0, 1)
            x_lo(V_INIT + 1, G_A)
            split(0, 2)

            def rotate(view, cos, sin, heads, width, i):
                h = width // 2

                def b(tab, c0, c1):
                    return tab[:, :, c0:c1].unsqueeze(2).to_broadcast([P, TT, heads, c1 - c0])

                a = rope_a[:].rearrange("p t h w -> p t (h w)")[:, :, 0:heads * width].rearrange(
                    "p t (h w) -> p t h w", h=heads)
                c = rope_b[:].rearrange("p t h w -> p t (h w)")[:, :, 0:heads * width].rearrange(
                    "p t (h w) -> p t h w", h=heads)
                tt_(a, view, b(cos, 0, width), ALU.mult).then_inc(rope_parts, 1)
                tt_(c[:, :, :, 0:h], view[:, :, :, h:width], b(sin, 0, h), ALU.mult).then_inc(rope_parts, 1)
                tt_(c[:, :, :, h:width], view[:, :, :, 0:h], b(sin, h, width), ALU.mult).then_inc(rope_parts, 1)
                dve.wait_ge(rope_parts, 3 * i + 3)
                tt_(view, a, c, ALU.add).then_inc(roped, 1)

            def rope_qk(p, k):
                dve.wait_ge(drained[k], (4 if k == 0 else 2) * p + 2)
                if not (isinstance(p, int) and p == 0 and k == 0):
                    dve.wait_ge(roped, 2 * p + k)
                rotate(stage[:].rearrange("p t (h w) -> p t h w", w=DA_DIM)[:, :, :, 0:DA_ROT], cosA, sinA, 4,
                       DA_ROT, 2 * p + k)

            def softmax_bias(maps_before, m, bank, scale):
                dve.wait_ge(scores_done, maps_before + m + 1)
                tt_(prob[:, m, :], bank[:, 0:KEYS], mask[:], ALU.add).then_inc(masked, 1)
                dve.wait_ge(masked, maps_before + m + 1)
                nc.vector.tensor_reduce(nmax[:, m, 0:1], prob[:, m, 0:P], AX.X, ALU.max)
                nc.vector.tensor_reduce(nmax[:, m, 1:2], prob[:, m, P:KEYS], AX.X, ALU.max).then_inc(maxed, 1)
                dve.wait_ge(maxed, maps_before + m + 1)
                ts_(bias[:, m, :], nmax[:, m, :], -scale, None, ALU.mult).then_inc(bias_ready, 1)

            def da_softmax(p, maps):
                for m in maps:
                    softmax_bias(4 * p, m, side[m], DA_SCALE)

            def da_weights(p):
                dve.wait_ge(exp_done, 4 * p + 4)
                nc.vector.reciprocal(rinv[:], rowsum[:]).then_inc(rinv_ready, 1)
                dve.wait_ge(rinv_ready, p + 1)
                ts_(rneg[:], rinv[:], neg_lam, None, ALU.mult).then_inc(rneg_ready, 1)
                tiles = [(h, t, c0, c1) for h in range(2) for t, (c0, c1) in enumerate(((0, P), (P, KEYS)))]
                for h, t, c0, c1 in tiles:
                    ts_(prob[:, 2 * h, c0:c1], prob[:, 2 * h, c0:c1], rinv[:, 2 * h, t:t + 1], None,
                        ALU.mult).then_inc(half_attn, 1)
                dve.wait_ge(rneg_ready, p + 1)
                for k, (h, t, c0, c1) in enumerate(tiles):
                    dve.wait_ge(half_attn, 4 * p + k + 1)
                    stt(out=attn[:, h, c0:c1], in0=prob[:, 2 * h + 1, c0:c1], scalar=rneg[:, 2 * h + 1, t:t + 1],
                        in1=prob[:, 2 * h, c0:c1], op0=ALU.mult, op1=ALU.add).then_inc(attn_ready, 1)

            def o_means(p):
                dve.wait_ge(oss_ready, p + 1)
                ts_(oms[:], oss[:], 1.0 / (2 * DA_DIM), SUB_EPS, ALU.mult, ALU.add).then_inc(oms_ready, 1)

            def o_scale(p):
                dve.wait_ge(ors_ready, p + 1)
                for h in range(2):
                    for t in range(TT):
                        done = ts_(o_sb[:, h, t, :], side[h][:, SEQ * t:SEQ * t + SEQ],
                                   ors[:, 2 * h + t:2 * h + t + 1], None, ALU.mult)
                done.then_inc(o_ready, 1)

            def o_lo(p):
                for h in range(2):
                    dve.wait_ge(opB_hi, 4 * p + 2 * h + 2)
                    for e in range(2):
                        stt(out=opB[:, bass.ds(4 * p + 2 * h + e, 1), 1, :],
                            in0=side[h][:, SEQ * e:SEQ * e + SEQ].unsqueeze(1),
                            scalar=gains[:, G_SUB + e:G_SUB + e + 1],
                            in1=opB[:, bass.ds(4 * p + 2 * h + e, 1), 0, :].bitcast(F32), op0=ALU.mult,
                            op1=ALU.subtract).then_inc(opB_lo, 1)

            def qkv(p, first):
                b = B_QKV + 3 * p
                pv = None if first else p - 1
                body(b, {3: lambda: x_lo(V_INIT + 2, G_A), 5: lambda: x_lo(V_INIT + 3, G_A), 6: start_angles,
                         9: lambda: stream_stats(0, False)} if first else {
                    3: lambda: da_softmax(pv, (0, 1)), 4: lambda: da_softmax(pv, (2, 3)), 6: lambda: da_weights(pv)})
                if not first:
                    rope_qk(p, 0)
                body(b + 1, {4: start_lambda, 5: lambda: rope_qk(p, 0), 6: other_gains} if first else {7: lambda: o_means(pv), 8: lambda: o_scale(pv)})
                rope_qk(p, 1)
                body(b + 2, {} if first else {4: lambda: o_lo(pv)})

            qkv(0, True)
            with dve.Fori(1, DA_PAIRS) as p:
                qkv(p, False)
            last = DA_PAIRS - 1

            def rest():
                o_means(last)
                o_scale(last)
                o_lo(last)

            body(B_WO, {3: lambda: da_softmax(last, (0, 1)), 4: lambda: da_softmax(last, (2, 3)),
                        6: lambda: da_weights(last), 7: rest})

            def add_product(b, s, uses, cols):
                used(b)
                for t in range(TT):
                    tt_(xs[:, t, cols], acc[s][:, t, :], xs[:, t, cols], ALU.add).then_inc(drained[s], 1)

            def out_proj(b0, uses, v0, gain):
                add_product(b0, 1, uses[1], slice(0, NB))
                for j in range(1, JB):
                    s = (j + 1) % 2
                    body(b0 + j, {4: lambda: x_lo(v0 + j - 1, gain)})
                    add_product(b0 + j, s, uses[s] + j // 2, slice(NB * j, NB * j + NB))

            out_proj(B_WO, U_WO, V_WO, G_MLP[0])

            def mlp(l, v_in, v_out, nxt):
                u = U_MLP[l]

                def square_up(s, t):
                    for k in range(2):
                        dve.wait_ge(relu_done, 2 * t + k + 1)
                        stt(out=sq_sb[:, NB * k:NB * k + NB], in0=acc[s][:, k, :], scalar=0.0,
                            in1=relu_sb[:, NB * k:NB * k + NB], op0=ALU.max, op1=ALU.mult).then_inc(drained[s], 1)

                def hid_lo_part(t, j):
                    for k in range(2):
                        dve.wait_ge(hid_hi, 2 * t + k + 1)
                        tt_(opB[:, bass.ds(4 * j + 2 * k, 2), 1, :],
                            sq_sb[:, NB * k:NB * k + NB].rearrange("p (c t) -> p c t", c=2),
                            opB[:, bass.ds(4 * j + 2 * k, 2), 0, :].bitcast(F32), ALU.subtract).then_inc(hid_lo, 1)

                def up_block(q, i, k, asides=None):
                    body(B_MLP[l] + 2 * JB * q + 2 * i + k, asides)
                    t = JB * (QUARTERS * l + q) + 2 * i + k
                    square_up(1 - k, t)
                    hid_lo_part(t, 2 * i + k)

                def add_scaled(b, s, prior, cols):
                    used(b)
                    dve.wait_ge(drained[s], prior)
                    dve.wait_ge(rs_ready, 2 * l + 2)
                    for t in range(TT):
                        stt(out=xs[:, t, cols], in0=acc[s][:, t, :], scalar=rs[:, 2 * l + 1, t:t + 1],
                            in1=xs[:, t, cols], op0=ALU.mult, op1=ALU.add).then_inc(drained[s], 1)

                for j in range(JB):
                    up_block(0, j // 2, j % 2, {} if j else {
                        4: lambda: x_lo(v_in + JB - 1, G_MLP[l]), 5: lambda: stream_stats(2 * l + 1, True)})
                with dve.Fori(0, QUARTERS - 1) as q:
                    with dve.Fori(0, JB // 2) as i:
                        for k in range(2):
                            b, s = B_MLP[l] + 2 * JB * q + JB + 2 * i + k, 1 - k
                            body(b)
                            add_scaled(b, s, 2 * (u[s] + JB * q + 2 + i), bass.ds(NB * (2 * i + k), NB))
                    with dve.Fori(0, JB // 2) as i:
                        for k in range(2):
                            up_block(q + 1, i, k)
                q = QUARTERS - 1
                for j in range(JB):
                    b, s = B_MLP[l] + 2 * JB * q + JB + j, (j + 1) % 2
                    asides = {}
                    if v_out is not None and j:
                        asides[4] = lambda: x_lo(v_out + j - 1, None)
                    if l == 1 and j == JB - 1:
                        for hf in range(3, 8):
                            split(b, hf)
                    else:
                        body(b, asides, nxt=nxt if j == JB - 1 else None)
                    add_scaled(b, s, 2 * (u[s] + JB * q + 2 + j // 2), slice(NB * j, NB * j + NB))
                    if l == 1:
                        dve.wait_ge(g_out_in, 16)
                        dve.wait_ge(drained[s], 2 * (u[s] + JB * q + 2 + j // 2) + 2)
                        for t in range(TT):
                            tt_(y_sb[j][:, t, :], xs[:, t, NB * j:NB * j + NB],
                                g_out[:, NB * j:NB * j + NB], ALU.mult).then_inc(xg_ready, 1)

            mlp(0, V_WO, V_MLP0, "dkv")

            def latent_stats(k, width):
                dve.wait_ge(lat_ss, 2 * k + 2)
                ts_(lms[:, k, :], lss[:, k, :], 1.0 / width, EPS, ALU.mult, ALU.add).then_inc(lat_ms, 1)

            def latent_lo(buf, c0, n, bank, before, gain):
                for c in range(n):
                    dve.wait_ge(latT_hi, before + min(n, 2 * (c // 2) + 2))
                    b, col = bank(c)
                    stt(out=buf[:, c0 + c, 1, :], in0=b[:, col:col + SEQ], scalar=gains[:, gain + c:gain + c + 1],
                        in1=buf[:, c0 + c, 0, :].bitcast(F32), op0=ALU.mult, op1=ALU.subtract).then_inc(latT_lo, 1)

            body(B_DKV, {4: lambda: x_lo(V_MLP0 + JB - 1, None), 5: lambda: stream_stats(2, False)}, kind="dkv",
                 nxt="rq")
            latent_stats(0, KV_LORA)
            body(B_RQ, {5: lambda: latent_lo(opB, 12, 4, lambda c: (side[c // 2], SEQ * (c % 2)), 0, G_KV)},
                 kind="rq", nxt="mla")
            dve.wait_ge(drained[0], 2 * (U_DKV[0] + 1))
            dve.wait_ge(roped, 2 * DA_PAIRS)
            rotate(kv_sb[:, 1, :, 0:ROPE].unsqueeze(2), cosB, sinB, 1, ROPE, 2 * DA_PAIRS)
            latent_stats(1, Q_LORA)
            latent_lo(opA, 0, 3, lambda c: (side[3], SEQ * c) if c < 2 else (side[2], SEQ), 4, G_Q)

            def rope_mla(p):
                dve.wait_ge(drained[0], 2 * (U_MLA[0] + p) + 2)
                dve.wait_ge(roped, 2 * DA_PAIRS + 1 + p)
                rotate(stage[:, :, 0:Q_LORA].rearrange("p t (h w) -> p t h w", h=2)[:, :, :, NOPE:NOPE + ROPE], cosB,
                       sinB, 2, ROPE, 2 * DA_PAIRS + 1 + p)

            def mla_softmax(p):
                for m in range(2):
                    softmax_bias(4 * DA_PAIRS + 2 * p, m, side[3 * (1 - m)], MLA_SCALE)

            def mla_weights(p):
                dve.wait_ge(exp_done, 4 * DA_PAIRS + 2 * p + 2)
                nc.vector.reciprocal(rinv[:, 0:2, :], rowsum[:, 0:2, :]).then_inc(rinv_ready, 1)
                dve.wait_ge(rinv_ready, DA_PAIRS + p + 1)
                for h in range(2):
                    for t, (c0, c1) in enumerate(((0, P), (P, KEYS))):
                        ts_(attn[:, h, c0:c1], prob[:, h, c0:c1], rinv[:, h, t:t + 1], None,
                            ALU.mult).then_inc(attn_ready, 1)

            def mla_lo(p):
                dve.wait_ge(opB_hi, 4 * DA_PAIRS + p + 1)
                tt_(opB[:, bass.ds(2 * p, 2), 1, :], side[1][:].rearrange("p (h t) -> p h t", h=2),
                    opB[:, bass.ds(2 * p, 2), 0, :].bitcast(F32), ALU.subtract).then_inc(opB_lo, 1)

            def mla_pair(g, u, p, prev=True, prev2=True, nxt="mla"):
                b = B_MLA + g
                nb, h0 = (b, 4) if u == 0 else (b + 1, 0)
                split(b, 4 * u + 3, "mla")
                split(nb, h0, nxt)
                if prev:
                    mla_softmax(p - 1)
                    mla_weights(p - 1)
                split(nb, h0 + 1, nxt)
                if prev2:
                    mla_lo(p - 2)
                split(nb, h0 + 2, nxt)
                rope_mla(p)

            mla_pair(0, 0, 0, prev=False, prev2=False)
            mla_pair(0, 1, 1, prev2=False)
            with dve.Fori(1, MLA_PAIRS // 2 - 1) as g:
                mla_pair(g, 0, 2 * g)
                mla_pair(g, 1, 2 * g + 1)
            mla_pair(MLA_PAIRS // 2 - 1, 0, MLA_PAIRS - 2)
            mla_pair(MLA_PAIRS // 2 - 1, 1, MLA_PAIRS - 1, nxt=None)
            last_pair = MLA_PAIRS - 1

            def weights_and_lo():
                mla_weights(last_pair)
                mla_lo(last_pair - 1)

            body(B_BWO, {4: lambda: mla_softmax(last_pair), 6: weights_and_lo, 7: lambda: mla_lo(last_pair)})
            out_proj(B_BWO, U_BWO, V_BWO, G_MLP[1])
            mlp(1, V_BWO, None, None)
            stream_stats(4, False)
            dve.wait_ge(rs_ready, 5)
            for j in range(JB):
                dve.wait_ge(xg_ready, 2 * j + 2)
                ts_(y_sb[j][:, 1, :], y_sb[j][:, 1, :], rs[:, 4, 1:2], None, ALU.mult).then_inc(out_ready[1], 1)


_INS = ["x", "positions", "a_norm_g", "a_w_qkv", "a_lambda", "a_subln_g", "a_w_o", "kv_in_norm_g", "w_dkv",
        "kv_norm_g", "w_ukv", "b_norm_g", "b_w_dq", "b_q_norm_g", "b_w_uq", "b_w_o", "mlp_norm_g", "w_up", "w_down",
        "final_norm_g"]


def kernel(**inputs):
    import concourse.bacc as _bacc
    from concourse.bass_utils import run_bass_kernel_spmd as _run

    nc = _bacc.Bacc("TRN2", target_bir_lowering=False, num_devices=1)
    arrays, args = {}, []
    for name in _INS:
        a = np.ascontiguousarray(inputs[name])
        arrays[f"in_{name}"] = a
        args.append(nc.dram_tensor(f"in_{name}", a.shape, mybir.dt.from_np(a.dtype), kind="ExternalInput").ap())
    arrays["in_freqs"] = rope_frequencies()
    args.append(nc.dram_tensor("in_freqs", (P, 48), F32, kind="ExternalInput").ap())
    args.append(nc.dram_tensor("out_0", (1, SEQ, D), F32, kind="ExternalOutput").ap())
    trunk(nc, *args)
    r = _run(nc, [arrays], core_ids=[0])
    return r.results[0]["out_0"]
```

```python
from contextlib import ExitStack

import concourse.bass as bass
import numpy as np
from concourse import mybir

F32 = mybir.dt.float32
F32R = mybir.dt.float32r
I32 = mybir.dt.int32
ALU = mybir.AluOpType
ACT = mybir.ActivationFunctionType
AX = mybir.AxisListType

P = 128
SEQ, D = 256, 2048
TT = SEQ // P
KC = D // P
NB = 512
DFF = 4 * D
DA_HEADS, DA_DIM, DA_ROT = 8, 128, 32
MLA_HEADS, Q_LORA, KV_LORA, NOPE, ROPE, VDIM = 16, 384, 512, 128, 64, 128
THETA = 500000.0
EPS, SUB_EPS = 1e-6, 1e-5
LAM_INIT = 0.2
DA_SCALE = float(DA_DIM) ** -0.5
MLA_SCALE = float(NOPE + ROPE) ** -0.5
MASKED = -3.0e38
KEYS = P + 2 * P

DA_PAIRS = DA_HEADS // 2
QUARTERS = DFF // D
JB = D // NB
MLA_PAIRS = MLA_HEADS // 2

B_QKV = 0
B_WO = B_QKV + 3 * DA_PAIRS
B_MLP = [B_WO + JB, 0]
B_DKV = B_MLP[0] + 2 * JB * QUARTERS
B_RQ = B_DKV + 1
B_MLA = B_RQ + 1
B_BWO = B_MLA + MLA_PAIRS // 2
B_MLP[1] = B_BWO + JB
B_END = B_MLP[1] + 2 * JB * QUARTERS

U_WO = (2 * DA_PAIRS, DA_PAIRS)
U_MLP = [(U_WO[0] + 2, U_WO[1] + 2), None]
U_DKV = (U_MLP[0][0] + 16, U_MLP[0][1] + 16)
U_MLA = (U_DKV[0] + 1, U_DKV[1] + 1)
U_BWO = (U_MLA[0] + MLA_PAIRS, U_MLA[1] + MLA_PAIRS)
U_MLP[1] = (U_BWO[0] + 2, U_BWO[1] + 2)

G_A, G_MLP, G_KVIN, G_B, G_KV, G_Q, G_SUB, G_END = 0, (16, 32), 48, 64, 80, 84, 87, 89

V_INIT, V_WO, V_MLP0, V_BWO, V_MLP1 = 0, 4, 8, 12, 16

TWO_PI = 2 * np.pi


def twelve_bit_parts(value, n):
    parts = []
    for _ in range(n):
        e = np.floor(np.log2(abs(value))) - 11
        part = np.trunc(value / 2.0 ** e) * 2.0 ** e
        parts.append(float(part))
        value -= part
    return parts


def rope_frequencies():
    a = np.float32(THETA) ** (-np.arange(0, DA_ROT, 2, dtype=np.float32) / np.float32(DA_ROT))
    b = np.float32(THETA) ** (-np.arange(0, ROPE, 2, dtype=np.float32) / np.float32(ROPE))
    return np.tile(np.concatenate([a, b]).astype(np.float32)[None], (P, 1))


def trunk(nc, x, positions, a_norm_g, a_w_qkv, a_lambda, a_subln_g, a_w_o, kv_in_norm_g, w_dkv, kv_norm_g,
          w_ukv, b_norm_g, b_w_dq, b_q_norm_g, b_w_uq, b_w_o, mlp_norm_g, w_up, w_down, final_norm_g, freqs,
          out):
    def chunked(w):
        return w.rearrange("(c p) n -> p c n", p=P)

    W_QKV, W_O, W_BO = chunked(a_w_qkv[0]), chunked(a_w_o[0]), chunked(b_w_o[0])
    W_UP = [chunked(w_up[l]) for l in range(2)]
    W_DOWN = [chunked(w_down[l]) for l in range(2)]
    W_DKV, W_DQ, W_UKV, W_UQ = chunked(w_dkv), chunked(b_w_dq[0]), chunked(w_ukv), chunked(b_w_uq[0])
    x_tok = x[0].rearrange("(t p) n -> p t n", p=P)
    out_tok = out[0].rearrange("(t p) n -> p t n", p=P)

    with ExitStack() as ctx:
        def sb(name, shape, dt=F32):
            return ctx.enter_context(nc.sbuf_tensor(name, shape, dt))

        def psum(name, shape):
            return ctx.enter_context(nc.psum_tensor(name, shape, F32))

        def sem(name):
            return ctx.enter_context(nc.semaphore(name))

        xs = sb("xs", [P, TT, D])
        opA = sb("opA", [P, KC, 2, SEQ], F32R)
        opB = sb("opB", [P, KC, 2, SEQ], F32R)
        raw = sb("raw", [P, 4, 4, NB])
        whi = sb("whi", [P, 8, NB], F32R)
        wlo = sb("wlo", [P, 8, NB], F32R)
        stage = sb("stage", [P, TT, NB])
        kv_sb = sb("kv_sb", [P, 2, TT, NB])
        qkT = sb("qkT", [P, 2, 4 * SEQ])
        krT = sb("krT", [ROPE, SEQ])
        rope_a = sb("rope_a", [P, TT, 4, DA_ROT])
        rope_b = sb("rope_b", [P, TT, 4, DA_ROT])
        prob = sb("prob", [P, 4, KEYS])
        attn = sb("attn", [P, 2, KEYS])
        attnT = sb("attnT", [P, 2, KEYS])
        o_sb = sb("o_sb", [P, 2, TT, 2 * DA_DIM])
        relu_sb = sb("relu_sb", [P, 2 * NB])
        sq_sb = sb("sq_sb", [P, 2 * NB])
        junk = sb("junk", [P, 2, NB])
        mask = sb("mask", [P, KEYS])
        ident = sb("ident", [P, P])
        gains = sb("gains", [P, G_END])
        invf = sb("invf", [P, 48])
        pos_i = sb("pos_i", [P, TT], I32)
        pos_f = sb("pos_f", [P, TT])
        cosA, sinA = sb("cosA", [P, TT, DA_ROT]), sb("sinA", [P, TT, DA_ROT])
        cosB, sinB = sb("cosB", [P, TT, ROPE]), sb("sinB", [P, TT, ROPE])
        lam_s = sb("lam_s", [P, 8])
        neg_half = sb("neg_half", [P, 4])
        xss = sb("xss", [P, 5, TT, JB])
        xms = sb("xms", [P, 5, TT])
        xms2 = sb("xms2", [P, 5, TT])
        rs = sb("rs", [P, 5, TT])
        lss = sb("lss", [P, 2, TT])
        lms = sb("lms", [P, 2, TT])
        lrs = sb("lrs", [P, 2, TT])
        nmax = sb("nmax", [P, 4, TT])
        bias = sb("bias", [P, 4, TT])
        rowsum = sb("rowsum", [P, 4, TT])
        rinv = sb("rinv", [P, 4, TT])
        rneg = sb("rneg", [P, 4, TT])
        oss = sb("oss", [P, 4])
        oms = sb("oms", [P, 4])
        ors = sb("ors", [P, 4])
        qT = qkT[:, 0, :].rearrange("p (h t) -> p h t", h=4)
        kT = qkT[:, 1, :].rearrange("p (h t) -> p h t", h=4)
        g_out = qkT[:].rearrange("p a n -> p (a n)")
        y_sb = [kv_sb[:, 0], kv_sb[:, 1], stage[:], o_sb[:].rearrange("p h t (a n) -> p (h t a) n", a=1).rearrange(
            "p (t k) n -> p t (k n)", t=TT)]
        gain_rows_a = relu_sb[0:KC, P:2 * P]
        gain_rows = relu_sb[0:G_END, 0:P]
        lam_rows = sq_sb[:, 0:4 * P].rearrange("p (a n) -> p a n", a=4)
        trig = prob[:, 0, :].rearrange("p (s w) -> p s w", s=2)[:, :, 0:TT * 48].rearrange(
            "p s (t f) -> p s t f", t=TT)
        turns = prob[:, 1, :].rearrange("p (s w) -> p s w", s=2)[:, :, 0:TT * 48].rearrange(
            "p s (t f) -> p s t f", t=TT)
        turns_lo = prob[:, 2, :].rearrange("p (s w) -> p s w", s=2)[:, :, 0:TT * 48].rearrange(
            "p s (t f) -> p s t f", t=TT)
        turns_hi = sb("turns_hi", [P, 2, TT, 48], F32R)

        acc = [psum(f"acc{s}", [P, 2, NB]) for s in range(2)]
        side = [psum(f"side{i}", [P, NB]) for i in range(4)]

        raw_ready = [sem(f"raw_ready{r}") for r in range(4)]
        first_ready = sem("first_ready")
        dq_ready = [sem(f"dq_ready{r}") for r in range(4)]
        x_in = [sem(f"x_in{j}") for j in range(JB)]
        small_in = sem("small_in")
        gain_a_in = sem("gain_a_in")
        gains_in = sem("gains_in")
        g_out_in = sem("g_out_in")
        out_done = sem("out_done")
        const_ready = sem("const_ready")
        gains_t = sem("gains_t")
        gains_ready = sem("gains_ready")
        trig_step = sem("trig_step")
        tables_ready = sem("tables_ready")
        lam_step = sem("lam_step")
        hi_ready = sem("hi_ready")
        lo_ready = sem("lo_ready")
        pe_halves = sem("pe_halves")
        bank0_done = sem("bank0_done")
        drained = [sem(f"drained{s}") for s in range(2)]
        xT_done = sem("xT_done")
        xT_hi = sem("xT_hi")
        xT_lo = sem("xT_lo")
        xsq = sem("xsq")
        xstat = sem("xstat")
        rs_ready = sem("rs_ready")
        rope_parts = sem("rope_parts")
        roped = sem("roped")
        qkT_done = sem("qkT_done")
        qkT_ready = sem("qkT_ready")
        scores_done = sem("scores_done")
        masked = sem("masked")
        maxed = sem("maxed")
        bias_ready = sem("bias_ready")
        exp_done = sem("exp_done")
        rinv_ready = sem("rinv_ready")
        rneg_ready = sem("rneg_ready")
        half_attn = sem("half_attn")
        attn_ready = sem("attn_ready")
        attnT_done = sem("attnT_done")
        attnT_ready = sem("attnT_ready")
        pv_done = sem("pv_done")
        oss_ready = sem("oss_ready")
        oms_ready = sem("oms_ready")
        ors_ready = sem("ors_ready")
        o_ready = [sem("o_ready0"), sem("o_ready1")]
        oT_done = sem("oT_done")
        opB_hi = sem("opB_hi")
        opB_lo = sem("opB_lo")
        relu_done = sem("relu_done")
        hid_hi = sem("hid_hi")
        hid_lo = sem("hid_lo")
        lat_ss = sem("lat_ss")
        lat_ms = sem("lat_ms")
        lat_rs = sem("lat_rs")
        ckv_ready = sem("ckv_ready")
        latT_done = sem("latT_done")
        latT_hi = sem("latT_hi")
        latT_lo = sem("latT_lo")
        krT_ready = sem("krT_ready")
        xg_ready = sem("xg_ready")
        out_ready = [sem("out_ready0"), sem("out_ready1")]

        block = ctx.enter_context(nc.Block())

        @block.sync
        def _(sp):
            def quad(b, r, src, first=False):
                if not first:
                    sp.wait_ge(lo_ready, 8 * b + 2 * r - 6)
                sp.dma_start(raw[:, r, 0:src.shape[1], 0:src.shape[2]], src).then_inc(raw_ready[r], 16)

            def whole(b, w, col, row=0):
                for r in range(4):
                    quad(b, r, w[:, bass.ds(row + 4 * r, 4), bass.ds(col, NB)])

            def qkv(p, first):
                if first:
                    sp.dma_start(gain_rows_a, a_norm_g[0].rearrange("(c p) -> c p", p=P)).then_inc(gain_a_in, 16)

                    def small_loads():
                        sp.dma_start(pos_i[:], positions.rearrange("a (t p) -> p (a t)", p=P),
                                      allow_slow_non_contiguous=True).then_inc(small_in, 16)
                        sp.dma_start(invf[:], freqs).then_inc(small_in, 16)
                        sp.dma_start(lam_rows, a_lambda.rearrange("a r n -> (a r n)").partition_broadcast(P).rearrange(
                            "p (r n) -> p r n", r=4)).then_inc(small_in, 16)
                        for row, g in ((G_MLP[0], mlp_norm_g[0]), (G_MLP[1], mlp_norm_g[1]), (G_KVIN, kv_in_norm_g),
                                       (G_B, b_norm_g[0]), (G_KV, kv_norm_g), (G_Q, b_q_norm_g[0]), (G_SUB, a_subln_g[0])):
                            n = g.shape[0] // P
                            sp.dma_start(gain_rows[row - KC:row - KC + n, :], g.rearrange("(c p) -> c p", p=P)).then_inc(gains_in, 16)

                    for j in range(JB):
                        sp.dma_start(xs[:, :, NB * j:NB * j + NB], x_tok[:, :, NB * j:NB * j + NB]).then_inc(x_in[j], 16)
                        if j == JB - 1:
                            small_loads()
                        if j == 0:
                            sp.dma_start(raw[:, 0, 0:2, :], W_QKV[:, 0:2, 0:NB]).then_inc(first_ready, 16)
                            sp.dma_start(raw[:, 0, 2:4, :], W_QKV[:, 2:4, 0:NB]).then_inc(raw_ready[0], 16)
                        else:
                            quad(B_QKV, j, W_QKV[:, 4 * j:4 * j + 4, 0:NB], True)
                else:
                    whole(B_QKV + 3 * p, W_QKV, NB * p)
                whole(B_QKV + 3 * p + 1, W_QKV, NB * p + D)
                whole(B_QKV + 3 * p + 2, W_QKV, NB * p + 2 * D)

            qkv(0, True)
            with sp.Fori(1, DA_PAIRS) as p:
                qkv(p, False)
            with sp.Fori(0, JB) as j:
                whole(B_WO + j, W_O, NB * j)

            def mlp(l):
                with sp.Fori(0, QUARTERS) as q:
                    with sp.Fori(0, JB) as j:
                        whole(B_MLP[l] + 2 * JB * q + j, W_UP[l], D * q + NB * j)
                    with sp.Fori(0, JB) as j:
                        whole(B_MLP[l] + 2 * JB * q + JB + j, W_DOWN[l], NB * j, row=KC * q)

            mlp(0)
            whole(B_DKV, W_DKV, 0)
            for r in range(4):
                quad(B_RQ, r, W_DKV[:, 4 * r:4 * r + 4, KV_LORA:KV_LORA + ROPE])
                sp.dma_start(raw[:, r, :, ROPE:ROPE + Q_LORA], W_DQ[:, 4 * r:4 * r + 4, :]).then_inc(dq_ready[r], 16)
            with sp.Fori(0, MLA_PAIRS // 2) as g:
                for u in range(2):
                    quad(B_MLA + g, 2 * u, W_UKV[:, :, bass.ds(2 * NB * g + NB * u, NB)])
                    quad(B_MLA + g, 2 * u + 1, W_UQ[:, :, bass.ds(2 * Q_LORA * g + Q_LORA * u, Q_LORA)])
            with sp.Fori(0, JB) as j:
                whole(B_BWO + j, W_BO, NB * j)
            mlp(1)
            for j in range(JB):
                for t in range(TT):
                    sp.wait_ge(out_ready[t], j + 1)
                sp.dma_start(out_tok[:, :, NB * j:NB * j + NB], y_sb[j]).then_inc(out_done, 16)
            sp.wait_ge(out_done, 16 * JB)

        @block.gpsimd
        def _(pool):
            nc.gpsimd.memset(neg_half[:], -0.5).then_inc(const_ready, 1)
            nc.gpsimd.memset(ident[:], 0.0).then_inc(const_ready, 1)
            nc.gpsimd.memset(mask[:], 0.0).then_inc(const_ready, 1)
            pool.wait_ge(const_ready, 3)
            nc.gpsimd.affine_select(out=ident[:], in_=ident[:], compare_op=ALU.not_equal, fill=1.0, base=0,
                                    pattern=[[-1, P]], channel_multiplier=1).then_inc(const_ready, 1)
            for c in (0, 2 * P):
                nc.gpsimd.affine_select(out=mask[:, c:c + P], in_=mask[:, c:c + P], compare_op=ALU.is_ge,
                                        fill=MASKED, base=0, pattern=[[-1, P]],
                                        channel_multiplier=1).then_inc(const_ready, 1)

            def stream_scale(t):
                pool.wait_ge(xstat, 2 * t + 2)
                nc.gpsimd.tensor_tensor(rs[:, t, :], xms2[:, t, :], neg_half[:, 0:TT], ALU.pow).then_inc(rs_ready, 1)

            def sub_norm(p):
                pool.wait_ge(oms_ready, p + 1)
                nc.gpsimd.tensor_tensor(ors[:], oms[:], neg_half[:], ALU.pow).then_inc(ors_ready, 1)

            stream_scale(0)
            with pool.Fori(0, DA_PAIRS) as p:
                sub_norm(p)
            stream_scale(2)
            for k in range(2):
                pool.wait_ge(lat_ms, k + 1)
                nc.gpsimd.tensor_tensor(lrs[:, k, :], lms[:, k, :], neg_half[:, 0:TT], ALU.pow).then_inc(lat_rs, 1)
            stream_scale(4)

        @block.tensor
        def _(pe):
            mm, tr = nc.tensor.matmul, nc.tensor.transpose

            def wait_bank(s, uses, bank):
                if not (isinstance(uses, int) and uses == 0):
                    pe.wait_ge(drained[s], 2 * uses - 1 + bank)

            def half_tok(b, hf, s, op, n=NB, chunks=2, first=False, last=False, uses=0, urgent=False):
                pe.wait_ge(lo_ready, 8 * b + hf + 1)
                place = 2 * (hf % 4)
                order = [(c, t) for c in range(chunks) for t in range(TT)]
                if urgent and (first or last):
                    order = [(c, t) for t in range(TT) for c in range(chunks)]
                for c, t in order:
                    if first and c == 0:
                        wait_bank(s, uses, t)
                    a_hi, a_lo = (op[c][i][:, P * t:P * t + P] for i in range(2))
                    w_hi, w_lo = whi[:, place + c, 0:n], wlo[:, place + c, 0:n]
                    o = acc[s][:, t, 0:n]
                    mm(o, a_hi, w_hi, start=first and c == 0, stop=False)
                    mm(o, a_hi, w_lo, start=False, stop=False)
                    done = mm(o, a_lo, w_hi, start=False, stop=last and c == chunks - 1)
                    if urgent and last and t == 0 and c == chunks - 1:
                        done.then_inc(bank0_done, 1)
                done.then_inc(pe_halves, 1)

            def chunks_of(buf, c0, n=2):
                return [[buf[:, c0 + c, i, :] for i in range(2)] for c in range(n)]

            def block_tok(b, s, uses, buf, n=NB, ready=None, aside=None, urgent=False):
                for hf in range(8):
                    if ready:
                        ready(hf)
                    half_tok(b, hf, s, chunks_of(buf, 2 * hf), n, first=hf == 0, last=hf == 7, uses=uses,
                             urgent=urgent)
                    if aside and hf in aside:
                        aside[hf]()

            def block_feat(b, s, uses, ready=None, aside=None):
                for hf in range(8):
                    if ready:
                        ready(hf)
                    pe.wait_ge(lo_ready, 8 * b + hf + 1)
                    place = 2 * (hf % 4)
                    for c in range(2):
                        x_hi, x_lo = (opA[:, 2 * hf + c, i, :] for i in range(2))
                        for f in range(4):
                            if hf == 0 and c == 0 and f % 2 == 0:
                                wait_bank(s, uses, f // 2)
                            w_hi = whi[:, place + c, P * f:P * f + P]
                            w_lo = wlo[:, place + c, P * f:P * f + P]
                            o = acc[s][:, f // 2, SEQ * (f % 2):SEQ * (f % 2) + SEQ]
                            first = hf == 0 and c == 0 and f % 2 == 0
                            end = hf == 7 and c == 1 and f % 2 == 1
                            mm(o, w_hi, x_hi, start=first, stop=False, skip_group_check=True)
                            mm(o, w_hi, x_lo, start=False, stop=False, skip_group_check=True)
                            done = mm(o, w_lo, x_hi, start=False, stop=end, skip_group_check=True)
                    done.then_inc(pe_halves, 1)
                    if aside and hf in aside:
                        aside[hf]()

            def transpose_x(v, s=None, uses=None):
                if s is not None:
                    pe.wait_ge(drained[s], 2 * uses)
                if v >= 2:
                    pe.wait_ge(xT_lo, 4 * (v - 1))
                j = v % JB
                for k in range(2):
                    bank = side[2 * (v % 2) + k]
                    for cc in range(2):
                        for t in range(TT):
                            col = NB * j + P * (2 * k + cc)
                            done = tr(bank[:, SEQ * cc + P * t:SEQ * cc + P * t + P], xs[:, t, col:col + P], ident[:])
                    done.then_inc(xT_done, 1)

            pe.wait_ge(const_ready, 4)
            pe.wait_ge(gain_a_in, 16)
            tr(side[3][:, 0:KC], gain_rows_a, ident[0:KC, 0:KC]).then_inc(gains_t, 1)
            pe.wait_ge(gains_ready, 1)

            def transpose_gains():
                pe.wait_ge(gains_in, 16 * 7)
                pe.wait_ge(xT_lo, 4 * JB)
                tr(side[3][:, 0:G_END - KC], gain_rows[0:G_END - KC, :],
                   ident[0:G_END - KC, 0:G_END - KC]).then_inc(gains_t, 1)

            def transpose_x_in(v):
                pe.wait_ge(x_in[v], 16)
                transpose_x(V_INIT + v)

            def keep_busy(n):
                for _ in range(n):
                    tr(side[2][:, 0:P], ident[:], ident[:])

            keep_busy(6)
            transpose_x_in(0)
            keep_busy(28)

            def transpose_qk(i, b0):
                pe.wait_ge(roped, i + 1)
                for hh in range(4):
                    for t in range(TT):
                        done = tr(side[b0 + hh // 2][:, SEQ * (hh % 2) + P * t:SEQ * (hh % 2) + P * t + P],
                                  stage[:, t, P * hh:P * hh + P], ident[:])
                done.then_inc(qkT_done, 1)

            def da_scores(p, first=False):
                pe.wait_ge(qkT_ready, 4 * p + 4)
                if not first:
                    pe.wait_ge(opB_lo, 4 * p)
                for m in range(4):
                    mm(side[m][:, 0:P], qT[:, m, 0:P], kT[:, m, 0:P], start=True, stop=True)
                    mm(side[m][:, P:KEYS], qT[:, m, P:SEQ], kT[:, m, :], start=True,
                       stop=True).then_inc(scores_done, 1)

            def transpose_attn(heads_before, b0, masks):
                pe.wait_ge(masked, masks)
                for h in range(2):
                    pe.wait_ge(attn_ready, 2 * heads_before + 2 * h + 2)
                    for k in range(3):
                        done = tr(side[b0 + h][:, P * k:P * k + P], attn[:, h, P * k:P * k + P], ident[:])
                    done.then_inc(attnT_done, 1)

            def da_values(p, v_drained, banks_read=None):
                pe.wait_ge(drained[0], v_drained)
                if banks_read is not None:
                    pe.wait_ge(qkT_ready, banks_read)
                for h in range(2):
                    pe.wait_ge(attnT_ready, 2 * p + h + 1)
                    cols = slice(2 * DA_DIM * h, 2 * DA_DIM * (h + 1))
                    mm(side[h][:, 0:SEQ], attnT[:, h, 0:P], kv_sb[:, 0, 0, cols], start=True, stop=True)
                    mm(side[h][:, SEQ:NB], attnT[:, h, P:2 * P], kv_sb[:, 0, 0, cols], start=True, stop=False)
                    mm(side[h][:, SEQ:NB], attnT[:, h, 2 * P:KEYS], kv_sb[:, 0, 1, cols], start=False,
                       stop=True).then_inc(pv_done, 1)

            def transpose_o(p):
                for h in range(2):
                    pe.wait_ge(o_ready[h], p + 1)
                    for e in range(2):
                        for t in range(TT):
                            done = tr(side[h][:, SEQ * e + P * t:SEQ * e + P * t + P], o_sb[:, h, t, P * e:P * e + P],
                                      ident[:])
                    done.then_inc(oT_done, 1)

            def opA_ready(first):
                return lambda hf: pe.wait_ge(xT_lo, 4 * (first + hf // 2) + 4)

            def qkv(p, first):
                b = B_QKV + 3 * p
                prev = None if first else p - 1
                if first:
                    block_tok(b, 0, 0, opA, urgent=True, ready=opA_ready(V_INIT), aside={
                        0: lambda: transpose_x_in(1), 1: lambda: transpose_x_in(2), 3: lambda: transpose_x_in(3)})
                else:
                    block_tok(b, 0, 2 * p, opA, urgent=True)
                block_tok(b + 1, 1, p, opA, urgent=True, aside={0: transpose_gains, 5: lambda: transpose_qk(2 * p, 0)} if first else {
                    1: lambda: transpose_attn(2 * prev, 2, 4 * prev + 4),
                    2: lambda: transpose_qk(2 * p, 0),
                    4: lambda: da_values(prev, 4 * prev + 4, 4 * prev + 6)})
                aside = {3: lambda: transpose_qk(2 * p + 1, 2), 5: lambda: da_scores(p, first)}
                if not first:
                    aside[1] = lambda: transpose_o(prev)
                block_tok(b + 2, 0, 2 * p + 1, opA, urgent=True, aside=aside)

            qkv(0, True)
            with pe.Fori(1, DA_PAIRS) as p:
                qkv(p, False)

            last = DA_PAIRS - 1
            block_tok(B_WO, 1, U_WO[1], opB, ready=lambda hf: pe.wait_ge(opB_lo, 2 * hf + 2), aside={
                2: lambda: transpose_attn(2 * last, 2, 4 * last + 4),
                3: lambda: da_values(last, 4 * last + 4),
                4: lambda: transpose_o(last)})

            def out_proj(b0, uses, v0):
                for j in range(1, JB):
                    s, ps = (j + 1) % 2, j % 2
                    block_tok(b0 + j, s, uses[s] + j // 2, opB, aside={
                        1: lambda: transpose_x(v0 + j - 1, ps, uses[ps] + (j - 1) // 2 + 1)})

            out_proj(B_WO, U_WO, V_WO)

            def mlp(l, v_in, v_out):
                u = U_MLP[l]

                def up(q):
                    with pe.Fori(0, JB // 2) as i:
                        for k in range(2):
                            block_feat(B_MLP[l] + 2 * JB * q + 2 * i + k, 1 - k, u[1 - k] + JB * q + i)

                def hidden_ready(q):
                    return lambda hf: pe.wait_ge(hid_lo, 2 * JB * (QUARTERS * l + q) + hf + 1)

                for j in range(JB):
                    s = (j + 1) % 2
                    block_feat(B_MLP[l] + j, s, u[s] + j // 2, ready=None if j else opA_ready(v_in), aside={} if j else {
                        1: lambda: transpose_x(v_in + JB - 1, 0, u[0])})
                with pe.Fori(0, QUARTERS - 1) as q:
                    with pe.Fori(0, JB // 2) as i:
                        for k in range(2):
                            block_tok(B_MLP[l] + 2 * JB * q + JB + 2 * i + k, 1 - k, u[1 - k] + JB * q + 2 + i, opB,
                                      ready=hidden_ready(q))
                    up(q + 1)
                q = QUARTERS - 1
                for j in range(JB):
                    s, ps = (j + 1) % 2, j % 2
                    aside = {}
                    if v_out is not None and j:
                        aside[1] = lambda: transpose_x(v_out + j - 1, ps, u[ps] + JB * q + 2 + (j - 1) // 2 + 1)
                    block_tok(B_MLP[l] + 2 * JB * q + JB + j, s, u[s] + JB * q + 2 + j // 2, opB,
                              ready=hidden_ready(q), aside=aside, urgent=l == 1 and j == JB - 1)

            mlp(0, V_WO, V_MLP0)

            def transpose_ckv():
                pe.wait_ge(ckv_ready, TT)
                pe.wait_ge(xT_lo, 4 * (V_MLP0 + JB))
                for k in range(2):
                    for cc in range(2):
                        for t in range(TT):
                            col = P * (2 * k + cc)
                            done = tr(side[k][:, SEQ * cc + P * t:SEQ * cc + P * t + P], stage[:, t, col:col + P], ident[:])
                    done.then_inc(latT_done, 1)

            block_tok(B_DKV, 1, U_DKV[1], opA, ready=opA_ready(V_MLP0), aside={
                1: lambda: transpose_x(V_MLP0 + JB - 1, 0, U_DKV[0])})
            block_tok(B_RQ, 0, U_DKV[0], opA, n=ROPE + Q_LORA, aside={2: transpose_ckv})

            def transpose_cq():
                pe.wait_ge(drained[0], 2 * (U_DKV[0] + 1))
                for c in range(3):
                    for t in range(TT):
                        bank, col = (side[3], SEQ * c) if c < 2 else (side[2], SEQ)
                        tr(bank[:, col + P * t:col + P * t + P], kv_sb[:, 1, t, ROPE + P * c:ROPE + P * c + P], ident[:])
                pe.wait_ge(roped, 2 * DA_PAIRS + 1)
                for t in range(TT):
                    done = tr(side[2][0:ROPE, P * t:P * t + P], kv_sb[:, 1, t, 0:ROPE], ident[:])
                done.then_inc(latT_done, 1)

            ckvT = chunks_of(opB, 12, 4)
            cqT = chunks_of(opA, 0, 3)
            qh = qT[:, 0:2, :]
            qr = qT[0:ROPE, 2:4, :]
            kh = kT[:, 0:2, :]

            def half_kv(b, hf, op, first, uses):
                pe.wait_ge(lo_ready, 8 * b + hf + 1)
                place = 2 * (hf % 4)
                for c in range(2):
                    w_hi, w_lo = (w[:, place + c, :].rearrange("p (h a n) -> p h a n", h=2, a=2) for w in (whi, wlo))
                    c_hi, c_lo = op[c]
                    start, end = first and c == 0, not first and c == 1
                    if start:
                        wait_bank(1, uses, 0)
                    for h in range(2):
                        o = acc[1][:, 0, SEQ * h:SEQ * h + SEQ]
                        mm(o, w_hi[:, h, 0, :], c_hi, start=start and h == 0, stop=False, skip_group_check=True)
                        mm(o, w_hi[:, h, 0, :], c_lo, start=False, stop=False, skip_group_check=True)
                        mm(o, w_lo[:, h, 0, :], c_hi, start=False, stop=end and h == 1, skip_group_check=True)
                    if start:
                        wait_bank(1, uses, 1)
                    for t in range(TT):
                        o = acc[1][:, 1, SEQ * t:SEQ * t + SEQ].rearrange("p (h n) -> p h n", h=2)
                        a_hi, a_lo = (v[:, P * t:P * t + P] for v in (c_hi, c_lo))
                        mm(o, a_hi, w_hi[:, :, 1, :], start=start and t == 0, stop=False, skip_group_check=True)
                        mm(o, a_hi, w_lo[:, :, 1, :], start=False, stop=False, skip_group_check=True)
                        done = mm(o, a_lo, w_hi[:, :, 1, :], start=False, stop=end and t == 1, skip_group_check=True)
                done.then_inc(pe_halves, 1)

            def mla_transposes(p):
                pe.wait_ge(attnT_ready, DA_HEADS + 2 * p)
                pe.wait_ge(roped, 2 * DA_PAIRS + 2 + p)
                for h in range(2):
                    for t in range(TT):
                        done = tr(side[0][:, SEQ * h + P * t:SEQ * h + P * t + P],
                                  stage[:, t, 192 * h:192 * h + P], ident[:])
                done.then_inc(qkT_done, 1)
                for h in range(2):
                    for t in range(TT):
                        done = tr(side[2][0:ROPE, SEQ * h + P * t:SEQ * h + P * t + P],
                                  stage[:, t, 192 * h + P:192 * h + P + ROPE], ident[:])
                done.then_inc(qkT_done, 1)

            def mla_scores(p):
                pe.wait_ge(drained[1], 2 * (U_MLA[1] + p) + 1)
                pe.wait_ge(qkT_ready, 2 * DA_PAIRS * 2 + 2 * p + 2)
                for h in range(2):
                    bank = side[3 * (1 - h)]
                    for q0, q1, k1, o0, o1 in ((0, P, P, 0, P), (P, SEQ, SEQ, P, KEYS)):
                        mm(bank[:, o0:o1], qh[:, h, q0:q1], kh[:, h, 0:k1], start=True, stop=False)
                        done = mm(bank[:, o0:o1], qr[:, h, q0:q1], krT[:, 0:k1], start=False, stop=True)
                    done.then_inc(scores_done, 1)

            def mla_values(p, par):
                pe.wait_ge(drained[1], 2 * (U_MLA[1] + p) + 2)
                pe.wait_ge(opB_lo, 4 * DA_PAIRS + p)
                for h in range(2):
                    pe.wait_ge(attnT_ready, DA_HEADS + 2 * p + h + 1)
                    v = slice(P * h, P * h + P)
                    mm(side[1][:, SEQ * h:SEQ * (h + 1)], kv_sb[:, par, 0, v], attnT[:, h, 0:SEQ], start=True,
                       stop=False, skip_group_check=True)
                    done = mm(side[1][:, SEQ * h + P:SEQ * (h + 1)], kv_sb[:, par, 1, v], attnT[:, h, SEQ:KEYS],
                              start=False, stop=True, skip_group_check=True)
                done.then_inc(pv_done, 1)

            def mla_weightsT(p):
                transpose_attn(DA_HEADS + 2 * p, 2, 4 * DA_PAIRS + 2 * p + 2)

            def mla_pair(g, u, p, prev=True, prev2=True):
                b = B_MLA + g
                half_kv(b, 4 * u, ckvT[0:2], True, U_MLA[1] + p)
                if prev:
                    mla_transposes(p - 1)
                else:
                    transpose_cq()
                half_kv(b, 4 * u + 1, ckvT[2:4], False, U_MLA[1] + p)
                if not prev:
                    pe.wait_ge(latT_lo, 7)
                    pe.wait_ge(krT_ready, 1)
                if prev:
                    mla_scores(p - 1)
                if prev2:
                    mla_values(p - 2, u)
                half_tok(b, 4 * u + 2, 0, cqT[0:2], n=Q_LORA, first=True, uses=U_MLA[0] + p)
                half_tok(b, 4 * u + 3, 0, cqT[2:3], n=Q_LORA, chunks=1, last=True)
                if prev:
                    mla_weightsT(p - 1)

            pe.wait_ge(latT_lo, 4)
            mla_pair(0, 0, 0, prev=False, prev2=False)
            mla_pair(0, 1, 1, prev2=False)
            with pe.Fori(1, MLA_PAIRS // 2) as g:
                mla_pair(g, 0, 2 * g)
                mla_pair(g, 1, 2 * g + 1)

            last_pair = MLA_PAIRS - 1

            def heads_ready(hf):
                pe.wait_ge(opB_lo, 4 * DA_PAIRS + hf + 1)

            def scores_and_values():
                mla_scores(last_pair)
                mla_values(last_pair - 1, 0)

            block_tok(B_BWO, 1, U_BWO[1], opB, ready=heads_ready, aside={
                0: lambda: mla_transposes(last_pair),
                1: scores_and_values,
                3: lambda: mla_weightsT(last_pair),
                4: lambda: mla_values(last_pair, 1)})
            out_proj(B_BWO, U_BWO, V_BWO)
            mlp(1, V_BWO, None)

        @block.scalar
        def _(act):
            fn = nc.scalar.activation

            def split(b, hf, kind=None):
                r = hf // 2
                c0, place = 2 * (hf % 2), 2 * (hf % 4)
                if isinstance(b, int) and b + hf == 0:
                    act.wait_ge(first_ready, 16)
                else:
                    act.wait_ge(raw_ready[r], 16 * b + 16)
                if kind == "rq":
                    act.wait_ge(dq_ready[r], 16)
                if not isinstance(b, int) or 8 * b + hf >= 4:
                    act.wait_ge(pe_halves, 8 * b + hf - 3)
                if kind in ("dkv", "rq"):
                    for c in range(2):
                        k = 4 * r + c0 + c
                        parts = [(0, NB, G_KVIN)] if kind == "dkv" else [(0, ROPE, G_KVIN), (ROPE, ROPE + Q_LORA, G_B)]
                        for n0, n1, g in parts:
                            done = fn(whi[:, place + c, n0:n1], raw[:, r, c0 + c, n0:n1], ACT.Copy,
                                      scale=gains[:, g + k:g + k + 1])
                else:
                    n, ch = (Q_LORA, 2 - hf % 2) if kind == "mla" and r % 2 else (NB, 2)
                    done = fn(whi[:, place:place + ch, 0:n], raw[:, r, c0:c0 + ch, 0:n], ACT.Copy)
                done.then_inc(hi_ready, 1)

            def body(b, asides=None, kind=None, nxt=None):
                for hf in range(3, 11):
                    if hf < 8:
                        split(b, hf, kind)
                    else:
                        split(b + 1, hf - 8, nxt)
                    if asides and hf in asides:
                        asides[hf]()

            def used(b):
                act.wait_ge(pe_halves, 8 * b + 8)

            def x_squares(v, s, uses):
                j = v % JB
                for t in range(TT):
                    act.wait_ge(drained[s], 2 * uses + t - 1)
                    act.wait_ge(xsq, 2 * v + t - 1)
                    fn(junk[:, t, :], xs[:, t, NB * j:NB * j + NB], ACT.Square,
                       accum_out=xss[:, v // JB, t, j:j + 1]).then_inc(xsq, 1)

            def x_hi(v, gain):
                j = v % JB
                for k in range(2):
                    act.wait_ge(xT_done, 2 * v + k + 1)
                    for cc in range(2):
                        c = JB * j + 2 * k + cc
                        g = {} if gain is None else {"scale": gains[:, gain + c:gain + c + 1]}
                        fn(opA[:, c, 0, :], side[2 * (v % 2) + k][:, SEQ * cc:SEQ * cc + SEQ], ACT.Copy,
                           **g).then_inc(xT_hi, 1)

            def start_tables():
                act.wait_ge(trig_step, 15)
                tables = ((cosA, 1, 0, 16, 1.0, 1.0), (sinA, 0, 0, 16, -1.0, 1.0), (cosB, 1, 16, 32, 1.0, 1.0),
                          (sinB, 0, 16, 32, -1.0, 1.0))
                for tab, k, f0, n, s0, s1 in tables:
                    fn(tab[:, :, 0:n], trig[:, k, :, f0:f0 + n], ACT.Sin, scale=s0)
                    fn(tab[:, :, n:2 * n], trig[:, k, :, f0:f0 + n], ACT.Sin, scale=s1).then_inc(tables_ready, 1)
                act.wait_ge(lam_step, 2)
                fn(lam_s[:, 2:4], lam_s[:, 0:2], ACT.Exp).then_inc(lam_step, 1)

            def start_squares(groups):
                for v in groups:
                    act.wait_ge(x_in[v], 16)
                    for t in range(TT):
                        if v:
                            act.wait_ge(xsq, 2 * v + t - 1)
                        fn(junk[:, t, :], xs[:, t, NB * v:NB * v + NB], ACT.Square,
                           accum_out=xss[:, 0, t, v:v + 1]).then_inc(xsq, 1)

            act.wait_ge(const_ready, 1)
            fn(rope_a[:, 0, 0, 0:4], neg_half[:], ACT.Copy)
            act.wait_ge(gains_ready, 1)
            x_hi(V_INIT, G_A)
            split(0, 0)
            split(0, 1)
            x_hi(V_INIT + 1, G_A)
            split(0, 2)

            def drain_scaled(b, s, dst, scale, n=NB):
                act.wait_ge(bank0_done, b + 1)
                for t in range(TT):
                    if t:
                        used(b)
                    fn(dst(t), acc[s][:, t, 0:n], ACT.Copy, scale=scale(t)).then_inc(drained[s], 1)

            def drain_qkv(b, s, dst, i=None):
                act.wait_ge(rs_ready, 1)
                if i is not None and not (isinstance(i, int) and i == 0):
                    act.wait_ge(qkT_done, i)
                drain_scaled(b, s, lambda t: dst[:, t, :], lambda t: rs[:, 0, t:t + 1])

            def copy_qkT(i, dst, b0):
                act.wait_ge(qkT_done, i + 1)
                for k in range(2):
                    fn(dst[:, 2 * k:2 * k + 2, :], side[b0 + k][:].rearrange("p (h t) -> p h t", h=2),
                       ACT.Copy).then_inc(qkT_ready, 1)

            def exps(maps_before, maps, banks, scale):
                for m in maps:
                    act.wait_ge(bias_ready, maps_before + m + 1)
                    for t, (c0, c1) in enumerate(((0, P), (P, KEYS))):
                        done = fn(prob[:, banks[m], c0:c1], prob[:, banks[m], c0:c1], ACT.Exp, scale=scale,
                                  bias=bias[:, banks[m], t:t + 1], accum_out=rowsum[:, banks[m], t:t + 1])
                    done.then_inc(exp_done, 1)

            def copy_attnT(heads_before, b0):
                for h in range(2):
                    act.wait_ge(attnT_done, heads_before + h + 1)
                    fn(attnT[:, h, :], side[b0 + h][:, 0:KEYS], ACT.Copy).then_inc(attnT_ready, 1)

            def o_squares(p):
                for h in range(2):
                    act.wait_ge(pv_done, 2 * p + h + 1)
                    for t in range(TT):
                        done = fn(junk[:, h, SEQ * t:SEQ * t + SEQ], side[h][:, SEQ * t:SEQ * t + SEQ], ACT.Square,
                                  accum_out=oss[:, 2 * h + t:2 * h + t + 1])
                done.then_inc(oss_ready, 1)

            def o_scale(p):
                act.wait_ge(ors_ready, p + 1)
                for t in range(TT):
                    done = fn(o_sb[:, 1, t, :], side[1][:, SEQ * t:SEQ * t + SEQ], ACT.Copy,
                              scale=ors[:, 2 + t:3 + t])
                done.then_inc(o_ready[1], 1)

            def o_hi(p):
                for h in range(2):
                    act.wait_ge(oT_done, 2 * p + h + 1)
                    for e in range(2):
                        fn(opB[:, bass.ds(4 * p + 2 * h + e, 1), 0, :], side[h][:, SEQ * e:SEQ * e + SEQ].unsqueeze(1),
                           ACT.Copy, scale=gains[:, G_SUB + e:G_SUB + e + 1]).then_inc(opB_hi, 1)

            def qkv(p, first):
                b = B_QKV + 3 * p
                pv = None if first else p - 1
                body(b, {3: lambda: x_hi(V_INIT + 2, G_A), 4: lambda: start_squares((0,)),
                         5: lambda: x_hi(V_INIT + 3, G_A), 6: lambda: start_squares((1,)),
                         7: lambda: start_squares((2,)), 8: lambda: start_squares((3,)),
                         10: start_tables} if first else {})
                drain_qkv(b, 0, stage, 2 * p)
                body(b + 1, {8: lambda: copy_qkT(2 * p, qT, 0)} if first else {
                    4: lambda: copy_attnT(2 * pv, 2),
                    5: lambda: copy_qkT(2 * p, qT, 0),
                    7: lambda: o_squares(pv),
                    8: lambda: o_scale(pv)})
                drain_qkv(b + 1, 1, stage, 2 * p + 1)
                asides = {6: lambda: copy_qkT(2 * p + 1, kT, 2),
                          9: lambda: exps(4 * p, (0, 1), (0, 1, 2, 3), DA_SCALE)}
                if not first:
                    asides[4] = lambda: o_hi(pv)
                body(b + 2, asides)
                drain_qkv(b + 2, 0, kv_sb[:, 0])
                exps(4 * p, (2, 3), (0, 1, 2, 3), DA_SCALE)

            qkv(0, True)
            act.wait_ge(gains_ready, 3)
            with act.Fori(1, DA_PAIRS) as p:
                qkv(p, False)
            last = DA_PAIRS - 1

            def squares_and_scale():
                o_squares(last)
                o_scale(last)

            body(B_WO, {5: lambda: copy_attnT(2 * last, 2), 6: squares_and_scale, 7: lambda: o_hi(last)})

            def out_proj(b0, uses, v0, gain):
                x_squares(v0, 1, uses[1] + 1)
                for j in range(1, JB):
                    s = (j + 1) % 2
                    body(b0 + j, {4: lambda: x_hi(v0 + j - 1, gain)})
                    x_squares(v0 + j, s, uses[s] + j // 2 + 1)

            out_proj(B_WO, U_WO, V_WO, G_MLP[0])

            def mlp(l, v_in, v_out, nxt, squares_from):
                u = U_MLP[l]

                def drain_up(b, s, t):
                    used(b)
                    for k in range(2):
                        fn(relu_sb[:, NB * k:NB * k + NB], acc[s][:, k, :], ACT.Relu).then_inc(relu_done, 1)

                def hid_hi_part(s, uses, t, j):
                    for k in range(2):
                        act.wait_ge(drained[s], 2 * uses + k + 1)
                        fn(opB[:, bass.ds(4 * j + 2 * k, 2), 0, :],
                           sq_sb[:, NB * k:NB * k + NB].rearrange("p (c t) -> p c t", c=2),
                           ACT.Copy).then_inc(hid_hi, 1)

                def up_block(q, i, k, asides=None):
                    b, s = B_MLP[l] + 2 * JB * q + 2 * i + k, 1 - k
                    body(b, asides)
                    t = JB * (QUARTERS * l + q) + 2 * i + k
                    drain_up(b, s, t)
                    hid_hi_part(s, u[s] + JB * q + i, t, 2 * i + k)

                for j in range(JB):
                    up_block(0, j // 2, j % 2, {} if j else {4: lambda: x_hi(v_in + JB - 1, G_MLP[l])})
                with act.Fori(0, QUARTERS - 1) as q:
                    with act.Fori(0, JB) as j:
                        body(B_MLP[l] + 2 * JB * q + JB + j)
                    with act.Fori(0, JB // 2) as i:
                        for k in range(2):
                            up_block(q + 1, i, k)
                q = QUARTERS - 1
                for j in range(JB):
                    s = (j + 1) % 2
                    asides = {}
                    if v_out is not None and j:
                        asides[4] = lambda: x_hi(v_out + j - 1, None)
                    if l == 1 and j == JB - 1:
                        for hf in range(3, 8):
                            split(B_MLP[l] + 2 * JB * q + JB + j, hf)
                    else:
                        body(B_MLP[l] + 2 * JB * q + JB + j, asides, nxt=nxt if j == JB - 1 else None)
                    x_squares(squares_from + j, s, u[s] + JB * q + 2 + j // 2 + 1)

            mlp(0, V_WO, V_MLP0, "dkv", V_MLP0)

            def latent(k, b, s, dst, n, c0):
                act.wait_ge(rs_ready, 3)
                used(b)
                for t in range(TT):
                    fn(dst[:, t, 0:n], acc[s][:, t, 0:n], ACT.Copy, scale=rs[:, 2, t:t + 1]).then_inc(drained[s], 1)
                for t in range(TT):
                    act.wait_ge(drained[s], 2 * U_DKV[s] + t + 1)
                    if k:
                        act.wait_ge(lat_ss, t + 1)
                    fn(junk[:, t, 0:n - c0], dst[:, t, c0:n], ACT.Square,
                       accum_out=lss[:, k, t:t + 1]).then_inc(lat_ss, 1)

            def ckv_scaled():
                act.wait_ge(lat_rs, 1)
                for t in range(TT):
                    fn(stage[:, t, :], stage[:, t, :], ACT.Copy, scale=lrs[:, 0, t:t + 1]).then_inc(ckv_ready, 1)

            def latent_hi(buf, c0, n, bank, gain, done_at):
                act.wait_ge(latT_done, done_at)
                for c in range(n):
                    b, col = bank(c)
                    fn(buf[:, c0 + c, 0, :], b[:, col:col + SEQ], ACT.Copy,
                       scale=gains[:, gain + c:gain + c + 1]).then_inc(latT_hi, 1)

            body(B_DKV, {4: lambda: x_hi(V_MLP0 + JB - 1, None)}, kind="dkv", nxt="rq")
            latent(0, B_DKV, 1, stage, KV_LORA, 0)
            body(B_RQ, {3: ckv_scaled, 5: lambda: latent_hi(opB, 12, 4, lambda c: (side[c // 2], SEQ * (c % 2)), G_KV, 2)},
                 kind="rq", nxt="mla")
            latent(1, B_RQ, 0, kv_sb[:, 1], ROPE + Q_LORA, ROPE)
            act.wait_ge(latT_done, 3)
            fn(krT[:], side[2][0:ROPE, 0:SEQ], ACT.Copy).then_inc(krT_ready, 1)
            latent_hi(opA, 0, 3, lambda c: (side[3], SEQ * c) if c < 2 else (side[2], SEQ), G_Q, 3)

            def mla_drain_kv(b, hf, par):
                act.wait_ge(pe_halves, 8 * b + hf + 1)
                fn(kT[:, 0:2, :], acc[1][:, 0, :].rearrange("p (h t) -> p h t", h=2), ACT.Copy).then_inc(drained[1], 1)
                fn(kv_sb[:, par, :, 0:2 * VDIM], acc[1][:, 1, :].rearrange("p (t n) -> p t n", t=TT),
                   ACT.Copy).then_inc(drained[1], 1)

            def mla_drain_q(b, hf):
                act.wait_ge(pe_halves, 8 * b + hf + 1)
                for t in range(TT):
                    fn(stage[:, t, 0:Q_LORA], acc[0][:, t, 0:Q_LORA], ACT.Copy,
                       scale=lrs[:, 1, t:t + 1]).then_inc(drained[0], 1)

            def mla_copies(p):
                act.wait_ge(qkT_done, 2 * DA_PAIRS + 2 * p + 1)
                fn(qT[:, 0:2, :], side[0][:].rearrange("p (h t) -> p h t", h=2), ACT.Copy).then_inc(qkT_ready, 1)
                act.wait_ge(qkT_done, 2 * DA_PAIRS + 2 * p + 2)
                fn(qT[0:ROPE, 2:4, :], side[2][0:ROPE, :].rearrange("p (h t) -> p h t", h=2),
                   ACT.Copy).then_inc(qkT_ready, 1)

            def mla_exps(p):
                exps(4 * DA_PAIRS + 2 * p, (0, 1), (0, 1), MLA_SCALE)

            def mla_hi(p):
                act.wait_ge(pv_done, DA_HEADS + p + 1)
                fn(opB[:, bass.ds(2 * p, 2), 0, :], side[1][:].rearrange("p (h t) -> p h t", h=2),
                   ACT.Copy).then_inc(opB_hi, 1)

            def mla_pair(g, u, p, prev=True, prev2=True, nxt="mla"):
                b = B_MLA + g
                nb, h0 = (b, 4) if u == 0 else (b + 1, 0)
                split(b, 4 * u + 3, "mla")
                if prev:
                    mla_copies(p - 1)
                split(nb, h0, nxt)
                if prev:
                    mla_exps(p - 1)
                split(nb, h0 + 1, nxt)
                if prev2:
                    mla_hi(p - 2)
                mla_drain_kv(b, 4 * u + 2, u)
                mla_drain_q(b, 4 * u + 3)
                split(nb, h0 + 2, nxt)
                if prev:
                    copy_attnT(DA_HEADS + 2 * (p - 1), 2)

            act.wait_ge(lat_rs, 2)
            mla_pair(0, 0, 0, prev=False, prev2=False)
            mla_pair(0, 1, 1, prev2=False)
            with act.Fori(1, MLA_PAIRS // 2 - 1) as g:
                mla_pair(g, 0, 2 * g)
                mla_pair(g, 1, 2 * g + 1)
            mla_pair(MLA_PAIRS // 2 - 1, 0, MLA_PAIRS - 2)
            mla_pair(MLA_PAIRS // 2 - 1, 1, MLA_PAIRS - 1, nxt=None)

            last_pair = MLA_PAIRS - 1

            def mla_rest():
                copy_attnT(DA_HEADS + 2 * last_pair, 2)
                mla_hi(last_pair)

            def mla_exps_and_hi():
                mla_exps(last_pair)
                mla_hi(last_pair - 1)

            body(B_BWO, {3: lambda: mla_copies(last_pair), 5: mla_exps_and_hi, 7: mla_rest})
            out_proj(B_BWO, U_BWO, V_BWO, G_MLP[1])
            act.wait_ge(opB_lo, 4 * DA_PAIRS + MLA_PAIRS)
            act.dma_start(g_out, final_norm_g.partition_broadcast(P)).then_inc(g_out_in, 16)
            mlp(1, V_BWO, None, None, V_MLP1)
            act.wait_ge(rs_ready, 5)
            for j in range(JB):
                act.wait_ge(xg_ready, 2 * j + 1)
                fn(y_sb[j][:, 0, :], y_sb[j][:, 0, :], ACT.Copy,
                   scale=rs[:, 4, 0:1]).then_inc(out_ready[0], 1)

        @block.vector
        def _(dve):
            tt_, ts_, stt = nc.vector.tensor_tensor, nc.vector.tensor_scalar, nc.vector.scalar_tensor_tensor

            def split(b, hf, kind=None):
                r = hf // 2
                c0, place = 2 * (hf % 2), 2 * (hf % 4)
                dve.wait_ge(hi_ready, 8 * b + hf + 1)
                if kind in ("dkv", "rq"):
                    for c in range(2):
                        k = 4 * r + c0 + c
                        parts = [(0, NB, G_KVIN)] if kind == "dkv" else [(0, ROPE, G_KVIN), (ROPE, ROPE + Q_LORA, G_B)]
                        for n0, n1, g in parts:
                            done = stt(out=wlo[:, place + c, n0:n1], in0=raw[:, r, c0 + c, n0:n1],
                                       scalar=gains[:, g + k:g + k + 1], in1=whi[:, place + c, n0:n1].bitcast(F32),
                                       op0=ALU.mult, op1=ALU.subtract)
                else:
                    n, ch = (Q_LORA, 2 - hf % 2) if kind == "mla" and r % 2 else (NB, 2)
                    done = tt_(wlo[:, place:place + ch, 0:n], raw[:, r, c0:c0 + ch, 0:n],
                               whi[:, place:place + ch, 0:n].bitcast(F32), ALU.subtract)
                done.then_inc(lo_ready, 1)

            def body(b, asides=None, kind=None, nxt=None):
                for hf in range(3, 11):
                    if hf < 8:
                        split(b, hf, kind)
                    else:
                        split(b + 1, hf - 8, nxt)
                    if asides and hf in asides:
                        asides[hf]()

            def used(b):
                dve.wait_ge(pe_halves, 8 * b + 8)

            def x_lo(v, gain):
                j = v % JB
                for k in range(2):
                    dve.wait_ge(xT_hi, 4 * v + 2 * k + 2)
                    for cc in range(2):
                        c = JB * j + 2 * k + cc
                        src, hi = side[2 * (v % 2) + k][:, SEQ * cc:SEQ * cc + SEQ], opA[:, c, 0, :].bitcast(F32)
                        if gain is None:
                            tt_(opA[:, c, 1, :], src, hi, ALU.subtract).then_inc(xT_lo, 1)
                        else:
                            stt(out=opA[:, c, 1, :], in0=src, scalar=gains[:, gain + c:gain + c + 1], in1=hi,
                                op0=ALU.mult, op1=ALU.subtract).then_inc(xT_lo, 1)

            def stream_stats(t, squared):
                dve.wait_ge(xsq, 2 * JB * (t + 1))
                nc.vector.tensor_reduce(xms[:, t, :], xss[:, t, :, :], AX.X, ALU.add).then_inc(xstat, 1)
                dve.wait_ge(xstat, 2 * t + 1)
                ts_(xms2[:, t, :], xms[:, t, :], 1.0 / D, EPS, ALU.mult, ALU.add).then_inc(xstat, 1)
                if squared:
                    dve.wait_ge(xstat, 2 * t + 2)
                    nc.vector.reciprocal(rs[:, t, :], xms2[:, t, :]).then_inc(rs_ready, 1)

            n_trig = [0]

            def step(ins):
                n_trig[0] += 1
                ins.then_inc(trig_step, 1)
                dve.wait_ge(trig_step, n_trig[0])

            def angles():
                dve.wait_ge(small_in, 48)
                tt_(lam_rows[:, 0:4:2, :], lam_rows[:, 0:4:2, :], lam_rows[:, 1:4:2, :], ALU.mult).then_inc(lam_step, 1)
                step(nc.vector.tensor_copy(pos_f[:], pos_i[:]))
                dve.wait_ge(lam_step, 1)
                nc.vector.tensor_reduce(lam_s[:, 0:2], lam_rows[:, 0:4:2, :], AX.X, ALU.add).then_inc(lam_step, 1)
                for k in range(2):
                    for t in range(TT):
                        last_angle = ts_(trig[:, k, t, :], invf[:], pos_f[:, t:t + 1], None, ALU.mult)
                step(last_angle)
                ts_(turns[:, 0], trig[:, 0], 1.0 / TWO_PI, None, ALU.mult)
                step(ts_(turns[:, 1], trig[:, 1], 1.0 / TWO_PI, 0.25, ALU.mult, ALU.add))

            def whole_turns():
                magic = 1.5 * 2.0 ** 23
                step(ts_(turns, turns, magic, None, ALU.add))
                step(ts_(turns, turns, magic, None, ALU.subtract))
                step(nc.vector.tensor_copy(turns_hi[:], turns))
                step(tt_(turns_lo, turns, turns_hi[:].bitcast(F32), ALU.subtract))
                minus_turns(two_pi[:1])

            def minus_turns(parts):
                for part in parts:
                    for turn in (turns_hi[:].bitcast(F32), turns_lo):
                        step(stt(out=trig, in0=turn, scalar=-part, in1=trig, op0=ALU.mult, op1=ALU.add))

            def last_angles():
                minus_turns(two_pi[1:])
                step(ts_(trig[:, 1], trig[:, 1], float(np.pi / 2), None, ALU.add))
                step(ts_(trig, trig, 3.1415925, -3.1415925, ALU.min, ALU.max))

            two_pi = twelve_bit_parts(TWO_PI, 3)

            def start_lambda():
                dve.wait_ge(lam_step, 3)
                tt_(lam_s[:, 4:5], lam_s[:, 3:4], lam_s[:, 2:3], ALU.subtract).then_inc(lam_step, 1)
                dve.wait_ge(lam_step, 4)
                ts_(lam_s[:, 5:6], lam_s[:, 4:5], LAM_INIT, None, ALU.subtract).then_inc(lam_step, 1)
                dve.wait_ge(tables_ready, 4)

            neg_lam = lam_s[:, 5:6]
            dve.wait_ge(gains_t, 1)
            nc.vector.tensor_copy(gains[:, 0:KC], side[3][:, 0:KC]).then_inc(gains_ready, 1)

            def other_gains():
                dve.wait_ge(gains_t, 2)
                nc.vector.tensor_copy(gains[:, KC:G_SUB], side[3][:, 0:G_SUB - KC]).then_inc(gains_ready, 1)
                ts_(gains[:, G_SUB:G_END], side[3][:, G_SUB - KC:G_END - KC], 1.0 - LAM_INIT, None,
                    ALU.mult).then_inc(gains_ready, 1)

            x_lo(V_INIT, G_A)
            split(0, 0)
            split(0, 1)
            x_lo(V_INIT + 1, G_A)
            split(0, 2)

            def rotate(view, cos, sin, heads, width, i):
                h = width // 2

                def b(tab, c0, c1):
                    return tab[:, :, c0:c1].unsqueeze(2).to_broadcast([P, TT, heads, c1 - c0])

                a = rope_a[:].rearrange("p t h w -> p t (h w)")[:, :, 0:heads * width].rearrange(
                    "p t (h w) -> p t h w", h=heads)
                c = rope_b[:].rearrange("p t h w -> p t (h w)")[:, :, 0:heads * width].rearrange(
                    "p t (h w) -> p t h w", h=heads)
                tt_(a, view, b(cos, 0, width), ALU.mult).then_inc(rope_parts, 1)
                tt_(c[:, :, :, 0:h], view[:, :, :, h:width], b(sin, 0, h), ALU.mult).then_inc(rope_parts, 1)
                tt_(c[:, :, :, h:width], view[:, :, :, 0:h], b(sin, h, width), ALU.mult).then_inc(rope_parts, 1)
                dve.wait_ge(rope_parts, 3 * i + 3)
                tt_(view, a, c, ALU.add).then_inc(roped, 1)

            def rope_qk(p, k):
                dve.wait_ge(drained[k], (4 if k == 0 else 2) * p + 2)
                if not (isinstance(p, int) and p == 0 and k == 0):
                    dve.wait_ge(roped, 2 * p + k)
                rotate(stage[:].rearrange("p t (h w) -> p t h w", w=DA_DIM)[:, :, :, 0:DA_ROT], cosA, sinA, 4,
                       DA_ROT, 2 * p + k)

            def softmax_bias(maps_before, m, bank, scale):
                dve.wait_ge(scores_done, maps_before + m + 1)
                tt_(prob[:, m, :], bank[:, 0:KEYS], mask[:], ALU.add).then_inc(masked, 1)
                dve.wait_ge(masked, maps_before + m + 1)
                nc.vector.tensor_reduce(nmax[:, m, 0:1], prob[:, m, 0:P], AX.X, ALU.max)
                nc.vector.tensor_reduce(nmax[:, m, 1:2], prob[:, m, P:KEYS], AX.X, ALU.max).then_inc(maxed, 1)
                dve.wait_ge(maxed, maps_before + m + 1)
                ts_(bias[:, m, :], nmax[:, m, :], -scale, None, ALU.mult).then_inc(bias_ready, 1)

            def da_softmax(p, maps):
                for m in maps:
                    softmax_bias(4 * p, m, side[m], DA_SCALE)

            def da_weights(p):
                dve.wait_ge(exp_done, 4 * p + 4)
                nc.vector.reciprocal(rinv[:], rowsum[:]).then_inc(rinv_ready, 1)
                dve.wait_ge(rinv_ready, p + 1)
                ts_(rneg[:], rinv[:], neg_lam, None, ALU.mult).then_inc(rneg_ready, 1)
                tiles = [(h, t, c0, c1) for h in range(2) for t, (c0, c1) in enumerate(((0, P), (P, KEYS)))]
                for h, t, c0, c1 in tiles:
                    ts_(prob[:, 2 * h, c0:c1], prob[:, 2 * h, c0:c1], rinv[:, 2 * h, t:t + 1], None,
                        ALU.mult).then_inc(half_attn, 1)
                dve.wait_ge(rneg_ready, p + 1)
                for k, (h, t, c0, c1) in enumerate(tiles):
                    dve.wait_ge(half_attn, 4 * p + k + 1)
                    stt(out=attn[:, h, c0:c1], in0=prob[:, 2 * h + 1, c0:c1], scalar=rneg[:, 2 * h + 1, t:t + 1],
                        in1=prob[:, 2 * h, c0:c1], op0=ALU.mult, op1=ALU.add).then_inc(attn_ready, 1)

            def o_means(p):
                dve.wait_ge(oss_ready, p + 1)
                ts_(oms[:], oss[:], 1.0 / (2 * DA_DIM), SUB_EPS, ALU.mult, ALU.add).then_inc(oms_ready, 1)

            def o_scale(p):
                dve.wait_ge(ors_ready, p + 1)
                for t in range(TT):
                    done = ts_(o_sb[:, 0, t, :], side[0][:, SEQ * t:SEQ * t + SEQ], ors[:, t:t + 1], None, ALU.mult)
                done.then_inc(o_ready[0], 1)

            def o_lo(p):
                for h in range(2):
                    dve.wait_ge(opB_hi, 4 * p + 2 * h + 2)
                    for e in range(2):
                        stt(out=opB[:, bass.ds(4 * p + 2 * h + e, 1), 1, :],
                            in0=side[h][:, SEQ * e:SEQ * e + SEQ].unsqueeze(1),
                            scalar=gains[:, G_SUB + e:G_SUB + e + 1],
                            in1=opB[:, bass.ds(4 * p + 2 * h + e, 1), 0, :].bitcast(F32), op0=ALU.mult,
                            op1=ALU.subtract).then_inc(opB_lo, 1)

            def qkv(p, first):
                b = B_QKV + 3 * p
                pv = None if first else p - 1
                body(b, {3: lambda: x_lo(V_INIT + 2, G_A), 5: lambda: x_lo(V_INIT + 3, G_A), 6: angles, 7: whole_turns, 8: last_angles,
                         9: lambda: stream_stats(0, False)} if first else {4: lambda: da_weights(pv)})
                if not first:
                    rope_qk(p, 0)
                body(b + 1, {4: start_lambda, 5: lambda: rope_qk(p, 0), 6: other_gains} if first else {7: lambda: o_means(pv), 8: lambda: o_scale(pv)})
                rope_qk(p, 1)
                asides = {} if first else {4: lambda: o_lo(pv)}
                asides.update({8: lambda: da_softmax(p, (0, 1)), 9: lambda: da_softmax(p, (2, 3))})
                body(b + 2, asides)

            qkv(0, True)
            with dve.Fori(1, DA_PAIRS) as p:
                qkv(p, False)
            last = DA_PAIRS - 1

            def mean_and_scale():
                o_means(last)
                o_scale(last)

            body(B_WO, {3: lambda: da_weights(last), 6: mean_and_scale, 7: lambda: o_lo(last)})

            def add_product(b, s, uses, cols):
                used(b)
                for t in range(TT):
                    tt_(xs[:, t, cols], acc[s][:, t, :], xs[:, t, cols], ALU.add).then_inc(drained[s], 1)

            def out_proj(b0, uses, v0, gain):
                add_product(b0, 1, uses[1], slice(0, NB))
                for j in range(1, JB):
                    s = (j + 1) % 2
                    body(b0 + j, {4: lambda: x_lo(v0 + j - 1, gain)})
                    add_product(b0 + j, s, uses[s] + j // 2, slice(NB * j, NB * j + NB))

            out_proj(B_WO, U_WO, V_WO, G_MLP[0])

            def mlp(l, v_in, v_out, nxt):
                u = U_MLP[l]

                def square_up(s, t):
                    for k in range(2):
                        dve.wait_ge(relu_done, 2 * t + k + 1)
                        stt(out=sq_sb[:, NB * k:NB * k + NB], in0=acc[s][:, k, :], scalar=0.0,
                            in1=relu_sb[:, NB * k:NB * k + NB], op0=ALU.max, op1=ALU.mult).then_inc(drained[s], 1)

                def hid_lo_part(t, j):
                    for k in range(2):
                        dve.wait_ge(hid_hi, 2 * t + k + 1)
                        tt_(opB[:, bass.ds(4 * j + 2 * k, 2), 1, :],
                            sq_sb[:, NB * k:NB * k + NB].rearrange("p (c t) -> p c t", c=2),
                            opB[:, bass.ds(4 * j + 2 * k, 2), 0, :].bitcast(F32), ALU.subtract).then_inc(hid_lo, 1)

                def up_block(q, i, k, asides=None):
                    body(B_MLP[l] + 2 * JB * q + 2 * i + k, asides)
                    t = JB * (QUARTERS * l + q) + 2 * i + k
                    square_up(1 - k, t)
                    hid_lo_part(t, 2 * i + k)

                def add_scaled(b, s, prior, cols, urgent=False):
                    if urgent:
                        dve.wait_ge(bank0_done, B_WO + 1)
                    else:
                        used(b)
                    dve.wait_ge(drained[s], prior)
                    dve.wait_ge(rs_ready, 2 * l + 2)
                    for t in range(TT):
                        if urgent and t:
                            used(b)
                        stt(out=xs[:, t, cols], in0=acc[s][:, t, :], scalar=rs[:, 2 * l + 1, t:t + 1],
                            in1=xs[:, t, cols], op0=ALU.mult, op1=ALU.add).then_inc(drained[s], 1)

                for j in range(JB):
                    up_block(0, j // 2, j % 2, {} if j else {
                        4: lambda: x_lo(v_in + JB - 1, G_MLP[l]), 5: lambda: stream_stats(2 * l + 1, True)})
                with dve.Fori(0, QUARTERS - 1) as q:
                    with dve.Fori(0, JB // 2) as i:
                        for k in range(2):
                            b, s = B_MLP[l] + 2 * JB * q + JB + 2 * i + k, 1 - k
                            body(b)
                            add_scaled(b, s, 2 * (u[s] + JB * q + 2 + i), bass.ds(NB * (2 * i + k), NB))
                    with dve.Fori(0, JB // 2) as i:
                        for k in range(2):
                            up_block(q + 1, i, k)
                q = QUARTERS - 1
                for j in range(JB):
                    b, s = B_MLP[l] + 2 * JB * q + JB + j, (j + 1) % 2
                    asides = {}
                    if v_out is not None and j:
                        asides[4] = lambda: x_lo(v_out + j - 1, None)
                    if l == 1 and j == JB - 1:
                        for hf in range(3, 8):
                            split(b, hf)
                    else:
                        body(b, asides, nxt=nxt if j == JB - 1 else None)
                    end = l == 1 and j == JB - 1
                    add_scaled(b, s, 2 * (u[s] + JB * q + 2 + j // 2), slice(NB * j, NB * j + NB), urgent=end)
                    if l == 1:
                        dve.wait_ge(g_out_in, 16)
                        for t in range(TT):
                            if t and end:
                                stream_stats(4, False)
                            dve.wait_ge(drained[s], 2 * (u[s] + JB * q + 2 + j // 2) + t + 1)
                            tt_(y_sb[j][:, t, :], xs[:, t, NB * j:NB * j + NB],
                                g_out[:, NB * j:NB * j + NB], ALU.mult).then_inc(xg_ready, 1)

            mlp(0, V_WO, V_MLP0, "dkv")

            def latent_stats(k, width):
                dve.wait_ge(lat_ss, 2 * k + 2)
                ts_(lms[:, k, :], lss[:, k, :], 1.0 / width, EPS, ALU.mult, ALU.add).then_inc(lat_ms, 1)

            def latent_lo(buf, c0, n, bank, before, gain):
                for c in range(n):
                    dve.wait_ge(latT_hi, before + min(n, 2 * (c // 2) + 2))
                    b, col = bank(c)
                    stt(out=buf[:, c0 + c, 1, :], in0=b[:, col:col + SEQ], scalar=gains[:, gain + c:gain + c + 1],
                        in1=buf[:, c0 + c, 0, :].bitcast(F32), op0=ALU.mult, op1=ALU.subtract).then_inc(latT_lo, 1)

            body(B_DKV, {4: lambda: x_lo(V_MLP0 + JB - 1, None), 5: lambda: stream_stats(2, False)}, kind="dkv",
                 nxt="rq")
            latent_stats(0, KV_LORA)
            body(B_RQ, {5: lambda: latent_lo(opB, 12, 4, lambda c: (side[c // 2], SEQ * (c % 2)), 0, G_KV)},
                 kind="rq", nxt="mla")
            dve.wait_ge(drained[0], 2 * (U_DKV[0] + 1))
            dve.wait_ge(roped, 2 * DA_PAIRS)
            rotate(kv_sb[:, 1, :, 0:ROPE].unsqueeze(2), cosB, sinB, 1, ROPE, 2 * DA_PAIRS)
            latent_stats(1, Q_LORA)
            latent_lo(opA, 0, 3, lambda c: (side[3], SEQ * c) if c < 2 else (side[2], SEQ), 4, G_Q)

            def rope_mla(p):
                dve.wait_ge(drained[0], 2 * (U_MLA[0] + p) + 2)
                dve.wait_ge(roped, 2 * DA_PAIRS + 1 + p)
                rotate(stage[:, :, 0:Q_LORA].rearrange("p t (h w) -> p t h w", h=2)[:, :, :, NOPE:NOPE + ROPE], cosB,
                       sinB, 2, ROPE, 2 * DA_PAIRS + 1 + p)

            def mla_softmax(p):
                for m in range(2):
                    softmax_bias(4 * DA_PAIRS + 2 * p, m, side[3 * (1 - m)], MLA_SCALE)

            def mla_weights(p):
                dve.wait_ge(exp_done, 4 * DA_PAIRS + 2 * p + 2)
                nc.vector.reciprocal(rinv[:, 0:2, :], rowsum[:, 0:2, :]).then_inc(rinv_ready, 1)
                dve.wait_ge(rinv_ready, DA_PAIRS + p + 1)
                for h in range(2):
                    for t, (c0, c1) in enumerate(((0, P), (P, KEYS))):
                        ts_(attn[:, h, c0:c1], prob[:, h, c0:c1], rinv[:, h, t:t + 1], None,
                            ALU.mult).then_inc(attn_ready, 1)

            def mla_lo(p):
                dve.wait_ge(opB_hi, 4 * DA_PAIRS + p + 1)
                tt_(opB[:, bass.ds(2 * p, 2), 1, :], side[1][:].rearrange("p (h t) -> p h t", h=2),
                    opB[:, bass.ds(2 * p, 2), 0, :].bitcast(F32), ALU.subtract).then_inc(opB_lo, 1)

            def mla_pair(g, u, p, prev=True, prev2=True, nxt="mla"):
                b = B_MLA + g
                nb, h0 = (b, 4) if u == 0 else (b + 1, 0)
                split(b, 4 * u + 3, "mla")
                split(nb, h0, nxt)
                if prev:
                    mla_softmax(p - 1)
                    mla_weights(p - 1)
                split(nb, h0 + 1, nxt)
                if prev2:
                    mla_lo(p - 2)
                rope_mla(p)
                split(nb, h0 + 2, nxt)

            mla_pair(0, 0, 0, prev=False, prev2=False)
            mla_pair(0, 1, 1, prev2=False)
            with dve.Fori(1, MLA_PAIRS // 2 - 1) as g:
                mla_pair(g, 0, 2 * g)
                mla_pair(g, 1, 2 * g + 1)
            mla_pair(MLA_PAIRS // 2 - 1, 0, MLA_PAIRS - 2)
            mla_pair(MLA_PAIRS // 2 - 1, 1, MLA_PAIRS - 1, nxt=None)
            last_pair = MLA_PAIRS - 1

            body(B_BWO, {4: lambda: mla_softmax(last_pair), 5: lambda: mla_weights(last_pair),
                         6: lambda: mla_lo(last_pair - 1), 7: lambda: mla_lo(last_pair)})
            out_proj(B_BWO, U_BWO, V_BWO, G_MLP[1])
            mlp(1, V_BWO, None, None)
            dve.wait_ge(rs_ready, 5)
            for j in range(JB):
                dve.wait_ge(xg_ready, 2 * j + 2)
                ts_(y_sb[j][:, 1, :], y_sb[j][:, 1, :], rs[:, 4, 1:2], None, ALU.mult).then_inc(out_ready[1], 1)


_INS = ["x", "positions", "a_norm_g", "a_w_qkv", "a_lambda", "a_subln_g", "a_w_o", "kv_in_norm_g", "w_dkv",
        "kv_norm_g", "w_ukv", "b_norm_g", "b_w_dq", "b_q_norm_g", "b_w_uq", "b_w_o", "mlp_norm_g", "w_up", "w_down",
        "final_norm_g"]


def kernel(**inputs):
    import concourse.bacc as _bacc
    from concourse.bass_utils import run_bass_kernel_spmd as _run

    nc = _bacc.Bacc("TRN2", target_bir_lowering=False, num_devices=1)
    arrays, args = {}, []
    for name in _INS:
        a = np.ascontiguousarray(inputs[name])
        arrays[f"in_{name}"] = a
        args.append(nc.dram_tensor(f"in_{name}", a.shape, mybir.dt.from_np(a.dtype), kind="ExternalInput").ap())
    arrays["in_freqs"] = rope_frequencies()
    args.append(nc.dram_tensor("in_freqs", (P, 48), F32, kind="ExternalInput").ap())
    args.append(nc.dram_tensor("out_0", (1, SEQ, D), F32, kind="ExternalOutput").ap())
    trunk(nc, *args)
    r = _run(nc, [arrays], core_ids=[0])
    return r.results[0]["out_0"]
```
